# Optimizing a Trainium2 kernel written in Bass

```python
import jax, jax.numpy as jnp
from jax import lax
import numpy as np

D_MODEL = 1024
BATCH = 1
SEQ = 512
DEPTH = 2
DEC_BATCH = 1
DEC_SEQ = 64
PAST_LEN = 256

CHUNK = 64
MLA_HEADS = 8
MLA_Q_RANK = 384
MLA_KV_RANK = 256
MLA_NOPE = 64
MLA_ROPE = 32
MLA_V = 64
MLA_SCALE = (MLA_NOPE + MLA_ROPE) ** -0.5
RET_HEADS = 4
RET_DK = 64
RET_DV = 128
BAND_HEADS = 8
BAND_HD = 64
BAND_PREV_CHUNKS = 8
BAND_WINDOW = BAND_PREV_CHUNKS * CHUNK
MAX_REL = 128
MEM_LEN = 256
MEM_HEADS = 4
MEM_HD = 128
D_FF = 4 * D_MODEL
N_BRANCH = 3
ROPE_THETA = 10000.0
EPS = 1e-6
Q_BLOCK = 128
NEG_INF = -1e30
IN_SIZES = (MLA_Q_RANK, MLA_KV_RANK, MLA_ROPE,
            RET_HEADS * RET_DK, RET_HEADS * RET_DK, RET_HEADS * RET_DV, RET_HEADS * RET_DV,
            BAND_HEADS * BAND_HD, BAND_HEADS * BAND_HD, BAND_HEADS * BAND_HD,
            N_BRANCH * D_MODEL)
IN_WIDTH = sum(IN_SIZES)

kernel_name = 'hybrid_mla_retention_band_stream_step'

def rms_norm(x, g):
    xf = x.astype(jnp.float32)
    y = xf * lax.rsqrt(jnp.mean(xf * xf, axis=-1, keepdims=True) + EPS)
    return (y * g.astype(jnp.float32)).astype(x.dtype)

def rope(x, pos):
    half = x.shape[-1] // 2
    inv = ROPE_THETA ** (-jnp.arange(half, dtype=jnp.float32) / half)
    ang = pos.astype(jnp.float32)[:, None] * inv[None, :]
    cos, sin = jnp.cos(ang)[:, None, :], jnp.sin(ang)[:, None, :]
    xf = x.astype(jnp.float32)
    x1, x2 = xf[..., :half], xf[..., half:]
    return jnp.concatenate([x1 * cos - x2 * sin, x2 * cos + x1 * sin], axis=-1).astype(x.dtype)

def split_cols(z):
    parts, start = [], 0
    for n in IN_SIZES:
        parts.append(z[..., start:start + n])
        start += n
    return parts

def mla_core(q_nope, q_pe, k_nope, k_pe, v, mask):
    s = (jnp.einsum('bqhd,bkhd->bhqk', q_nope, k_nope)
         + jnp.einsum('bqhd,bkd->bhqk', q_pe, k_pe)).astype(jnp.float32) * MLA_SCALE
    if mask is not None:
        s = jnp.where(mask, s, NEG_INF)
    p = jax.nn.softmax(s, axis=-1).astype(v.dtype)
    return jnp.einsum('bhqk,bkhd->bqhd', p, v)

def mla_prompt(q_nope, q_pe, k_nope, k_pe, v):
    B, S, H, _ = q_nope.shape
    nb = S // Q_BLOCK
    blocks = lambda t: t.reshape(B, nb, Q_BLOCK, H, t.shape[-1]).swapaxes(0, 1)
    k_chunk = jnp.arange(S) // CHUNK

    def one_block(args):
        i, qn, qp = args
        q_chunk = (i * Q_BLOCK + jnp.arange(Q_BLOCK)) // CHUNK
        return mla_core(qn, qp, k_nope, k_pe, v, k_chunk[None, :] <= q_chunk[:, None])

    o = lax.map(one_block, (jnp.arange(nb), blocks(q_nope), blocks(q_pe)))
    return o.swapaxes(0, 1).reshape(B, S, H, v.shape[-1])

def ret_log_decay():
    return jnp.log1p(-jnp.exp2(-5.0 - jnp.arange(RET_HEADS, dtype=jnp.float32)))

def retention_chunk(q, k, v, state, log_g):
    L = q.shape[1]
    idx = jnp.arange(L, dtype=jnp.float32)
    diff = idx[:, None] - idx[None, :]
    decay = jnp.where(diff >= 0, jnp.exp(log_g[:, None, None] * jnp.maximum(diff, 0.0)), 0.0)
    s = jnp.einsum('blhd,bmhd->bhlm', q, k) * decay[None]
    inner = jnp.einsum('bhlm,bmhe->blhe', s, v)
    cross = jnp.einsum('blhd,bhde->blhe', q, state) * jnp.exp(log_g[None, :] * (idx[:, None] + 1.0))[None, :, :, None]
    w = jnp.exp(log_g[None, :] * (L - 1.0 - idx[:, None]))
    new_state = state * jnp.exp(log_g * L)[None, :, None, None] + jnp.einsum('blhd,blhe,lh->bhde', k, v, w)
    return inner + cross, new_state

def retention_prompt(q, k, v, log_g):
    B, S, H, dk = q.shape
    nC = S // CHUNK
    to_chunks = lambda t: t.reshape(B, nC, CHUNK, H, t.shape[-1]).swapaxes(0, 1)

    def step(state, xs):
        qc, kc, vc = xs
        o, state = retention_chunk(qc, kc, vc, state, log_g)
        return state, o

    s0 = jnp.zeros((B, H, dk, v.shape[-1]), jnp.float32)
    state, o = lax.scan(step, s0, (to_chunks(q), to_chunks(k), to_chunks(v)))
    return o.swapaxes(0, 1).reshape(B, S, H, v.shape[-1]), state

def head_group_norm(o, g):
    mu = jnp.mean(o, axis=-1, keepdims=True)
    var = jnp.mean(jnp.square(o - mu), axis=-1, keepdims=True)
    y = (o - mu) * lax.rsqrt(var + EPS)
    return y.reshape(o.shape[0], o.shape[1], -1) * g.astype(jnp.float32)

def rel_bias(table, rel):
    return table[:, jnp.clip(rel, -MAX_REL, MAX_REL) + MAX_REL].astype(jnp.float32)

def band_core(q, k, v, bias, valid):
    s = jnp.einsum('bqhd,bkhd->bhqk', q, k).astype(jnp.float32) * (BAND_HD ** -0.5) + bias[None]
    if valid is not None:
        s = jnp.where(valid, s, NEG_INF)
    p = jax.nn.softmax(s, axis=-1).astype(v.dtype)
    return jnp.einsum('bhqk,bkhd->bqhd', p, v)

def band_prompt(q, k, v, table):
    B, S, H, D = q.shape
    nC = S // CHUNK
    span = BAND_WINDOW + CHUNK
    pad = ((0, 0), (BAND_WINDOW, 0), (0, 0), (0, 0))
    kp, vp = jnp.pad(k, pad), jnp.pad(v, pad)
    j = jnp.arange(span)
    bias = rel_bias(table, BAND_WINDOW + jnp.arange(CHUNK)[:, None] - j[None, :])
    qc = q.reshape(B, nC, CHUNK, H, D).swapaxes(0, 1)

    def one_chunk(args):
        c, qb = args
        kb = lax.dynamic_slice_in_dim(kp, c * CHUNK, span, axis=1)
        vb = lax.dynamic_slice_in_dim(vp, c * CHUNK, span, axis=1)
        valid = c * CHUNK - BAND_WINDOW + j >= 0
        return band_core(qb, kb, vb, bias, valid)

    o = lax.map(one_chunk, (jnp.arange(nC), qc))
    return o.swapaxes(0, 1).reshape(B, S, H, D)

def band_sample(q, k, v, cache_k, cache_v, table):
    L, W = q.shape[1], cache_k.shape[1]
    kpos = jnp.concatenate([jnp.arange(W) - W, jnp.arange(L)])
    bias = rel_bias(table, jnp.arange(L)[:, None] - kpos[None, :])
    return band_core(q, jnp.concatenate([cache_k, k], axis=1), jnp.concatenate([cache_v, v], axis=1), bias, None)

def memory_kv(mem, g, w_k, w_v):
    m = rms_norm(mem, g)
    return jnp.einsum('bmd,dhe->bmhe', m, w_k), jnp.einsum('bmd,dhe->bmhe', m, w_v)

def memory_attend(u, mk, mv, w_q, w_o):
    q = jnp.einsum('bsd,dhe->bshe', u, w_q)
    s = jnp.einsum('bshe,bmhe->bhsm', q, mk).astype(jnp.float32) * (MEM_HD ** -0.5)
    p = jax.nn.softmax(s, axis=-1).astype(mv.dtype)
    o = jnp.einsum('bhsm,bmhe->bshe', p, mv)
    return jnp.einsum('bshe,hed->bsd', o, w_o)

def trunk_layer(x, pos, l, P, mem_k, mem_v, past):
    B, S, _ = x.shape
    u = rms_norm(x, P['g_pre_mix'][l])
    z = jnp.einsum('bsd,de->bse', u, P['w_in'][l])
    zq, zkv, zpe, rq, rk, rv, rg, cq, ck, cv, zg = split_cols(z)
    heads = lambda t, h: t.reshape(B, S, h, -1)
    q_a = jnp.einsum('bsr,rhd->bshd', rms_norm(zq, P['g_mla_q'][l]), P['w_mla_uq'][l])
    q_nope, q_pe = q_a[..., :MLA_NOPE], rope(q_a[..., MLA_NOPE:], pos)
    ckv = rms_norm(zkv, P['g_mla_kv'][l])
    kpe = rope(zpe[:, :, None, :], pos)[:, :, 0, :]
    q_b = rope(heads(rq, RET_HEADS), pos).astype(jnp.float32)
    k_b = rope(heads(rk, RET_HEADS), pos).astype(jnp.float32) * (RET_DK ** -0.5)
    v_b = heads(rv, RET_HEADS).astype(jnp.float32)
    log_g = ret_log_decay()
    q_c, k_c, v_c = heads(cq, BAND_HEADS), heads(ck, BAND_HEADS), heads(cv, BAND_HEADS)
    table = P['band_rel_bias'][l]
    if past is None:
        ckv_all, kpe_all = ckv, kpe
    else:
        c_ckv, c_kpe, s_ret, c_bk, c_bv = past
        ckv_all = jnp.concatenate([c_ckv, ckv], axis=1)
        kpe_all = jnp.concatenate([c_kpe, kpe], axis=1)
    kv = jnp.einsum('bkr,rhd->bkhd', ckv_all, P['w_mla_ukv'][l])
    k_nope, v_a = kv[..., :MLA_NOPE], kv[..., MLA_NOPE:]
    if past is None:
        o_a = mla_prompt(q_nope, q_pe, k_nope, kpe_all, v_a)
        o_b, ret_state = retention_prompt(q_b, k_b, v_b, log_g)
        o_c = band_prompt(q_c, k_c, v_c, table)
        new = (ckv, kpe, ret_state.astype(x.dtype), k_c[:, -BAND_WINDOW:], v_c[:, -BAND_WINDOW:])
    else:
        o_a = mla_core(q_nope, q_pe, k_nope, kpe_all, v_a, None)
        o_b, ret_state = retention_chunk(q_b, k_b, v_b, s_ret.astype(jnp.float32), log_g)
        o_c = band_sample(q_c, k_c, v_c, c_bk, c_bv, table)
        new = (ckv, kpe, ret_state.astype(s_ret.dtype), k_c, v_c)
    y_b = (head_group_norm(o_b, P['g_ret_gn'][l]) * jax.nn.silu(rg.astype(jnp.float32))).astype(x.dtype)
    br_a = jnp.einsum('bse,ed->bsd', o_a.reshape(B, S, -1), P['w_br_a'][l])
    br_b = jnp.einsum('bse,ed->bsd', y_b, P['w_br_b'][l])
    br_c = jnp.einsum('bse,ed->bsd', o_c.reshape(B, S, -1), P['w_br_c'][l])
    gates = jax.nn.sigmoid((zg + P['b_gate'][l]).astype(jnp.float32)).astype(x.dtype)
    gates = gates.reshape(B, S, N_BRANCH, D_MODEL)
    merged = gates[:, :, 0] * br_a + gates[:, :, 1] * br_b + gates[:, :, 2] * br_c
    x = x + rms_norm(jnp.einsum('bsd,de->bse', merged, P['w_out'][l]), P['g_post_mix'][l])
    u = rms_norm(x, P['g_pre_mem'][l])
    x = x + rms_norm(memory_attend(u, mem_k, mem_v, P['w_mem_q'][l], P['w_mem_o'][l]), P['g_post_mem'][l])
    u = rms_norm(x, P['g_pre_ff'][l])
    h = jnp.square(jax.nn.relu(jnp.einsum('bsd,df->bsf', u, P['w_up'][l])))
    x = x + rms_norm(jnp.einsum('bsf,fd->bsd', h, P['w_down'][l]), P['g_post_ff'][l])
    return x, new

def setup_inputs(seed: int = 0) -> dict:
    key = jax.random.key(seed)
    ks = iter(jax.random.split(key, 40))
    nrm = lambda shape, scale: jax.random.normal(next(ks), shape, jnp.float32) * scale
    gain = lambda shape: 1.0 + nrm(shape, 0.05)
    bw = min(BAND_WINDOW, PAST_LEN)
    return {
        'x_prompt': nrm((BATCH, SEQ, D_MODEL), 1.0),
        'x_sample': nrm((DEC_BATCH, DEC_SEQ, D_MODEL), 1.0),
        'cache_mla_ckv': nrm((DEPTH, DEC_BATCH, PAST_LEN, MLA_KV_RANK), 1.0),
        'cache_mla_kpe': nrm((DEPTH, DEC_BATCH, PAST_LEN, MLA_ROPE), 1.0),
        'state_ret': nrm((DEPTH, DEC_BATCH, RET_HEADS, RET_DK, RET_DV), 1.0),
        'cache_band_k': nrm((DEPTH, DEC_BATCH, bw, BAND_HEADS, BAND_HD), 1.0),
        'cache_band_v': nrm((DEPTH, DEC_BATCH, bw, BAND_HEADS, BAND_HD), 1.0),
        'cache_mem_k': nrm((DEPTH, DEC_BATCH, MEM_LEN, MEM_HEADS, MEM_HD), 1.0),
        'cache_mem_v': nrm((DEPTH, DEC_BATCH, MEM_LEN, MEM_HEADS, MEM_HD), 1.0),
        'mem_prompt': nrm((BATCH, MEM_LEN, D_MODEL), 1.0),
        'g_pre_mix': gain((DEPTH, D_MODEL)),
        'w_in': nrm((DEPTH, D_MODEL, IN_WIDTH), D_MODEL ** -0.5),
        'g_mla_q': gain((DEPTH, MLA_Q_RANK)),
        'w_mla_uq': nrm((DEPTH, MLA_Q_RANK, MLA_HEADS, MLA_NOPE + MLA_ROPE), MLA_Q_RANK ** -0.5),
        'g_mla_kv': gain((DEPTH, MLA_KV_RANK)),
        'w_mla_ukv': nrm((DEPTH, MLA_KV_RANK, MLA_HEADS, MLA_NOPE + MLA_V), MLA_KV_RANK ** -0.5),
        'g_ret_gn': gain((DEPTH, RET_HEADS * RET_DV)),
        'band_rel_bias': nrm((DEPTH, BAND_HEADS, 2 * MAX_REL + 1), 0.2),
        'w_br_a': nrm((DEPTH, MLA_HEADS * MLA_V, D_MODEL), (MLA_HEADS * MLA_V) ** -0.5),
        'w_br_b': nrm((DEPTH, RET_HEADS * RET_DV, D_MODEL), (RET_HEADS * RET_DV) ** -0.5),
        'w_br_c': nrm((DEPTH, BAND_HEADS * BAND_HD, D_MODEL), (BAND_HEADS * BAND_HD) ** -0.5),
        'b_gate': nrm((DEPTH, N_BRANCH * D_MODEL), 0.02),
        'w_out': nrm((DEPTH, D_MODEL, D_MODEL), D_MODEL ** -0.5),
        'g_post_mix': gain((DEPTH, D_MODEL)),
        'g_pre_mem': gain((DEPTH, D_MODEL)),
        'g_mem': gain((DEPTH, D_MODEL)),
        'w_mem_q': nrm((DEPTH, D_MODEL, MEM_HEADS, MEM_HD), D_MODEL ** -0.5),
        'w_mem_k': nrm((DEPTH, D_MODEL, MEM_HEADS, MEM_HD), D_MODEL ** -0.5),
        'w_mem_v': nrm((DEPTH, D_MODEL, MEM_HEADS, MEM_HD), D_MODEL ** -0.5),
        'w_mem_o': nrm((DEPTH, MEM_HEADS, MEM_HD, D_MODEL), (MEM_HEADS * MEM_HD) ** -0.5),
        'g_post_mem': gain((DEPTH, D_MODEL)),
        'g_pre_ff': gain((DEPTH, D_MODEL)),
        'w_up': nrm((DEPTH, D_MODEL, D_FF), D_MODEL ** -0.5),
        'w_down': nrm((DEPTH, D_FF, D_MODEL), D_FF ** -0.5),
        'g_post_ff': gain((DEPTH, D_MODEL)),
    }

def reference(x_prompt, x_sample, cache_mla_ckv, cache_mla_kpe, state_ret, cache_band_k, cache_band_v,
              cache_mem_k, cache_mem_v, mem_prompt, g_pre_mix, w_in, g_mla_q, w_mla_uq, g_mla_kv, w_mla_ukv,
              g_ret_gn, band_rel_bias, w_br_a, w_br_b, w_br_c, b_gate, w_out, g_post_mix, g_pre_mem, g_mem,
              w_mem_q, w_mem_k, w_mem_v, w_mem_o, g_post_mem, g_pre_ff, w_up, w_down, g_post_ff):
    P = dict(g_pre_mix=g_pre_mix, w_in=w_in, g_mla_q=g_mla_q, w_mla_uq=w_mla_uq, g_mla_kv=g_mla_kv,
             w_mla_ukv=w_mla_ukv, g_ret_gn=g_ret_gn, band_rel_bias=band_rel_bias, w_br_a=w_br_a,
             w_br_b=w_br_b, w_br_c=w_br_c, b_gate=b_gate, w_out=w_out, g_post_mix=g_post_mix,
             g_pre_mem=g_pre_mem, w_mem_q=w_mem_q, w_mem_o=w_mem_o, g_post_mem=g_post_mem,
             g_pre_ff=g_pre_ff, w_up=w_up, w_down=w_down, g_post_ff=g_post_ff)
    pos_p = jnp.arange(x_prompt.shape[1])
    pos_s = cache_mla_ckv.shape[2] + jnp.arange(x_sample.shape[1])
    xp, xs = x_prompt, x_sample
    new_p = [[] for _ in range(7)]
    new_s = [[] for _ in range(5)]
    for l in range(DEPTH):
        mk, mv = memory_kv(mem_prompt, g_mem[l], w_mem_k[l], w_mem_v[l])
        xp, st_p = trunk_layer(xp, pos_p, l, P, mk, mv, None)
        xs, st_s = trunk_layer(xs, pos_s, l, P, cache_mem_k[l], cache_mem_v[l],
                               (cache_mla_ckv[l], cache_mla_kpe[l], state_ret[l], cache_band_k[l], cache_band_v[l]))
        for acc, t in zip(new_p, st_p + (mk, mv)):
            acc.append(t)
        for acc, t in zip(new_s, st_s):
            acc.append(t)
    stack = lambda ts: jnp.stack(ts, axis=0)
    return (xp, xs,
            stack(new_p[0]), stack(new_p[1]), stack(new_p[2]), stack(new_p[3]), stack(new_p[4]),
            stack(new_p[5]), stack(new_p[6]),
            stack(new_s[0]), stack(new_s[1]), stack(new_s[2]), stack(new_s[3]), stack(new_s[4]))


_drawn_inputs = setup_inputs


def setup_inputs(seed=0):
    import zlib

    import numpy as np

    out = dict(_drawn_inputs(seed))
    spreads = {}
    factors = {'g_mla_q': 6.287, 'b_gate': 7.125}
    for name, (base, spread) in spreads.items():
        noise = np.random.default_rng([zlib.crc32(name.encode()), seed]).standard_normal(out[name].shape)
        drawn = base * np.exp(spread * noise) if base else spread * noise
        out[name] = __import__('jax').numpy.asarray(drawn.astype(out[name].dtype))
    for name, factor in factors.items():
        out[name] = (out[name] * factor).astype(out[name].dtype)
    return out
```

```python
from contextlib import ExitStack

import numpy as np

import concourse.bass as bass
from concourse import mybir

F32 = mybir.dt.float32
F32R = mybir.dt.float32r
ALU = mybir.AluOpType
ACT = mybir.ActivationFunctionType
AX_X = mybir.AxisListType.X

P = 128
DEPTH = 2
D = 1024
SEQ, DEC, PAST, MEM = 512, 64, 256, 256
NT = SEQ + DEC
HALF = NT // 2
KEYS = NT + PAST
KT = D // P
MLA_HEADS, NOPE, ROPE, MLA_V = 8, 64, 32, 64
QK = NOPE + ROPE
QR, CR = 384 // P, 256 // P
RET_HEADS, RET_DK, RET_DV = 4, 64, 128
BAND_HEADS, BAND_HD = 8, 64
MEM_HEADS, MEM_HD = 4, 128
FF = 4 * D
FF_CHUNKS = FF // D
OT = 512 // P
CHUNK = 64
EPS = 1e-6
NEG = -1e30

U_MLA_IN = QR + CR + 1
U_BRANCH = KT + KT // 2
U_RET = 2 * (2 + 2 * 2)
U_BAND = 4 * 3
U_MEM = MEM_HEADS * 3
U_FF = 2 * FF // P
_UNITS = U_MLA_IN + MLA_HEADS + 3 * U_BRANCH + U_RET + U_BAND + KT + U_MEM + KT // 2 + U_FF
UNITS = (_UNITS + 3) // 4 * 4
SPARE = UNITS - _UNITS
RING, RAW = 4, 2
LEAD = RING

GAINS = {}
_c = 0
for _n, _w in (("pre_mix", KT), ("post_mix", KT), ("pre_mem", KT), ("mem", KT), ("post_mem", KT),
               ("pre_ff", KT), ("post_ff", KT), ("mla_q", QR), ("mla_kv", CR), ("ret_gn", RET_HEADS),
               ("b_gate", 3 * KT)):
    GAINS[_n] = _c
    _c += _w
NGAIN = _c

CONST = {}
_c = 0
for _n, _w in (("ident", P), ("ones", P), ("rot_ret", P), ("rot_pe", P), ("first", P), ("neg", P),
               ("cross", 2 * P), ("decay", RET_HEADS * P), ("w_prompt", RET_HEADS), ("w_sample", RET_HEADS),
               ("g_prompt", 2), ("g_sample", 2)):
    CONST[_n] = _c
    _c += _w
NCONST = _c

Q_TILES = [(i * P, P, [(0, (i + 1) * P)], [(j * P, P, j) for j in range(i + 1)]) for i in range(SEQ // P)]
Q_TILES.append((SEQ, DEC, [(NT, PAST), (SEQ, DEC)], [(0, P, 4), (P, P, 5), (2 * P, DEC, 6)]))
MEM_TILES = [(i * P, P, [(0, MEM)], [(0, P, 0), (P, P, 1)]) for i in range(SEQ // P)]
MEM_TILES.append((SEQ, DEC, [(MEM, MEM)], [(0, P, 2), (P, P, 3)]))
NQ = len(Q_TILES)
V_TOKENS = [(i * P, P, i) for i in range(SEQ // P)]
ITEMS = (MLA_HEADS + BAND_HEADS + MEM_HEADS) * NQ
I_BAND = MLA_HEADS * NQ
I_MEM = I_BAND + BAND_HEADS * NQ

HALVES = [(0, HALF, 0), (512, HALF, HALF)]

JOBS = 258
DVE_FREED = JOBS - 3 * KT
GATES = 3 * KT + RET_HEADS
REQS = 25
READY = 27
STORES = 2 + 2 * 2 + 2 * (BAND_HEADS // 2) + 2 * MEM_HEADS
PHASES = 4


def build(nc, x_in, mem_in, w_in, ckv_in, kpe_in, state_in, bandk_in, bandv_in, memk_in, memv_in,
          bias_in, gain_in, const_in, rope_in, y_out, ckv_out, kpe_out, retp_out, rets_out,
          bandk_out, bandv_out, memk_out, memv_out):
    with ExitStack() as ctx:
        def sb(name, cols, dt=F32):
            return ctx.enter_context(nc.sbuf_tensor(name, [P, cols], dt))

        def bank(name, n):
            return ctx.enter_context(nc.psum_tensor(name, [P, 512 * n], F32))

        def sem(name):
            return ctx.enter_context(nc.semaphore(name))

        def tiles(ap, k):
            return ap.rearrange("p (k n) -> p k n", k=k)

        x_sb = sb("x", KT * NT)
        m_sb = sb("m", KT * NT)
        tmp_sb = sb("tmp", 2 * NT)
        rstd = sb("rstd", NT)
        q_sb = sb("q", 2 * NT)
        k_sb = sb("k", 2 * KEYS)
        v_sb = sb("v", 2 * 7 * P)
        prob_sb = sb("prob", 2 * 512)
        probT = sb("probT", 512)
        bias_sb = sb("bias", 2 * 512)
        cs_sb = sb("cs", 2 * NT)
        const = sb("const", NCONST)
        gain = sb("gain", NGAIN)
        small = sb("small", 16)
        raw = sb("raw", RAW * D)
        w_hi = sb("w_hi", RING * D, F32R)
        w_lo = sb("w_lo", RING * D, F32R)
        arena = sb("arena", 3 * KT * NT + 2 * QR * NT + 2 * CR * KEYS, F32R)

        X, M = tiles(x_sb[:, :], KT), tiles(m_sb[:, :], KT)
        TMP, Q, K = tiles(tmp_sb[:, :], 2), tiles(q_sb[:, :], 2), tiles(k_sb[:, :], 2)
        V = v_sb[:, :].rearrange("p (s t n) -> p s t n", s=2, t=7)
        PROB, BIAS = tiles(prob_sb[:, :], 2), tiles(bias_sb[:, :], 2)
        COS, SIN = cs_sb[:, 0:NT], cs_sb[:, NT:2 * NT]
        SQ = Q
        vT = tmp_sb[:, 0:KEYS]
        RAWS = tiles(raw[:, :], RAW)
        WHI, WLO = tiles(w_hi[:, :], RING), tiles(w_lo[:, :], RING)
        ZQ = tiles(m_sb[:, 0:QR * NT], QR)
        CKV = tiles(m_sb[:, QR * NT:QR * NT + CR * KEYS], CR)
        ST = tiles(k_sb[:, KEYS:KEYS + 6 * P], 6)
        KW = V[:, 1]
        QX = Q[:, 1]

        U0, O0, Z0 = 0, 2 * KT * NT, 3 * KT * NT

        def region(start, k, n):
            return tiles(arena[:, start:start + k * n], k)

        U_HL = region(U0, KT, NT), region(U0 + KT * NT, KT, NT)
        O_HL = region(O0, OT, NT), region(O0 + OT * NT, OT, NT)
        ZQ_HL = region(Z0 - 0, QR, NT), region(Z0 + QR * NT, QR, NT)
        CKV_HL = region(Z0 + 2 * QR * NT, CR, KEYS), region(Z0 + 2 * QR * NT + CR * KEYS, CR, KEYS)
        H_HL = region(O0, KT, NT), region(Z0, KT, NT)
        MEM_HL = region(Z0, KT, MEM), region(Z0 + KT * MEM, KT, MEM)

        job_ps = [bank(f"job{i}", 2) for i in range(2)]
        score_ps = [bank(f"score{i}", 1) for i in range(2)]
        turn_ps = bank("turn", 1)
        out_ps = bank("outp", 1)

        def halves(ap):
            return ap.rearrange("p (b n) -> p b n", b=2)

        def job_halves(s, p0=0, p1=P):
            return halves(job_ps[s][p0:p1, :])[:, :, 0:HALF]

        def cst(name, i=0, w=1, p0=0, p1=P):
            return const[p0:p1, CONST[name] + i:CONST[name] + i + w]

        def g_col(name, i):
            return gain[:, GAINS[name] + i:GAINS[name] + i + 1]

        IDENT = cst("ident", 0, P)
        ONES = cst("ones", 0, P)

        raw_loaded = [sem(f"raw_loaded{i}") for i in range(RAW)]
        hi_done, lo_done = sem("hi_done"), sem("lo_done")
        job_done, job_free, gate_done = sem("job_done"), sem("job_free"), sem("gate_done")
        sq_ready, sq_used = sem("sq_ready"), sem("sq_used")
        act_asked, act_done = sem("act_asked"), sem("act_done")
        ready = sem("ready")
        score_done, negmax, exp_done, probs = sem("score_done"), sem("negmax"), sem("exp_done"), sem("probs")
        turn_done, turned, out_done, out_free = sem("turn_done"), sem("turned"), sem("out_done"), sem("out_free")
        x_loaded, c_loaded = sem("x_loaded"), sem("c_loaded")
        layer_loaded, r_loaded = sem("layer_loaded"), sem("r_loaded")
        kv_loaded = [sem(f"kv_loaded{i}") for i in range(2)]
        b_loaded = [sem(f"b_loaded{i}") for i in range(2)]
        mem_loaded = sem("mem_loaded")
        store_asked, stored = sem("store_asked"), sem("stored")
        phase_done = sem("phase_done")

        settled = [sem(f"settled_{e}") for e in ("pe", "dve")]

        block = ctx.enter_context(nc.Block())

        @block.tensor
        def _(pe):
            pe.sem_inc(job_done, 1)
            pe.sem_inc(sq_used, 1)
            pe.sem_inc(out_done, 1)
            pe.wait_ge(c_loaded, 16)
            with pe.Fori(0, DEPTH) as l:
                n = dict(job=0, unit=0, freed=0, gate=0, sq=0, squ=0, ready=0, item=0)
                at = dict(job=0, unit=0)
                owner = [("job_free", -2), ("job_free", -1)]

                def slot(freed_by="dve"):
                    s = n["job"] % 2
                    who, i = owner[s]
                    if who == "job_free":
                        pe.wait_ge(job_free, l * DVE_FREED + at["job"] + i + 3)
                    else:
                        pe.wait_ge(gate_done, l * GATES + i + 1)
                    if freed_by == "dve":
                        owner[s] = ("job_free", n["freed"])
                        n["freed"] += 1
                    else:
                        owner[s] = ("gate", n["gate"])
                        n["gate"] += 1
                    n["job"] += 1
                    return job_ps[s]

                def evicted():
                    pe.wait_ge(job_free, l * DVE_FREED + at["job"] + n["freed"] + 2)

                def settle():
                    pe.sem_inc(settled[0], 1)

                def wait_ready():
                    n["ready"] += 1
                    pe.wait_ge(ready, l * READY + n["ready"])

                def unit():
                    pe.wait_ge(lo_done, l * UNITS + at["unit"] + n["unit"] + 3)
                    s = n["unit"] % RING
                    n["unit"] += 1
                    return s

                def project(s, kt, hl, at_col=0, step=P, m=P, pieces=HALVES, each_ready=False, freed_by="dve",
                            k0=0):
                    ps = slot(freed_by)
                    for k in range(kt):
                        if each_ready and k % 2 == 0:
                            wait_ready()
                        c = at_col + k * step
                        for w, x in ((WHI, hl[0]), (WHI, hl[1]), (WLO, hl[0])):
                            for po, nn, so in pieces:
                                mm = pe.matmul(ps[0:m, po:po + nn], w[:, s, c:c + m], x[:, k, so:so + nn],
                                               start=(k == 0 and w is WHI and x is hl[0]),
                                               stop=(k == kt - 1 and w is WLO))
                    mm.then_inc(job_done, 1)

                def plain(lhsT, rhs, m=P, pieces=HALVES):
                    ps = slot()
                    for po, nn, so in pieces:
                        mm = pe.matmul(ps[0:m, po:po + nn], lhsT, rhs[:, so:so + nn], start=True, stop=True)
                    mm.then_inc(job_done, 1)

                def stat(kt, pieces=HALVES):
                    ps = slot()
                    for k in range(kt):
                        n["sq"] += 1
                        pe.wait_ge(sq_ready, l * SQUARES + n["sq"])
                        for po, nn, so in pieces:
                            mm = pe.matmul(ps[:, po:po + nn], ONES, SQ[:, k % 2, so:so + nn],
                                           start=(k == 0), stop=(k == kt - 1))
                        if k < kt - 2:
                            mm.then_inc(sq_used, 1)
                    mm.then_inc(job_done, 1)

                def turn_values(toks):
                    evicted()
                    ps = slot()
                    for c, w, t in toks:
                        o = (t // 4) * 512 + (t % 4) * P
                        mm = pe.transpose(ps[0:w, o:o + P], vT[:, c:c + w], IDENT)
                    mm.then_inc(job_done, 1)

                def scores(i, head):
                    qs, q0, kr, mask, tile = head["q"], head["rows"][0], head["rows"], head["mask"], head["tiles"]
                    t0, nq, segs, _ = tile[i]
                    it = n["item"]
                    s = it % 2
                    pe.wait_ge(probs, l * ITEMS + it + 1)
                    if nq < P:
                        settle()
                    o = 0
                    for c, w in segs:
                        msk = mask and nq == P
                        mm = pe.matmul(score_ps[s][0:nq, o:o + w], Q[kr[0]:kr[1], qs, t0:t0 + nq],
                                       K[kr[0]:kr[1], head["k"], c:c + w], start=True, stop=not msk)
                        if msk:
                            mm = pe.matmul(score_ps[s][0:nq, w - P:w], cst("first", 0, P, 0, 1),
                                           cst("neg", 0, P, 0, 1), start=False, stop=True)
                        o += w
                    mm.then_inc(score_done, 1)
                    n["item"] += 1

                def turn_and_sum(it, i, head):
                    t0, nq, _, kts = head["tiles"][i]
                    pe.wait_ge(probs, l * ITEMS + it + 3)
                    pe.wait_ge(turned, l * ITEMS + it + 1)
                    if nq < P:
                        settle()
                    for j, (c, w, _) in enumerate(kts):
                        mm = pe.transpose(turn_ps[0:w, j * P:j * P + nq], PROB[0:nq, it % 2, c:c + w],
                                          cst("ident", 0, nq, 0, nq))
                    mm.then_inc(turn_done, 1)
                    pe.wait_ge(turned, l * ITEMS + it + 2)
                    pe.wait_ge(out_free, l * ITEMS + it + 1)
                    v0, v1, o0 = head["v"]
                    for j, (c, w, t) in enumerate(kts):
                        mm = pe.matmul(out_ps[o0:o0 + v1 - v0, 0:nq], V[0:w, head["vs"], t, v0:v1],
                                       probT[0:w, j * P:j * P + nq], start=(j == 0), stop=(j == len(kts) - 1))
                    mm.then_inc(out_done, 1)

                def attend(heads, prep):
                    flat = [(h, i) for h in heads for i in range(NQ)]
                    base = n["item"]
                    prep(0)
                    evicted()
                    scores(0, flat[0][0])
                    for j, (h, i) in enumerate(flat):
                        if "prep" in h and i == 1:
                            prep(h["prep"])
                        if j + 1 < len(flat):
                            if i == NQ - 1:
                                evicted()
                            scores(flat[j + 1][1], flat[j + 1][0])
                        turn_and_sum(base + j, i, h)
                    pe.wait_ge(out_free, l * ITEMS + n["item"] + 1)

                def branch():
                    for e2 in range(KT // 2):
                        for e in range(2):
                            project(unit(), KT, U_HL, freed_by="act")
                        s = unit()
                        for e in range(2):
                            project(s, OT, O_HL, at_col=e * OT * P)

                stat(KT)
                for i in range(QR + CR + 1):
                    project(unit(), KT, U_HL, each_ready=(i == 0))
                stat(QR)
                stat(CR)
                evicted()
                plain(cst("rot_pe", 0, QK, 0, QK), TMP[0:QK, 0], m=QK)
                wait_ready()

                def prep_mla(h):
                    s = unit()
                    project(s, QR, ZQ_HL, step=QK, m=QK)
                    project(s, CR, CKV_HL, at_col=QR * QK)
                    project(s, CR, CKV_HL, at_col=QR * QK, pieces=[(0, PAST, NT)])
                    pe.wait_ge(job_free, l * DVE_FREED + at["job"] + n["freed"] + 2 - 2)
                    plain(cst("rot_pe", 0, QK, 0, QK), Q[0:QK, h % 2], m=QK)
                    turn_values(V_TOKENS + [(NT, P, 4), (NT + P, P, 5), (SEQ, DEC, 6)])

                heads = [dict(q=h % 2, k=h % 2, rows=(0, QK), mask=True, tiles=Q_TILES, vs=h % 2,
                              v=(0, MLA_V, (h % 2) * MLA_V)) for h in range(MLA_HEADS)]
                for h in range(MLA_HEADS - 1):
                    heads[h]["prep"] = h + 1
                attend(heads, prep_mla)
                branch()

                for p in range(RET_HEADS // 2):
                    project(unit(), KT, U_HL)
                    project(unit(), KT, U_HL)
                    evicted()
                    plain(cst("rot_ret", 0, P), Q[:, 0])
                    plain(cst("rot_ret", 0, P), K[:, 0])
                    evicted()
                    ps = slot()
                    for c, w, t in V_TOKENS + [(SEQ, DEC, 4)]:
                        mm = pe.transpose(ps[0:w, t * P:(t + 1) * P], K[:, 0, c:c + w], IDENT)
                    mm.then_inc(job_done, 1)
                    for j in range(2):
                        r0, r1 = j * RET_DK, (j + 1) * RET_DK
                        project(unit(), KT, U_HL)
                        turn_values(V_TOKENS + [(SEQ, DEC, 4)])
                        ps = slot()
                        for c, w, t in V_TOKENS + [(SEQ, DEC, 4)]:
                            mm = pe.matmul(ps[0:w, t * P:t * P + w], K[r0:r1, 0, c:c + w], Q[r0:r1, 0, c:c + w],
                                           start=True, stop=True)
                        mm.then_inc(job_done, 1)
                        evicted()
                        ps = slot()
                        for c, w, t in V_TOKENS + [(SEQ, DEC, 4)]:
                            mm = pe.matmul(ps[r0:r1, t * P:(t + 1) * P], KW[0:w, t, r0:r1], V[0:w, 0, t, :],
                                           start=True, stop=True)
                        mm.then_inc(job_done, 1)
                        wait_ready()
                        ps = slot()
                        for c, w, t in V_TOKENS + [(SEQ, DEC, 4)]:
                            cross = t > 0
                            mm = pe.matmul(ps[:, t * P:t * P + w], V[:, 0, t, :], prob_sb[:, t * P:t * P + w],
                                           start=True, stop=not cross)
                            if cross:
                                st = ST[r0:r1, t - 1 if t < 4 else 4, :]
                                mm = pe.matmul(ps[:, t * P:t * P + w], st, QX[r0:r1, c:c + w],
                                               start=False, stop=True)
                        mm.then_inc(job_done, 1)
                        evicted()
                        plain(ONES, TMP[:, 0])
                        wait_ready()
                        plain(ONES, TMP[:, 0])
                        project(unit(), KT, U_HL)
                        n["gate"] += 1
                wait_ready()
                branch()

                def prep_band(p):
                    for _ in range(3):
                        project(unit(), KT, U_HL)
                    turn_values(V_TOKENS + [(SEQ, DEC, 6)])
                    pe.wait_ge(kv_loaded[p % 2], (l * 4 + p // 2 + 1) * 32)

                heads = [dict(q=h // 2 % 2, k=h // 2 % 2, rows=((h % 2) * 64, (h % 2) * 64 + 64), mask=False,
                              tiles=Q_TILES, vs=h // 2 % 2, v=((h % 2) * 64, (h % 2) * 64 + 64, (h % 2) * 64))
                         for h in range(BAND_HEADS)]
                for p in range(BAND_HEADS // 2 - 1):
                    heads[2 * p + 1]["prep"] = p + 1
                attend(heads, prep_band)
                branch()

                for e in range(KT):
                    project(unit(), KT, U_HL, each_ready=(e == 0))
                stat(KT)

                stat(KT, [(0, MEM, 0)])
                stat(KT)

                def prep_mem(h):
                    project(unit(), KT, MEM_HL, pieces=[(0, MEM, 0)])
                    project(unit(), KT, MEM_HL, pieces=[(0, MEM, 0)])
                    turn_values([(0, P, 0), (P, P, 1)])
                    project(unit(), KT, U_HL, each_ready=(h == 0))
                    pe.wait_ge(kv_loaded[h % 2], (l * 4 + 2 + h // 2 + 1) * 32)

                heads = [dict(q=h % 2, k=h % 2, rows=(0, P), mask=False, tiles=MEM_TILES, vs=h % 2, v=(0, P, 0))
                         for h in range(MEM_HEADS)]
                for h in range(MEM_HEADS - 1):
                    heads[h]["prep"] = h + 1
                wait_ready()
                attend(heads, prep_mem)
                for e2 in range(KT // 2):
                    s = unit()
                    for e in range(2):
                        project(s, OT, O_HL, at_col=e * OT * P)
                stat(KT)

                stat(KT)
                for _ in range(4):
                    wait_ready()
                settle()
                with pe.Fori(0, FF_CHUNKS) as c:
                    at["job"], at["unit"] = c * (2 * KT), c * (2 * KT)
                    for e in range(KT):
                        project(unit(), KT, U_HL)
                    for e in range(KT):
                        if e == 0:
                            evicted()
                        project(unit(), KT, H_HL)
                at["job"] = at["unit"] = 0
                n["unit"] += (FF_CHUNKS - 1) * 2 * KT
                for k in ("job", "freed"):
                    n[k] += (FF_CHUNKS - 1) * 2 * KT
                owner[n["job"] % 2], owner[1 - n["job"] % 2] = [("job_free", n["freed"] - i) for i in (2, 1)]
                stat(KT)
                if n["job"] % 2:
                    plain(cst("ident", 0, P), TMP[:, 0], pieces=[(0, P, 0)])
                for _ in range(SPARE):
                    unit()
                counted(**n)

        @block.gpsimd
        def _(pool):
            pool.sem_inc(lo_done, 2)

            def lo(g, u):
                pool.wait_ge(hi_done, g + 1)
                nc.gpsimd.tensor_tensor(WLO[:, u % RING, :], RAWS[:, u % RAW, :], WHI[:, u % RING, :].bitcast(F32),
                                        ALU.subtract).then_inc(lo_done, 1)

            with pool.Fori(0, DEPTH * UNITS, RING) as g:
                for j in range(RING):
                    lo(g + j, j)
            for j in range(LEAD - 1):
                lo(DEPTH * UNITS + j, j)

        @block.scalar
        def _(act):
            def load(g, u):
                act.dma_start(RAWS[:, u % RAW, :], w_in[bass.ds(g, 1)].rearrange("a p n -> p (a n)"))\
                    .then_inc(raw_loaded[u % RAW], 16)

            def hi(g, turn, u):
                act.wait_ge(raw_loaded[u % RAW], (turn + u // RAW + 1) * 16)
                act.activation(WHI[:, u % RING, :], RAWS[:, u % RAW, :], ACT.Copy).then_inc(hi_done, 1)

            load(0, 0)
            load(1, 1)
            for u in range(LEAD - 1):
                hi(u, 0, u)
                act.wait_ge(lo_done, u + 3)
                if u < 2:
                    load(u + 2, u + 2)
            act.wait_ge(c_loaded, 16)
            act.wait_ge(x_loaded, 16)
            with act.Fori(0, DEPTH) as l:
                n = dict(job=0, unit=0, gate=0, squ=0, sq=0, ask=0, item=0)
                at = dict(job=0, unit=0)

                def place():
                    u = n["unit"]
                    act.wait_ge(job_done, l * JOBS + at["job"] + n["job"] + 1)
                    hi(None, l * (UNITS // RAW) + at["unit_raw"], u + 3)
                    act.wait_ge(lo_done, l * UNITS + at["unit"] + u + 2 + 1 + 2)
                    load(l * UNITS + at["unit"] + (u + 4), u + 4)
                    n["unit"] += 1

                at["unit_raw"] = 0

                def asked():
                    n["ask"] += 1
                    act.wait_ge(act_asked, l * REQS + n["ask"])

                def squares(src, kt, w=NT):
                    asked()
                    for k in range(kt):
                        if k >= 2:
                            n["squ"] += 1
                            act.wait_ge(sq_used, l * SQ_USES + n["squ"] + 1)
                        act.activation(SQ[:, k % 2, 0:w], src(k), ACT.Square).then_inc(sq_ready, 1)
                    n["job"] += 1
                    root(rstd[:, 0:w])

                def root(ap):
                    asked()
                    act.activation(ap, ap, ACT.Sqrt).then_inc(act_done, 1)

                def exps(i, head):
                    it = n["item"]
                    _, nq, segs, _ = head["tiles"][i]
                    w = sum(s[1] for s in segs)
                    act.wait_ge(negmax, l * ITEMS + it + 1)
                    src = score_ps[it % 2][0:nq, 0:w] if head["scale"] else PROB[0:nq, it % 2, 0:w]
                    act.activation(PROB[0:nq, it % 2, 0:w], src, ACT.Exp,
                                   bias=small[0:nq, it % 2 * 4 + 1:it % 2 * 4 + 2], scale=head["scale"] or 1.0,
                                   accum_out=small[0:nq, it % 2 * 4 + 2:it % 2 * 4 + 3]).then_inc(exp_done, 1)
                    n["item"] += 1

                def attend(heads, prep):
                    flat = [(h, i) for h in heads for i in range(NQ)]
                    prep(0)
                    exps(0, flat[0][0])
                    for j, (h, i) in enumerate(flat):
                        if "prep" in h and i == 1:
                            prep(h["prep"])
                        if j + 1 < len(flat):
                            exps(flat[j + 1][1], flat[j + 1][0])

                def branch(b):
                    asked()
                    for e in range(KT):
                        place()
                        n["job"] += 1
                        act.wait_ge(job_done, l * JOBS + n["job"] + 1)
                        act.activation(halves(TMP[:, e % 2]), job_halves((n["job"] - 1) % 2), ACT.Sigmoid,
                                       bias=g_col("b_gate", b * KT + e)).then_inc(gate_done, 1)
                        n["gate"] += 1
                        if e % 2:
                            place()
                            n["job"] += 2

                squares(lambda k: X[:, k], KT)
                for _ in range(U_MLA_IN):
                    place()
                    n["job"] += 1
                squares(lambda k: ZQ[:, k], QR)
                squares(lambda k: CKV[:, k, 0:NT], CR)
                n["job"] += 1

                def prep_mla(h):
                    place()
                    n["job"] += 5

                heads = [dict(tiles=Q_TILES, scale=QK ** -0.5) for h in range(MLA_HEADS)]
                for h in range(MLA_HEADS - 1):
                    heads[h]["prep"] = h + 1
                attend(heads, prep_mla)
                branch(0)

                for p in range(RET_HEADS // 2):
                    place()
                    n["job"] += 1
                    place()
                    n["job"] += 1 + 2 + 1
                    for j in range(2):
                        place()
                        n["job"] += 5
                        n["job"] += 2
                        root(rstd[:, :])
                        place()
                        n["job"] += 1
                        act.wait_ge(job_done, l * JOBS + n["job"] + 1)
                        act.activation(halves(TMP[:, 0]), job_halves((n["job"] - 1) % 2), ACT.Sigmoid)\
                            .then_inc(gate_done, 1)
                        n["gate"] += 1
                branch(1)

                def prep_band(p):
                    for _ in range(3):
                        place()
                        n["job"] += 1
                    n["job"] += 1

                heads = [dict(tiles=Q_TILES, scale=None) for h in range(BAND_HEADS)]
                for p in range(BAND_HEADS // 2 - 1):
                    heads[2 * p + 1]["prep"] = p + 1
                attend(heads, prep_band)
                branch(2)

                for _ in range(KT):
                    place()
                    n["job"] += 1
                squares(lambda k: M[:, k], KT)
                squares(lambda k: M[:, k, 0:MEM], KT, MEM)
                squares(lambda k: X[:, k], KT)

                def prep_mem(h):
                    place()
                    n["job"] += 1
                    place()
                    n["job"] += 1 + 1
                    place()
                    n["job"] += 1

                heads = [dict(tiles=MEM_TILES, scale=MEM_HD ** -0.5) for h in range(MEM_HEADS)]
                for h in range(MEM_HEADS - 1):
                    heads[h]["prep"] = h + 1
                attend(heads, prep_mem)
                for _ in range(KT // 2):
                    place()
                    n["job"] += 2
                squares(lambda k: M[:, k], KT)
                squares(lambda k: X[:, k], KT)
                with act.Fori(0, FF_CHUNKS) as c:
                    at["job"], at["unit"], at["unit_raw"] = c * (2 * KT), c * (2 * KT), c * (2 * KT // RAW)
                    for _ in range(2 * KT):
                        place()
                        n["job"] += 1
                at["job"] = at["unit"] = at["unit_raw"] = 0
                n["unit"] += (FF_CHUNKS - 1) * 2 * KT
                n["job"] += (FF_CHUNKS - 1) * 2 * KT
                squares(lambda k: M[:, k], KT)
                n["job"] += n["job"] % 2
                for _ in range(SPARE):
                    place()
                counted(**n)
            for s in range(RAW):
                act.wait_ge(raw_loaded[s], (DEPTH * UNITS + LEAD) // RAW * 16)

        @block.vector
        def _(dve):
            v = nc.vector
            dve.sem_inc(job_free, 2)
            dve.sem_inc(probs, 2)
            dve.sem_inc(turned, 1)
            dve.sem_inc(out_free, 1)
            dve.sem_inc(phase_done, 1)
            v.memset(small[:, :], 0.0)
            dve.drain()
            dve.wait_ge(x_loaded, 16)
            dve.wait_ge(c_loaded, 16)
            with dve.Fori(0, DEPTH) as l:
                n = dict(job=0, freed=0, gate=0, ready=0, ask=0, done=0, item=0, store=0)
                at = dict(job=0)

                def job():
                    n["job"] += 1
                    dve.wait_ge(job_done, l * JOBS + at["job"] + n["job"] + 1)
                    return (n["job"] - 1) % 2

                def skip():
                    n["job"] += 1

                def free(ins):
                    n["freed"] += 1
                    ins.then_inc(job_free, 1)

                def is_ready(ins):
                    n["ready"] += 1
                    ins.then_inc(ready, 1)

                def ask(ins):
                    n["ask"] += 1
                    ins.then_inc(act_asked, 1)

                def wait_act():
                    n["done"] += 1
                    dve.wait_ge(act_done, l * ROOTS + n["done"])

                def split(src, hi, lo):
                    v.tensor_copy(hi, src)
                    dve.drain()
                    return v.tensor_tensor(lo, src, hi.bitcast(F32), ALU.subtract)

                def copy_job(dst, p0=0, p1=P):
                    s = job()
                    free(v.tensor_copy(halves(dst), job_halves(s, p0, p1)))

                def store(ins=None):
                    n["store"] += 1
                    dve.drain()
                    dve.sem_inc(store_asked, 1)

                def wait_stores():
                    dve.wait_ge(stored, (l * STORES + n["store"]) * 16)

                def inv_root(scale, w=NT):
                    s = job()
                    if w == NT:
                        dst, src = halves(rstd[:, :]), job_halves(s)
                    else:
                        dst, src = rstd[:, 0:w], job_ps[s][:, 0:w]
                    free(v.tensor_scalar(dst, src, scale, EPS, ALU.mult, ALU.add))
                    dve.drain()
                    dve.sem_inc(act_asked, 1)
                    n["ask"] += 1
                    wait_act()
                    v.reciprocal(rstd[:, 0:w], rstd[:, 0:w])
                    dve.drain()

                def squares_may_start():
                    dve.drain()
                    dve.sem_inc(act_asked, 1)
                    n["ask"] += 1

                def norm_split(src, name, kt, hl, w=NT, each=True):
                    for k in range(0, kt, 2):
                        for j in range(2):
                            v.scalar_tensor_tensor(out=TMP[:, j, 0:w], in0=src(k + j), scalar=g_col(name, k + j),
                                                   in1=rstd[:, 0:w], op0=ALU.mult, op1=ALU.mult)
                        dve.drain()
                        ins = split(TMP[:, :, 0:w], hl[0][:, k:k + 2], hl[1][:, k:k + 2])
                        if each:
                            is_ready(ins)
                        dve.drain()
                    if not each:
                        is_ready(v.tensor_copy(small[:, 12:13], small[:, 13:14]))

                def post_norm(name):
                    squares_may_start()
                    inv_root(1.0 / D)
                    for k in range(0, KT, 2):
                        for j in range(2):
                            v.scalar_tensor_tensor(out=TMP[:, j], in0=M[:, k + j], scalar=g_col(name, k + j),
                                                   in1=rstd[:, :], op0=ALU.mult, op1=ALU.mult)
                        dve.drain()
                        v.tensor_tensor(X[:, k:k + 2], X[:, k:k + 2], TMP, ALU.add)
                        dve.drain()

                def rope(buf, p0, p1, scale=None):
                    s = job()
                    free(v.tensor_tensor(halves(rstd[p0:p1, :]), job_halves(s, p0, p1), halves(SIN[p0:p1, :]),
                                         ALU.mult))
                    v.tensor_tensor(buf[p0:p1, :], buf[p0:p1, :], COS[p0:p1, :], ALU.mult)
                    dve.drain()
                    if scale is None:
                        return v.tensor_tensor(buf[p0:p1, :], buf[p0:p1, :], rstd[p0:p1, :], ALU.add)
                    v.tensor_tensor(buf[p0:p1, :], buf[p0:p1, :], rstd[p0:p1, :], ALU.add)
                    dve.drain()
                    return v.tensor_scalar(buf[p0:p1, :], buf[p0:p1, :], scale, None, ALU.mult)

                def maxima(i, head):
                    it = n["item"]
                    s = it % 2
                    t0, nq, segs, _ = head["tiles"][i]
                    w = sum(x[1] for x in segs)
                    dve.wait_ge(score_done, l * ITEMS + it + 1)
                    src = score_ps[s][0:nq, 0:w]
                    if head["bias"] is not None:
                        h = head["bias"]
                        if i == 0:
                            dve.wait_ge(b_loaded[h % 2], (l * 4 + h // 2 + 1) * 16)
                        b0 = 512 - w if nq == P else P
                        v.scalar_tensor_tensor(out=PROB[0:nq, s, 0:w], in0=src, scalar=BAND_HD ** -0.5,
                                               in1=BIAS[0:nq, h % 2, b0:b0 + w], op0=ALU.mult, op1=ALU.add)
                        dve.drain()
                        src = PROB[0:nq, s, 0:w]
                    v.reduce_max(small[0:nq, s * 4:s * 4 + 1], src, AX_X)
                    dve.drain()
                    v.tensor_scalar(small[0:nq, s * 4 + 1:s * 4 + 2], small[0:nq, s * 4:s * 4 + 1],
                                    -(head["scale"] or 1.0), None, ALU.mult).then_inc(negmax, 1)
                    n["item"] += 1

                def finish(it, i, head):
                    s = it % 2
                    t0, nq, segs, kts = head["tiles"][i]
                    w = sum(x[1] for x in segs)
                    dve.wait_ge(exp_done, l * ITEMS + it + 1)
                    v.reciprocal(small[0:nq, s * 4 + 3:s * 4 + 4], small[0:nq, s * 4 + 2:s * 4 + 3])
                    dve.drain()
                    v.tensor_scalar(PROB[0:nq, s, 0:w], PROB[0:nq, s, 0:w], small[0:nq, s * 4 + 3:s * 4 + 4], None,
                                    ALU.mult).then_inc(probs, 1)
                    dve.wait_ge(turn_done, l * ITEMS + it + 1)
                    dve.wait_ge(out_done, l * ITEMS + it + 1)
                    full = [k for k in kts if k[1] == P]
                    part = [k for k in kts if k[1] < P]
                    a = probT[:, 0:len(full) * P].rearrange("p (k n) -> p k n", n=P)[:, :, 0:nq]
                    b = turn_ps[:, 0:len(full) * P].rearrange("p (k n) -> p k n", n=P)[:, :, 0:nq]
                    ins = v.tensor_copy(a, b)
                    for k in part:
                        j = len(full)
                        ins = v.tensor_copy(probT[0:k[1], j * P:j * P + nq], turn_ps[0:k[1], j * P:j * P + nq])
                    ins.then_inc(turned, 1)
                    dve.wait_ge(out_done, l * ITEMS + it + 2)
                    ot, o0, o1 = head["o"]
                    split(out_ps[o0:o1, 0:nq], O_HL[0][o0:o1, ot, t0:t0 + nq], O_HL[1][o0:o1, ot, t0:t0 + nq])\
                        .then_inc(out_free, 1)

                def attend(heads, prep):
                    flat = [(h, i) for h in heads for i in range(NQ)]
                    base = n["item"]
                    prep(0)
                    maxima(0, flat[0][0])
                    for j, (h, i) in enumerate(flat):
                        if "prep" in h and i == 1:
                            prep(h["prep"])
                        if j + 1 < len(flat):
                            maxima(flat[j + 1][1], flat[j + 1][0])
                        finish(base + j, i, h)

                def branch(first):
                    squares_may_start()
                    for e in range(KT):
                        if e % 2 == 0:
                            skip()
                            skip()
                        s = job()
                        n["gate"] += 1
                        dve.wait_ge(gate_done, l * GATES + n["gate"])
                        if first:
                            free(v.tensor_tensor(halves(M[:, e]), job_halves(s), halves(TMP[:, e % 2]), ALU.mult))
                        else:
                            v.tensor_tensor(halves(TMP[:, e % 2]), job_halves(s), halves(TMP[:, e % 2]), ALU.mult)
                            dve.drain()
                            free(v.tensor_tensor(M[:, e], M[:, e], TMP[:, e % 2], ALU.add))

                dve.wait_ge(layer_loaded, (l + 1) * 16 * LAYER_LOADS)
                dve.sem_inc(settled[1], 1)
                squares_may_start()
                inv_root(1.0 / D)
                norm_split(lambda k: X[:, k], "pre_mix", KT, U_HL)
                for k in range(QR):
                    copy_job(ZQ[:, k])
                for k in range(CR):
                    copy_job(CKV[:, k, 0:NT])
                copy_job(TMP[:, 0])
                squares_may_start()
                inv_root(1.0 / (QR * P))
                for k in range(QR):
                    v.scalar_tensor_tensor(out=ZQ[:, k], in0=ZQ[:, k], scalar=g_col("mla_q", k), in1=rstd[:, :],
                                           op0=ALU.mult, op1=ALU.mult)
                squares_may_start()
                split(m_sb[:, 0:QR * NT], arena[:, Z0:Z0 + QR * NT], arena[:, Z0 + QR * NT:Z0 + 2 * QR * NT])
                dve.drain()
                inv_root(1.0 / (CR * P))
                for k in range(CR):
                    v.scalar_tensor_tensor(out=CKV[:, k, 0:NT], in0=CKV[:, k, 0:NT], scalar=g_col("mla_kv", k),
                                           in1=rstd[:, :], op0=ALU.mult, op1=ALU.mult)
                dve.drain()
                z = Z0 + 2 * QR * NT
                split(m_sb[:, QR * NT:QR * NT + CR * KEYS], arena[:, z:z + CR * KEYS],
                      arena[:, z + CR * KEYS:z + 2 * CR * KEYS])
                dve.drain()
                s = job()
                free(v.tensor_tensor(halves(rstd[NOPE:QK, :]), job_halves(s, NOPE, QK), halves(SIN[NOPE:QK, :]),
                                     ALU.mult))
                v.tensor_tensor(TMP[NOPE:QK, 0], TMP[NOPE:QK, 0], COS[NOPE:QK, :], ALU.mult)
                dve.drain()
                for b in range(2):
                    ins = v.tensor_tensor(K[NOPE:QK, b, 0:NT], TMP[NOPE:QK, 0], rstd[NOPE:QK, :], ALU.add)
                is_ready(ins)
                store()
                store()
                dve.drain()

                def prep_mla(h):
                    b = h % 2
                    copy_job(Q[0:QK, b], 0, QK)
                    s = job()
                    v.tensor_copy(halves(K[0:NOPE, b, 0:NT]), job_halves(s, 0, NOPE))
                    free(v.tensor_copy(halves(vT[:, 0:NT]), job_halves(s)))
                    s = job()
                    v.tensor_copy(K[0:NOPE, b, NT:KEYS], job_ps[s][0:NOPE, 0:PAST])
                    free(v.tensor_copy(vT[:, NT:KEYS], job_ps[s][:, 0:PAST]))
                    dve.drain()
                    rope_q(b)
                    s = job()
                    v.tensor_copy(V[:, b, 0:4, 0:MLA_V], tiles(job_ps[s][:, 0:512], 4)[:, :, NOPE:P])
                    v.tensor_copy(V[:, b, 4:6, 0:MLA_V], tiles(job_ps[s][:, 512:768], 2)[:, :, NOPE:P])
                    free(v.tensor_copy(V[0:DEC, b, 6, 0:MLA_V], job_ps[s][0:DEC, 768 + NOPE:768 + P]))

                def rope_q(b):
                    s = job()
                    v.tensor_tensor(halves(rstd[NOPE:QK, :]), job_halves(s, NOPE, QK), halves(SIN[NOPE:QK, :]),
                                    ALU.mult)
                    v.tensor_tensor(Q[NOPE:QK, b], Q[NOPE:QK, b], COS[NOPE:QK, :], ALU.mult)
                    dve.drain()
                    free(v.tensor_tensor(Q[NOPE:QK, b], Q[NOPE:QK, b], rstd[NOPE:QK, :], ALU.add))

                heads = [dict(tiles=Q_TILES, scale=QK ** -0.5, bias=None,
                              o=(h // 2, h % 2 * 64, h % 2 * 64 + 64)) for h in range(MLA_HEADS)]
                for h in range(MLA_HEADS - 1):
                    heads[h]["prep"] = h + 1
                attend(heads, prep_mla)
                dve.drain()
                wait_stores()
                dve.sem_inc(phase_done, 1)
                branch(True)

                dve.wait_ge(r_loaded, (l + 1) * 16 * RET_LOADS)
                v.memset(V[DEC:P, 0, 4, :], 0.0)
                v.memset(prob_sb[DEC:P, 512:512 + DEC], 0.0)
                for p in range(RET_HEADS // 2):
                    copy_job(Q[:, 0])
                    copy_job(K[:, 0, 0:NT])
                    dve.drain()
                    s = job()
                    v.tensor_tensor(halves(rstd[:, :]), job_halves(s), halves(SIN), ALU.mult)
                    v.tensor_tensor(Q[:, 0], Q[:, 0], COS, ALU.mult)
                    dve.drain()
                    free(v.tensor_tensor(Q[:, 0], Q[:, 0], rstd[:, :], ALU.add))
                    dve.drain()
                    for t in range(5):
                        w = P if t < 4 else DEC
                        v.tensor_tensor(QX[:, t * P:t * P + w], Q[:, 0, t * P:t * P + w], cst("cross", p * P, w),
                                        ALU.mult)
                    s = job()
                    v.tensor_tensor(halves(rstd[:, :]), job_halves(s), halves(SIN), ALU.mult)
                    v.tensor_tensor(K[:, 0, 0:NT], K[:, 0, 0:NT], COS, ALU.mult)
                    dve.drain()
                    v.tensor_tensor(K[:, 0, 0:NT], K[:, 0, 0:NT], rstd[:, :], ALU.add)
                    dve.drain()
                    free(v.tensor_scalar(K[:, 0, 0:NT], K[:, 0, 0:NT], RET_DK ** -0.5, None, ALU.mult))
                    s = job()
                    for j in range(2):
                        h, r0 = 2 * p + j, j * RET_DK
                        v.tensor_scalar(KW[:, 0:4, r0:r0 + RET_DK], tiles(job_ps[s][:, 0:512], 4)[:, :, r0:r0 + RET_DK],
                                        cst("w_prompt", h), None, ALU.mult)
                        ins = v.tensor_scalar(KW[0:DEC, 4, r0:r0 + RET_DK], job_ps[s][0:DEC, 512 + r0:512 + r0 + RET_DK],
                                              cst("w_sample", h, 1, 0, DEC), None, ALU.mult)
                    free(ins)
                    if p:
                        wait_stores()
                    for j in range(2):
                        h, r0, r1 = 2 * p + j, j * RET_DK, (j + 1) * RET_DK
                        copy_job(TMP[:, 0])
                        s = job()
                        v.tensor_copy(V[:, 0, 0:4, :], tiles(job_ps[s][:, 0:512], 4))
                        free(v.tensor_copy(V[0:DEC, 0, 4, :], job_ps[s][0:DEC, 512:512 + P]))
                        s = job()
                        for t in range(4):
                            v.tensor_tensor(prob_sb[:, t * P:(t + 1) * P], job_ps[s][:, t * P:(t + 1) * P],
                                            cst("decay", h * P, P), ALU.mult)
                        free(v.tensor_tensor(prob_sb[0:DEC, 512:512 + DEC], job_ps[s][0:DEC, 512:512 + DEC],
                                             cst("decay", h * P, DEC, 0, DEC), ALU.mult))
                        s = job()
                        gp, gs = cst("g_prompt", p, 1, r0, r1), cst("g_sample", p, 1, r0, r1)
                        v.tensor_copy(ST[r0:r1, 4, :], probT[r0:r1, p * P:(p + 1) * P])
                        v.tensor_copy(ST[r0:r1, 0, :], job_ps[s][r0:r1, 0:P])
                        for t in range(1, 4):
                            dve.drain()
                            v.scalar_tensor_tensor(out=ST[r0:r1, t, :], in0=ST[r0:r1, t - 1, :], scalar=gp,
                                                   in1=job_ps[s][r0:r1, t * P:(t + 1) * P], op0=ALU.mult, op1=ALU.add)
                        free(v.scalar_tensor_tensor(out=ST[r0:r1, 5, :], in0=ST[r0:r1, 4, :], scalar=gs,
                                                    in1=job_ps[s][r0:r1, 512:512 + P], op0=ALU.mult, op1=ALU.add))
                        is_ready(v.tensor_copy(small[:, 12:13], small[:, 13:14]))
                        s = job()
                        v.tensor_copy(TMP[:, 0, 0:SEQ], job_ps[s][:, 0:SEQ])
                        free(v.tensor_copy(TMP[:, 0, SEQ:NT], job_ps[s][:, 512:512 + DEC]))
                        dve.drain()
                        s = job()
                        free(v.scalar_tensor_tensor(out=halves(TMP[:, 1]), in0=job_halves(s), scalar=-1.0 / RET_DV,
                                                    in1=halves(TMP[:, 0]), op0=ALU.mult, op1=ALU.add))
                        dve.drain()
                        is_ready(v.tensor_tensor(TMP[:, 0], TMP[:, 1], TMP[:, 1], ALU.mult))
                        inv_root(1.0 / RET_DV)
                        v.scalar_tensor_tensor(out=TMP[:, 1], in0=TMP[:, 1], scalar=g_col("ret_gn", h),
                                               in1=rstd[:, :], op0=ALU.mult, op1=ALU.mult)
                        dve.drain()
                        s = job()
                        n["gate"] += 1
                        dve.wait_ge(gate_done, l * GATES + n["gate"])
                        free(v.tensor_tensor(halves(TMP[:, 0]), job_halves(s), halves(TMP[:, 0]), ALU.mult))
                        dve.drain()
                        v.tensor_tensor(TMP[:, 1], TMP[:, 1], TMP[:, 0], ALU.mult)
                        dve.drain()
                        split(TMP[:, 1], O_HL[0][:, h], O_HL[1][:, h])
                        dve.drain()
                    store()
                    store()
                is_ready(v.tensor_copy(small[:, 12:13], small[:, 13:14]))
                dve.drain()
                wait_stores()
                dve.sem_inc(phase_done, 1)
                branch(False)

                def prep_band(p):
                    b = p % 2
                    copy_job(Q[:, b])
                    wait_stores()
                    copy_job(K[:, b, 0:NT])
                    copy_job(vT[:, 0:NT])
                    s = job()
                    v.tensor_copy(V[:, b, 0:4, :], tiles(job_ps[s][:, 0:512], 4))
                    free(v.tensor_copy(V[0:DEC, b, 6, :], job_ps[s][0:DEC, 1024 - 256:1024 - 128]))
                    store()
                    store()

                heads = [dict(tiles=Q_TILES, scale=None, bias=h, o=(h // 2, h % 2 * 64, h % 2 * 64 + 64))
                         for h in range(BAND_HEADS)]
                for p in range(BAND_HEADS // 2 - 1):
                    heads[2 * p + 1]["prep"] = p + 1
                attend(heads, prep_band)
                dve.drain()
                wait_stores()
                dve.sem_inc(phase_done, 1)
                branch(False)
                dve.drain()
                for k in range(0, KT, 2):
                    is_ready(split(M[:, k:k + 2], U_HL[0][:, k:k + 2], U_HL[1][:, k:k + 2]))
                for k in range(KT):
                    copy_job(M[:, k])
                post_norm("post_mix")

                dve.drain()
                dve.sem_inc(phase_done, 1)
                dve.wait_ge(mem_loaded, (l + 1) * 16)
                dve.sem_inc(settled[1], 1)
                squares_may_start()
                inv_root(1.0 / D, MEM)
                norm_split(lambda k: M[:, k, 0:MEM], "mem", KT, MEM_HL, MEM, each=False)
                squares_may_start()
                inv_root(1.0 / D)
                norm_split(lambda k: X[:, k], "pre_mem", KT, U_HL)

                def prep_mem(h):
                    b = h % 2
                    wait_stores()
                    s = job()
                    free(v.tensor_copy(K[:, b, 0:MEM], job_ps[s][:, 0:MEM]))
                    s = job()
                    free(v.tensor_copy(vT[:, 0:MEM], job_ps[s][:, 0:MEM]))
                    s = job()
                    free(v.tensor_copy(V[:, b, 0:2, :], tiles(job_ps[s][:, 0:256], 2)))
                    store()
                    store()
                    copy_job(Q[:, b])

                heads = [dict(tiles=MEM_TILES, scale=MEM_HD ** -0.5, bias=None, o=(h, 0, P)) for h in range(MEM_HEADS)]
                for h in range(MEM_HEADS - 1):
                    heads[h]["prep"] = h + 1
                attend(heads, prep_mem)
                wait_stores()
                for k in range(KT):
                    copy_job(M[:, k])
                post_norm("post_mem")

                squares_may_start()
                inv_root(1.0 / D)
                norm_split(lambda k: X[:, k], "pre_ff", KT, U_HL)
                v.memset(m_sb[:, :], 0.0)
                dve.drain()
                with dve.Fori(0, FF_CHUNKS) as c:
                    at["job"] = c * (2 * KT)
                    for e in range(KT):
                        s = job()
                        v.tensor_scalar(halves(TMP[:, e % 2]), job_halves(s), 0.0, None, ALU.max)
                        dve.drain()
                        v.tensor_tensor(TMP[:, e % 2], TMP[:, e % 2], TMP[:, e % 2], ALU.mult)
                        dve.drain()
                        free(split(TMP[:, e % 2], H_HL[0][:, e], H_HL[1][:, e]))
                    for e in range(KT):
                        s = job()
                        free(v.tensor_tensor(halves(M[:, e]), job_halves(s), halves(M[:, e]), ALU.add))
                    dve.drain()
                at["job"] = 0
                for k in ("job", "freed"):
                    n[k] += (FF_CHUNKS - 1) * 2 * KT
                post_norm("post_ff")
                if n["job"] % 2:
                    s = job()
                    free(v.tensor_copy(small[:, 14:15], job_ps[s][:, 0:1]))
                dve.drain()
                dve.sem_inc(phase_done, 1)
                counted(**n)

        @block.sync
        def _(sp):
            sp.dma_start(const[:, :], const_in).then_inc(c_loaded, 16)
            sp.dma_start(x_sb[:, :], x_in).then_inc(x_loaded, 16)

            def row(t, l, *more):
                ap = t[bass.ds(l, 1)]
                return ap

            with sp.Fori(0, DEPTH) as l:
                n = dict(store=0)

                def store(dst, src):
                    n["store"] += 1
                    sp.wait_ge(store_asked, l * STORES + n["store"])
                    sp.dma_start(dst, src).then_inc(stored, 16)

                sp.wait_ge(phase_done, l * DVE_PHASES + 1)
                sp.dma_start(gain[:, :], gain_in[bass.ds(l, 1)].rearrange("a p n -> p (a n)")).then_inc(layer_loaded, 16)
                sp.dma_start(cs_sb[:, :], rope_in[0]).then_inc(layer_loaded, 16)
                sp.dma_start(CKV[:, :, NT:KEYS], ckv_in[bass.ds(l, 1)].rearrange("a p k n -> p (a k) n"))\
                    .then_inc(layer_loaded, 16)
                for b in range(2):
                    sp.dma_start(K[NOPE:QK, b, NT:KEYS], kpe_in[bass.ds(l, 1)].rearrange("a p n -> p (a n)"))\
                        .then_inc(layer_loaded, 16)
                store(ckv_out[bass.ds(l, 1)].rearrange("a p k n -> p (a k) n"), CKV[:, :, 0:NT])
                store(kpe_out[bass.ds(l, 1)].rearrange("a p n -> p (a n)"), K[NOPE:QK, 0, 0:NT])
                sp.wait_ge(phase_done, l * DVE_PHASES + 2)
                sp.dma_start(cs_sb[:, :], rope_in[1]).then_inc(r_loaded, 16)
                sp.dma_start(probT[:, 0:2 * P], state_in[bass.ds(l, 1)].rearrange("a p h n -> p (a h n)"))\
                    .then_inc(r_loaded, 16)
                for p in range(2):
                    store(retp_out[bass.ds(l, 1), :, p].rearrange("a p n -> p (a n)"), ST[:, 3, :])
                    store(rets_out[bass.ds(l, 1), :, p].rearrange("a p n -> p (a n)"), ST[:, 5, :])
                sp.wait_ge(phase_done, l * DVE_PHASES + 3)

                def load_bias(h):
                    sp.dma_start(BIAS[:, h % 2], bias_in[bass.ds(l, 1), h].rearrange("a p n -> p (a n)"))\
                        .then_inc(b_loaded[h % 2], 16)

                def load_band(p):
                    sp.dma_start(K[:, p % 2, NT:KEYS], bandk_in[bass.ds(l, 1), p].rearrange("a p n -> p (a n)"))\
                        .then_inc(kv_loaded[p % 2], 16)
                    sp.dma_start(V[:, p % 2, 4:6, :], bandv_in[bass.ds(l, 1), p].rearrange("a p t n -> p (a t) n"))\
                        .then_inc(kv_loaded[p % 2], 16)

                for i in range(2):
                    load_bias(i)
                    load_band(i)
                for p in range(BAND_HEADS // 2):
                    store(bandk_out[bass.ds(l, 1), p].rearrange("a p n -> p (a n)"), K[:, p % 2, 0:NT])
                    store(bandv_out[bass.ds(l, 1), p].rearrange("a p n -> p (a n)"), vT[:, 0:NT])
                    for h in (2 * p, 2 * p + 1):
                        if h + 2 < BAND_HEADS:
                            sp.wait_ge(out_free, l * ITEMS + I_BAND + (h + 1) * NQ + 1)
                            load_bias(h + 2)
                    if p + 2 < BAND_HEADS // 2:
                        load_band(p + 2)

                def load_mem(h):
                    sp.dma_start(K[:, h % 2, MEM:2 * MEM], memk_in[bass.ds(l, 1), h].rearrange("a p n -> p (a n)"))\
                        .then_inc(kv_loaded[h % 2], 16)
                    sp.dma_start(V[:, h % 2, 2:4, :], memv_in[bass.ds(l, 1), h].rearrange("a p t n -> p (a t) n"))\
                        .then_inc(kv_loaded[h % 2], 16)

                sp.wait_ge(phase_done, l * DVE_PHASES + 4)
                for i in range(2):
                    load_mem(i)
                sp.wait_ge(phase_done, l * DVE_PHASES + 5)
                sp.dma_start(M[:, :, 0:MEM], mem_in).then_inc(mem_loaded, 16)
                for h in range(MEM_HEADS):
                    store(memk_out[bass.ds(l, 1), h].rearrange("a p n -> p (a n)"), K[:, h % 2, 0:MEM])
                    store(memv_out[bass.ds(l, 1), h].rearrange("a p n -> p (a n)"), vT[:, 0:MEM])
                    if h + 2 < MEM_HEADS:
                        sp.wait_ge(out_free, l * ITEMS + I_MEM + (h + 1) * NQ + 1)
                        load_mem(h + 2)
            sp.wait_ge(phase_done, DEPTH * DVE_PHASES + 1)
            sp.dma_start(y_out, x_sb[:, :]).then_inc(stored, 16)
            sp.wait_ge(stored, (DEPTH * STORES + 1) * 16)


SQUARES = 7 * KT + QR + CR
SQ_USES = 7 * (KT - 2) + QR - 2
ROOTS = 9 + RET_HEADS
LAYER_LOADS = 5
RET_LOADS = 2
DVE_PHASES = 5


def counted(**n):
    want = dict(job=JOBS, unit=UNITS, freed=DVE_FREED, gate=GATES, ready=READY, ask=REQS, item=ITEMS, done=ROOTS,
                store=STORES)
    assert all(want.get(k, v) == v for k, v in n.items()), n


def constants():
    c = np.zeros((P, NCONST), np.float32)

    def put(name, a):
        c[:a.shape[0], CONST[name]:CONST[name] + a.shape[1]] = a

    put("ident", np.eye(P))
    put("ones", np.ones((P, P)))
    for name, half, r0, r1 in (("rot_ret", RET_DK // 2, 0, P), ("rot_pe", ROPE // 2, NOPE, QK)):
        m = np.zeros((P, P))
        for i in range(r0, r1):
            j = (i - r0) % (2 * half)
            if j < half:
                m[i + half, i] = -1
            else:
                m[i - half, i] = 1
        put(name, m)
    first = np.zeros((1, P))
    first[0, :CHUNK] = 1
    put("first", first)
    neg = np.zeros((1, P))
    neg[0, CHUNK:] = NEG
    put("neg", neg)
    g = np.log1p(-np.exp2(-5.0 - np.arange(RET_HEADS)))
    t = np.arange(P)
    cross = np.zeros((P, 2 * P))
    gp, gs = np.zeros((P, 2)), np.zeros((P, 2))
    for p in range(2):
        for j in range(2):
            r = slice(j * RET_DK, (j + 1) * RET_DK)
            cross[r, p * P:(p + 1) * P] = np.exp(g[2 * p + j] * (t + 1.0))
            gp[r, p] = np.exp(g[2 * p + j] * P)
            gs[r, p] = np.exp(g[2 * p + j] * DEC)
    put("cross", cross)
    put("g_prompt", gp)
    put("g_sample", gs)
    diff = t[None, :] - t[:, None]
    put("decay", np.concatenate([np.where(diff >= 0, np.exp(x * np.maximum(diff, 0)), 0) for x in g], 1))
    put("w_prompt", np.stack([np.exp(x * (P - 1.0 - t)) for x in g], 1))
    put("w_sample", np.stack([np.exp(x * (DEC - 1.0 - t[:DEC])) for x in g], 1))
    pos = np.concatenate([np.arange(SEQ), PAST + np.arange(DEC)]).astype(np.float32)
    rope = np.zeros((2, P, 2 * NT), np.float32)
    for i, (half, r0, r1) in enumerate(((ROPE // 2, NOPE, QK), (RET_DK // 2, 0, P))):
        inv = np.float32(10000.0) ** (-np.arange(half, dtype=np.float32) / np.float32(half))
        ang = (inv[:, None] * pos[None, :]).astype(np.float32)
        rows = (np.arange(r0, r1) - r0) % half
        rope[i, r0:r1, :NT] = np.cos(ang)[rows]
        rope[i, r0:r1, NT:] = np.sin(ang)[rows]
    return c, rope


def kernel(**inputs):
    import concourse.bacc as bacc
    from concourse.bass_utils import run_bass_kernel_spmd

    a = {k: np.asarray(v) for k, v in inputs.items()}

    def fm(x):
        return x.T.reshape(-1, P, x.shape[0]).transpose(1, 0, 2)

    def w_tile(w, width=P):
        return w.reshape(-1, P, w.shape[1]).transpose(1, 0, 2).reshape(P, -1)

    units = []

    def add(*parts):
        u = np.concatenate(parts, 1)
        units.append(np.pad(u, ((0, 0), (0, D - u.shape[1]))))

    sizes = (384, 256, 32, 256, 256, 512, 512, 512, 512, 512, 3072)
    off = np.concatenate([[0], np.cumsum(sizes)])
    zq, zkv, zpe, rq, rk, rv, rg, cq, ck, cv, zg = off[:11]
    for l in range(DEPTH):
        w = a["w_in"][l]
        cols = lambda c: w_tile(w[:, c:c + P])

        def branch(b, wb):
            for e in range(0, KT, 2):
                add(cols(zg + b * D + e * P))
                add(cols(zg + b * D + (e + 1) * P))
                add(w_tile(wb[:, e * P:(e + 1) * P]), w_tile(wb[:, (e + 1) * P:(e + 2) * P]))

        for i in range(QR):
            add(cols(zq + i * P))
        for i in range(CR):
            add(cols(zkv + i * P))
        add(cols(zpe - NOPE))
        for h in range(MLA_HEADS):
            add(w_tile(a["w_mla_uq"][l][:, h]), w_tile(a["w_mla_ukv"][l][:, h]))
        branch(0, a["w_br_a"][l])
        for p in range(2):
            add(cols(rq + p * P))
            add(cols(rk + p * P))
            for h in (2 * p, 2 * p + 1):
                add(cols(rv + h * P))
                add(cols(rg + h * P))
        branch(1, a["w_br_b"][l])
        for p in range(4):
            for c in (cq, ck, cv):
                add(cols(c + p * P))
        branch(2, a["w_br_c"][l])
        for e in range(KT):
            add(w_tile(a["w_out"][l][:, e * P:(e + 1) * P]))
        for h in range(MEM_HEADS):
            for name in ("w_mem_k", "w_mem_v", "w_mem_q"):
                add(w_tile(a[name][l][:, h]))
        wo = a["w_mem_o"][l].reshape(MEM_HEADS * MEM_HD, D)
        for e in range(0, KT, 2):
            add(w_tile(wo[:, e * P:(e + 1) * P]), w_tile(wo[:, (e + 1) * P:(e + 2) * P]))
        for c in range(FF_CHUNKS):
            for e in range(KT):
                add(w_tile(a["w_up"][l][:, c * D + e * P:c * D + (e + 1) * P]))
            for e in range(KT):
                add(w_tile(a["w_down"][l][c * D:(c + 1) * D, e * P:(e + 1) * P]))
        for _ in range(SPARE):
            units.append(np.zeros((P, D), np.float32))
        assert len(units) == (l + 1) * UNITS
    for _ in range(LEAD):
        units.append(np.zeros((P, D), np.float32))

    def col(x):
        return x.reshape(DEPTH, -1, P).transpose(0, 2, 1)

    gains = np.concatenate([col(a[k]) for k in ("g_pre_mix", "g_post_mix", "g_pre_mem", "g_mem", "g_post_mem",
                                                "g_pre_ff", "g_post_ff", "g_mla_q", "g_mla_kv", "g_ret_gn",
                                                "b_gate")], 2)
    consts, rope = constants()
    rel = np.arange(P)[:, None] + (SEQ - P) - np.arange(SEQ)[None, :]
    bias = a["band_rel_bias"][:, :, np.clip(rel, -128, 128) + 128].astype(np.float32)
    bias[:, :, :CHUNK, SEQ - CHUNK:] = NEG

    def keyT(x, g):
        return x.reshape(DEPTH, x.shape[2], g, P).transpose(0, 2, 3, 1)

    def val(x, g):
        return x.reshape(DEPTH, 2, P, g, P).transpose(0, 3, 2, 1, 4)

    ins = dict(
        x=fm(np.concatenate([a["x_prompt"][0], a["x_sample"][0]])).reshape(P, -1),
        mem=fm(a["mem_prompt"][0]), w=np.stack(units),
        ckv=np.stack([fm(a["cache_mla_ckv"][l, 0]) for l in range(DEPTH)]),
        kpe=a["cache_mla_kpe"][:, 0].transpose(0, 2, 1),
        state=a["state_ret"][:, 0].reshape(DEPTH, 2, P, RET_DV).transpose(0, 2, 1, 3),
        bandk=keyT(a["cache_band_k"], 4), bandv=val(a["cache_band_v"], 4),
        memk=keyT(a["cache_mem_k"], 4), memv=val(a["cache_mem_v"], 4),
        bias=bias, gain=gains, const=consts, rope=rope)
    outs = dict(
        y=(P, KT * NT), o_ckv=(DEPTH, P, CR, NT), o_kpe=(DEPTH, ROPE, NT), o_retp=(DEPTH, P, 2, RET_DV),
        o_rets=(DEPTH, P, 2, RET_DV), o_bandk=(DEPTH, 4, P, NT), o_bandv=(DEPTH, 4, P, NT),
        o_memk=(DEPTH, 4, P, MEM), o_memv=(DEPTH, 4, P, MEM))
    nc = bacc.Bacc("TRN2", target_bir_lowering=False, num_devices=1)
    arrays = {k: np.ascontiguousarray(v) for k, v in ins.items()}
    args = [nc.dram_tensor("in_" + k, v.shape, F32, kind="ExternalInput").ap() for k, v in arrays.items()]
    args += [nc.dram_tensor("out_" + k, s, F32, kind="ExternalOutput").ap() for k, s in outs.items()]
    build(nc, *args)
    r = run_bass_kernel_spmd(nc, [{"in_" + k: v for k, v in arrays.items()}], core_ids=[0]).results[0]
    r = {k: r["out_" + k] for k in outs}

    y = np.asarray(r["y"]).reshape(P, KT, NT).transpose(2, 1, 0).reshape(NT, D)
    ckv = np.asarray(r["o_ckv"]).transpose(0, 3, 2, 1).reshape(DEPTH, NT, CR * P)
    kpe = np.asarray(r["o_kpe"]).transpose(0, 2, 1)
    ret = [np.asarray(r[k]).transpose(0, 2, 1, 3).reshape(DEPTH, 1, RET_HEADS, RET_DK, RET_DV)
           for k in ("o_retp", "o_rets")]
    bk, bv = (np.asarray(r[k]).transpose(0, 3, 1, 2).reshape(DEPTH, NT, BAND_HEADS, BAND_HD)
              for k in ("o_bandk", "o_bandv"))
    mk, mv = (np.asarray(r[k]).transpose(0, 3, 1, 2).reshape(DEPTH, 1, MEM, MEM_HEADS, MEM_HD)
              for k in ("o_memk", "o_memv"))
    cut = lambda t: (np.ascontiguousarray(t[:, None, :SEQ]), np.ascontiguousarray(t[:, None, SEQ:]))
    (pc, sc), (pk, sk), (pbk, sbk), (pbv, sbv) = cut(ckv), cut(kpe), cut(bk), cut(bv)
    return (np.ascontiguousarray(y[None, :SEQ]), np.ascontiguousarray(y[None, SEQ:]), pc, pk, ret[0], pbk, pbv,
            mk, mv, sc, sk, ret[1], sbk, sbv)
```

```python
from contextlib import ExitStack

import numpy as np

import concourse.bass as bass
from concourse import mybir

F32 = mybir.dt.float32
F32R = mybir.dt.float32r
ALU = mybir.AluOpType
ACT = mybir.ActivationFunctionType
AX_X = mybir.AxisListType.X

P = 128
DEPTH = 2
D = 1024
SEQ, DEC, PAST, MEM = 512, 64, 256, 256
NT = SEQ + DEC
HALF = NT // 2
KEYS = NT + PAST
KT = D // P
MLA_HEADS, NOPE, ROPE, MLA_V = 8, 64, 32, 64
QK = NOPE + ROPE
QR, CR = 384 // P, 256 // P
RET_HEADS, RET_DK, RET_DV = 4, 64, 128
BAND_HEADS, BAND_HD = 8, 64
MEM_HEADS, MEM_HD = 4, 128
FF = 4 * D
FF_CHUNKS = FF // D
OT = 512 // P
CHUNK = 64
EPS = 1e-6
NEG = -1e30

U_MLA_IN = QR + CR + 1
U_BRANCH = KT + KT // 2
U_RET = 2 * (2 + 2 * 2)
U_BAND = 4 * 3
U_MEM = MEM_HEADS * 3
U_FF = 2 * FF // P
_UNITS = U_MLA_IN + MLA_HEADS + 3 * U_BRANCH + U_RET + U_BAND + KT + U_MEM + KT // 2 + U_FF
UNITS = (_UNITS + 3) // 4 * 4
SPARE = UNITS - _UNITS
RING, RAW = 4, 2
LEAD = RING

GAINS = {}
_c = 0
for _n, _w in (("pre_mix", KT), ("post_mix", KT), ("pre_mem", KT), ("mem", KT), ("post_mem", KT),
               ("pre_ff", KT), ("post_ff", KT), ("mla_q", QR), ("mla_kv", CR), ("ret_gn", RET_HEADS),
               ("b_gate", 3 * KT)):
    GAINS[_n] = _c
    _c += _w
NGAIN = _c

CONST = {}
_c = 0
for _n, _w in (("ident", P), ("ones", P), ("rot_ret", P), ("rot_pe", P), ("first", P), ("neg", P),
               ("cross", 2 * P), ("decay", RET_HEADS * P), ("w_prompt", RET_HEADS), ("w_sample", RET_HEADS),
               ("g_prompt", 2), ("g_sample", 2)):
    CONST[_n] = _c
    _c += _w
NCONST = _c

Q_TILES = [(i * P, (0, (i + 1) * P), [(j * P, P, j) for j in range(i + 1)]) for i in range(SEQ // P)]
Q_TILES.append((NT - P, (SEQ, DEC + PAST), [(DEC, P, 4), (DEC + P, P, 5), (0, DEC, 6)]))
MEM_TILES = [(i * P, (0, MEM), [(0, P, 0), (P, P, 1)]) for i in range(SEQ // P)]
MEM_TILES.append((NT - P, (MEM, MEM), [(0, P, 2), (P, P, 3)]))
NQ = len(Q_TILES)
V_TOKENS = [(i * P, P, i) for i in range(SEQ // P)]
ITEMS = (MLA_HEADS + BAND_HEADS + MEM_HEADS) * NQ
I_BAND = MLA_HEADS * NQ
I_MEM = I_BAND + BAND_HEADS * NQ



def out_tokens(tiles, i):
    t0 = tiles[i][0]
    return (t0, t0 + P, 0) if i < NQ - 1 else (SEQ, NT, P - DEC)


def plan(groups, per_group, offsets):
    at = {-1: [(0, step) for step in range(len(offsets))]}
    for g in range(1, groups):
        for step, off in enumerate(offsets):
            assert off < per_group - 2
            at.setdefault((g - 1) * per_group + off, []).append((g, step))
    return at


PLAN_MLA = plan(MLA_HEADS, NQ, (-1, 0, 1, 2))
PLAN_BAND = plan(BAND_HEADS // 2, 2 * NQ, (1, 3, 5, 7))
PLAN_MEM = plan(MEM_HEADS, NQ, (-1, 0, 1, 2))

HALVES = [(0, HALF, 0), (512, HALF, HALF)]

JOBS = 258
DVE_FREED = JOBS - 3 * KT
GATES = 3 * KT + RET_HEADS
REQS = 25
READY = 27
STORES = 2 + 2 * 2 + 2 * (BAND_HEADS // 2) + 2 * MEM_HEADS
PHASES = 4


def build(nc, x_in, mem_in, w_in, ckv_in, kpe_in, state_in, bandk_in, bandv_in, memk_in, memv_in,
          bias_in, gain_in, const_in, rope_in, y_out, ckv_out, kpe_out, retp_out, rets_out,
          bandk_out, bandv_out, memk_out, memv_out):
    with ExitStack() as ctx:
        def sb(name, cols, dt=F32):
            return ctx.enter_context(nc.sbuf_tensor(name, [P, cols], dt))

        def bank(name, n):
            return ctx.enter_context(nc.psum_tensor(name, [P, 512 * n], F32))

        def sem(name):
            return ctx.enter_context(nc.semaphore(name))

        def tiles(ap, k):
            return ap.rearrange("p (k n) -> p k n", k=k)

        x_sb = sb("x", KT * NT)
        m_sb = sb("m", KT * NT)
        tmp_sb = sb("tmp", 2 * NT)
        rstd = sb("rstd", NT)
        q_sb = sb("q", 2 * NT)
        k_sb = sb("k", 2 * KEYS)
        v_sb = sb("v", 2 * 7 * P)
        prob_sb = sb("prob", 2 * 512)
        probT = sb("probT", 512)
        bias_sb = sb("bias", 2 * 512)
        cs_sb = sb("cs", 2 * NT)
        const = sb("const", NCONST)
        gain = sb("gain", NGAIN)
        small = sb("small", 16)
        raw = sb("raw", RAW * D)
        w_hi = sb("w_hi", RING * D, F32R)
        w_lo = sb("w_lo", RING * D, F32R)
        arena = sb("arena", 3 * KT * NT + 2 * QR * NT + 2 * CR * KEYS, F32R)

        X, M = tiles(x_sb[:, :], KT), tiles(m_sb[:, :], KT)
        TMP, Q, K = tiles(tmp_sb[:, :], 2), tiles(q_sb[:, :], 2), tiles(k_sb[:, :], 2)
        V = v_sb[:, :].rearrange("p (s t n) -> p s t n", s=2, t=7)
        PROB, BIAS = tiles(prob_sb[:, :], 2), tiles(bias_sb[:, :], 2)
        COS, SIN = cs_sb[:, 0:NT], cs_sb[:, NT:2 * NT]
        SQ = Q
        vT = tmp_sb[:, 0:KEYS]
        RAWS = tiles(raw[:, :], RAW)
        WHI, WLO = tiles(w_hi[:, :], RING), tiles(w_lo[:, :], RING)
        ZQ = tiles(m_sb[:, 0:QR * NT], QR)
        CKV = tiles(m_sb[:, QR * NT:QR * NT + CR * KEYS], CR)
        ST = tiles(k_sb[:, KEYS:KEYS + 6 * P], 6)
        KW = V[:, 1]
        QX = Q[:, 1]

        U0, O0, Z0 = 0, 2 * KT * NT, 3 * KT * NT

        def region(start, k, n):
            return tiles(arena[:, start:start + k * n], k)

        U_HL = region(U0, KT, NT), region(U0 + KT * NT, KT, NT)
        O_HL = region(O0, OT, NT), region(O0 + OT * NT, OT, NT)
        ZQ_HL = region(Z0 - 0, QR, NT), region(Z0 + QR * NT, QR, NT)
        CKV_HL = region(Z0 + 2 * QR * NT, CR, KEYS), region(Z0 + 2 * QR * NT + CR * KEYS, CR, KEYS)
        H_HL = region(O0, KT, NT), region(Z0, KT, NT)
        MEM_HL = region(Z0, KT, MEM), region(Z0 + KT * MEM, KT, MEM)

        job_ps = [bank(f"job{i}", 2) for i in range(2)]
        score_ps = [bank(f"score{i}", 1) for i in range(2)]
        turn_ps = bank("turn", 1)
        out_ps = bank("outp", 1)

        def halves(ap):
            return ap.rearrange("p (b n) -> p b n", b=2)

        def job_halves(s, p0=0, p1=P):
            return halves(job_ps[s][p0:p1, :])[:, :, 0:HALF]

        def cst(name, i=0, w=1, p0=0, p1=P):
            return const[p0:p1, CONST[name] + i:CONST[name] + i + w]

        def g_col(name, i):
            return gain[:, GAINS[name] + i:GAINS[name] + i + 1]

        IDENT = cst("ident", 0, P)
        ONES = cst("ones", 0, P)

        raw_loaded = [sem(f"raw_loaded{i}") for i in range(RAW)]
        hi_done, lo_done = sem("hi_done"), sem("lo_done")
        job_done, job_free, gate_done = sem("job_done"), sem("job_free"), sem("gate_done")
        sq_ready, sq_used = sem("sq_ready"), sem("sq_used")
        act_asked, act_done = sem("act_asked"), sem("act_done")
        ready = sem("ready")
        out_rounded = sem("out_rounded")
        score_done, negmax, exp_done, probs = sem("score_done"), sem("negmax"), sem("exp_done"), sem("probs")
        turn_done, turned, out_done, out_free = sem("turn_done"), sem("turned"), sem("out_done"), sem("out_free")
        x_loaded, c_loaded = sem("x_loaded"), sem("c_loaded")
        layer_loaded, r_loaded = sem("layer_loaded"), sem("r_loaded")
        kv_loaded = [sem(f"kv_loaded{i}") for i in range(2)]
        b_loaded = [sem(f"b_loaded{i}") for i in range(2)]
        mem_loaded = sem("mem_loaded")
        store_asked, stored = sem("store_asked"), sem("stored")
        phase_done = sem("phase_done")

        settled = [sem(f"settled_{e}") for e in ("pe", "dve")]

        block = ctx.enter_context(nc.Block())

        @block.tensor
        def _(pe):
            pe.sem_inc(job_done, 1)
            pe.sem_inc(sq_used, 1)
            pe.sem_inc(out_done, 1)
            pe.wait_ge(c_loaded, 16)
            with pe.Fori(0, DEPTH) as l:
                n = dict(job=0, unit=0, freed=0, gate=0, sq=0, squ=0, ready=0, item=0)
                at = dict(job=0, unit=0)
                owner = [("job_free", -2), ("job_free", -1)]

                def slot(freed_by="dve"):
                    s = n["job"] % 2
                    who, i = owner[s]
                    if who == "job_free":
                        pe.wait_ge(job_free, l * DVE_FREED + at["job"] + i + 3)
                    else:
                        pe.wait_ge(gate_done, l * GATES + i + 1)
                    if freed_by == "dve":
                        owner[s] = ("job_free", n["freed"])
                        n["freed"] += 1
                    else:
                        owner[s] = ("gate", n["gate"])
                        n["gate"] += 1
                    n["job"] += 1
                    return job_ps[s]

                def evicted():
                    pe.wait_ge(job_free, l * DVE_FREED + at["job"] + n["freed"] + 2)

                def settle():
                    pe.sem_inc(settled[0], 1)

                def wait_ready():
                    n["ready"] += 1
                    pe.wait_ge(ready, l * READY + n["ready"])

                def unit():
                    pe.wait_ge(lo_done, l * UNITS + at["unit"] + n["unit"] + 3)
                    s = n["unit"] % RING
                    n["unit"] += 1
                    return s

                def project(s, kt, hl, at_col=0, step=P, m=P, pieces=HALVES, each_ready=False, freed_by="dve",
                            k0=0):
                    ps = slot(freed_by)
                    for k in range(kt):
                        if each_ready and k % 2 == 0:
                            wait_ready()
                        c = at_col + k * step
                        for w, x in ((WHI, hl[0]), (WHI, hl[1]), (WLO, hl[0])):
                            for po, nn, so in pieces:
                                mm = pe.matmul(ps[0:m, po:po + nn], w[:, s, c:c + m], x[:, k, so:so + nn],
                                               start=(k == 0 and w is WHI and x is hl[0]),
                                               stop=(k == kt - 1 and w is WLO))
                    mm.then_inc(job_done, 1)

                def plain(lhsT, rhs, m=P, pieces=HALVES):
                    ps = slot()
                    for po, nn, so in pieces:
                        mm = pe.matmul(ps[0:m, po:po + nn], lhsT, rhs[:, so:so + nn], start=True, stop=True)
                    mm.then_inc(job_done, 1)

                def stat(kt, pieces=HALVES):
                    ps = slot()
                    for k in range(kt):
                        n["sq"] += 1
                        pe.wait_ge(sq_ready, l * SQUARES + n["sq"])
                        for po, nn, so in pieces:
                            mm = pe.matmul(ps[:, po:po + nn], ONES, SQ[:, k % 2, so:so + nn],
                                           start=(k == 0), stop=(k == kt - 1))
                        if k < kt - 2:
                            mm.then_inc(sq_used, 1)
                    mm.then_inc(job_done, 1)

                def turn_values(toks):
                    evicted()
                    ps = slot()
                    for c, w, t in toks:
                        o = (t // 4) * 512 + (t % 4) * P
                        mm = pe.transpose(ps[0:w, o:o + P], vT[:, c:c + w], IDENT)
                    mm.then_inc(job_done, 1)

                def scores(i, head):
                    t0, (c, w), _ = head["tiles"][i]
                    r0, r1 = head["rows"]
                    it = n["item"]
                    s = it % 2
                    pe.wait_ge(probs, l * ITEMS + it + 1)
                    chunked = head["mask"] and i < NQ - 1
                    mm = pe.matmul(score_ps[s][:, 0:w], Q[r0:r1, head["q"], t0:t0 + P], K[r0:r1, head["k"], c:c + w],
                                   start=True, stop=not chunked)
                    if chunked:
                        mm = pe.matmul(score_ps[s][:, w - P:w], cst("first", 0, P, 0, 1), cst("neg", 0, P, 0, 1),
                                       start=False, stop=True)
                    mm.then_inc(score_done, 1)
                    n["item"] += 1

                def turn(it, i, head):
                    pe.wait_ge(probs, l * ITEMS + it + 3)
                    pe.wait_ge(turned, l * ITEMS + it + 1)
                    for j, (c, w, _) in enumerate(head["tiles"][i][2]):
                        mm = pe.transpose(turn_ps[0:w, j * P:(j + 1) * P], PROB[:, it % 2, c:c + w], IDENT)
                    mm.then_inc(turn_done, 1)

                def weigh(it, i, head):
                    kts = head["tiles"][i][2]
                    pe.wait_ge(turned, l * ITEMS + it + 2)
                    pe.wait_ge(out_free, l * ITEMS + it + 1)
                    v0, v1, o0 = head["v"]
                    for j, (c, w, t) in enumerate(kts):
                        mm = pe.matmul(out_ps[o0:o0 + v1 - v0, 0:P], V[0:w, head["vs"], t, v0:v1],
                                       probT[0:w, j * P:(j + 1) * P], start=(j == 0), stop=(j == len(kts) - 1))
                    mm.then_inc(out_done, 1)

                def attend(heads, steps, when):
                    flat = [(h, i) for h in heads for i in range(NQ)]
                    base = n["item"]
                    groups = [steps(g) for g in range(1 + max(g for w in when.values() for g, _ in w))]
                    for g, step in when[-1]:
                        groups[g][step]()
                    evicted()
                    for h, i in flat[:2]:
                        scores(i, h)
                    for j in range(len(flat) + 1):
                        if j:
                            weigh(base + j - 1, flat[j - 1][1], flat[j - 1][0])
                        if j < len(flat):
                            turn(base + j, flat[j][1], flat[j][0])
                        if j + 2 < len(flat):
                            if flat[j + 2][1] == 0:
                                evicted()
                            scores(flat[j + 2][1], flat[j + 2][0])
                        for g, step in when.get(j, ()):
                            groups[g][step]()
                    pe.wait_ge(out_free, l * ITEMS + n["item"] + 1)

                def branch():
                    for e2 in range(KT // 2):
                        for e in range(2):
                            project(unit(), KT, U_HL, freed_by="act")
                        s = unit()
                        for e in range(2):
                            project(s, OT, O_HL, at_col=e * OT * P)

                stat(KT)
                for i in range(QR + CR + 1):
                    project(unit(), KT, U_HL, each_ready=(i == 0))
                stat(QR)
                stat(CR)
                evicted()
                plain(cst("rot_pe", 0, QK, 0, QK), TMP[0:QK, 0], m=QK)
                wait_ready()

                def steps_mla(h):
                    s = []

                    def queries():
                        s.append(unit())
                        project(s[0], QR, ZQ_HL, step=QK, m=QK)

                    def keys_values():
                        project(s[0], CR, CKV_HL, at_col=QR * QK)
                        project(s[0], CR, CKV_HL, at_col=QR * QK, pieces=[(0, PAST, NT)])

                    def rotate():
                        evicted()
                        plain(cst("rot_pe", 0, QK, 0, QK), Q[0:QK, h % 2], m=QK)

                    return [queries, keys_values, rotate,
                            lambda: turn_values(V_TOKENS + [(NT, P, 4), (NT + P, P, 5), (SEQ, DEC, 6)])]

                heads = [dict(q=h % 2, k=h % 2, rows=(0, QK), mask=True, tiles=Q_TILES, vs=h % 2,
                              v=(0, MLA_V, (h % 2) * MLA_V)) for h in range(MLA_HEADS)]
                attend(heads, steps_mla, PLAN_MLA)
                branch()

                for p in range(RET_HEADS // 2):
                    project(unit(), KT, U_HL)
                    project(unit(), KT, U_HL)
                    evicted()
                    plain(cst("rot_ret", 0, P), Q[:, 0])
                    plain(cst("rot_ret", 0, P), K[:, 0])
                    evicted()
                    ps = slot()
                    for c, w, t in V_TOKENS + [(SEQ, DEC, 4)]:
                        mm = pe.transpose(ps[0:w, t * P:(t + 1) * P], K[:, 0, c:c + w], IDENT)
                    mm.then_inc(job_done, 1)
                    for j in range(2):
                        r0, r1 = j * RET_DK, (j + 1) * RET_DK
                        project(unit(), KT, U_HL)
                        turn_values(V_TOKENS + [(SEQ, DEC, 4)])
                        ps = slot()
                        for c, w, t in V_TOKENS + [(SEQ, DEC, 4)]:
                            mm = pe.matmul(ps[0:w, t * P:t * P + w], K[r0:r1, 0, c:c + w], Q[r0:r1, 0, c:c + w],
                                           start=True, stop=True)
                        mm.then_inc(job_done, 1)
                        evicted()
                        ps = slot()
                        for c, w, t in V_TOKENS + [(SEQ, DEC, 4)]:
                            mm = pe.matmul(ps[r0:r1, t * P:(t + 1) * P], KW[0:w, t, r0:r1], V[0:w, 0, t, :],
                                           start=True, stop=True)
                        mm.then_inc(job_done, 1)
                        wait_ready()
                        ps = slot()
                        for c, w, t in V_TOKENS + [(SEQ, DEC, 4)]:
                            cross = t > 0
                            mm = pe.matmul(ps[:, t * P:t * P + w], V[:, 0, t, :], prob_sb[:, t * P:t * P + w],
                                           start=True, stop=not cross)
                            if cross:
                                st = ST[r0:r1, t - 1 if t < 4 else 4, :]
                                mm = pe.matmul(ps[:, t * P:t * P + w], st, QX[r0:r1, c:c + w],
                                               start=False, stop=True)
                        mm.then_inc(job_done, 1)
                        evicted()
                        plain(ONES, TMP[:, 0])
                        wait_ready()
                        plain(ONES, TMP[:, 0])
                        project(unit(), KT, U_HL)
                        n["gate"] += 1
                wait_ready()
                branch()

                def steps_band(p):
                    def values():
                        turn_values(V_TOKENS + [(SEQ, DEC, 6)])
                        pe.wait_ge(kv_loaded[p % 2], (l * 4 + p // 2 + 1) * 32)

                    return [lambda: project(unit(), KT, U_HL)] * 3 + [values]

                heads = [dict(q=h // 2 % 2, k=h // 2 % 2, rows=((h % 2) * 64, (h % 2) * 64 + 64), mask=False,
                              tiles=Q_TILES, vs=h // 2 % 2, v=((h % 2) * 64, (h % 2) * 64 + 64, (h % 2) * 64))
                         for h in range(BAND_HEADS)]
                attend(heads, steps_band, PLAN_BAND)
                branch()

                for e in range(KT):
                    project(unit(), KT, U_HL, each_ready=(e == 0))
                stat(KT)

                stat(KT, [(0, MEM, 0)])
                stat(KT)

                def steps_mem(h):
                    def query():
                        project(unit(), KT, U_HL, each_ready=(h == 0))
                        pe.wait_ge(kv_loaded[h % 2], (l * 4 + 2 + h // 2 + 1) * 32)

                    return [lambda: project(unit(), KT, MEM_HL, pieces=[(0, MEM, 0)])] * 2 + [
                        lambda: turn_values([(0, P, 0), (P, P, 1)]), query]

                heads = [dict(q=h % 2, k=h % 2, rows=(0, P), mask=False, tiles=MEM_TILES, vs=h % 2, v=(0, P, 0))
                         for h in range(MEM_HEADS)]
                wait_ready()
                attend(heads, steps_mem, PLAN_MEM)
                for e2 in range(KT // 2):
                    s = unit()
                    for e in range(2):
                        project(s, OT, O_HL, at_col=e * OT * P)
                stat(KT)

                stat(KT)
                for _ in range(4):
                    wait_ready()
                settle()
                with pe.Fori(0, FF_CHUNKS) as c:
                    at["job"], at["unit"] = c * (2 * KT), c * (2 * KT)
                    for e in range(KT):
                        project(unit(), KT, U_HL)
                    for e in range(KT):
                        if e == 0:
                            evicted()
                        project(unit(), KT, H_HL)
                at["job"] = at["unit"] = 0
                n["unit"] += (FF_CHUNKS - 1) * 2 * KT
                for k in ("job", "freed"):
                    n[k] += (FF_CHUNKS - 1) * 2 * KT
                owner[n["job"] % 2], owner[1 - n["job"] % 2] = [("job_free", n["freed"] - i) for i in (2, 1)]
                stat(KT)
                if n["job"] % 2:
                    plain(cst("ident", 0, P), TMP[:, 0], pieces=[(0, P, 0)])
                for _ in range(SPARE):
                    unit()
                counted(**n)

        @block.gpsimd
        def _(pool):
            pool.sem_inc(lo_done, 2)

            def lo(g, u):
                pool.wait_ge(hi_done, g + 1)
                nc.gpsimd.tensor_tensor(WLO[:, u % RING, :], RAWS[:, u % RAW, :], WHI[:, u % RING, :].bitcast(F32),
                                        ALU.subtract).then_inc(lo_done, 1)

            with pool.Fori(0, DEPTH * UNITS, RING) as g:
                for j in range(RING):
                    lo(g + j, j)
            for j in range(LEAD - 1):
                lo(DEPTH * UNITS + j, j)

        @block.scalar
        def _(act):
            def load(g, u):
                act.dma_start(RAWS[:, u % RAW, :], w_in[bass.ds(g, 1)].rearrange("a p n -> p (a n)"))\
                    .then_inc(raw_loaded[u % RAW], 16)

            def hi(g, turn, u):
                act.wait_ge(raw_loaded[u % RAW], (turn + u // RAW + 1) * 16)
                act.activation(WHI[:, u % RING, :], RAWS[:, u % RAW, :], ACT.Copy).then_inc(hi_done, 1)

            act.sem_inc(turned, 1)
            load(0, 0)
            load(1, 1)
            for u in range(LEAD - 1):
                hi(u, 0, u)
                act.wait_ge(lo_done, u + 3)
                if u < 2:
                    load(u + 2, u + 2)
            act.wait_ge(c_loaded, 16)
            act.wait_ge(x_loaded, 16)
            with act.Fori(0, DEPTH) as l:
                n = dict(job=0, unit=0, gate=0, squ=0, sq=0, ask=0, item=0)
                at = dict(job=0, unit=0)

                def place():
                    u = n["unit"]
                    act.wait_ge(job_done, l * JOBS + at["job"] + n["job"] + 1)
                    hi(None, l * (UNITS // RAW) + at["unit_raw"], u + 3)
                    act.wait_ge(lo_done, l * UNITS + at["unit"] + u + 2 + 1 + 2)
                    load(l * UNITS + at["unit"] + (u + 4), u + 4)
                    n["unit"] += 1

                at["unit_raw"] = 0

                def asked():
                    n["ask"] += 1
                    act.wait_ge(act_asked, l * REQS + n["ask"])

                def squares(src, kt, w=NT):
                    asked()
                    for k in range(kt):
                        if k >= 2:
                            n["squ"] += 1
                            act.wait_ge(sq_used, l * SQ_USES + n["squ"] + 1)
                        act.activation(SQ[:, k % 2, 0:w], src(k), ACT.Square).then_inc(sq_ready, 1)
                    n["job"] += 1
                    root(rstd[:, 0:w])

                def root(ap):
                    asked()
                    act.activation(ap, ap, ACT.Sqrt).then_inc(act_done, 1)

                def exps(i, head):
                    it = n["item"]
                    s = it % 2
                    w = head["tiles"][i][1][1]
                    act.wait_ge(negmax, l * ITEMS + it + 1)
                    src = PROB[:, s, 0:w] if head["bias"] else score_ps[s][:, 0:w]
                    act.activation(PROB[:, s, 0:w], src, ACT.Exp, bias=small[:, s * 4 + 1:s * 4 + 2],
                                   accum_out=small[:, s * 4 + 2:s * 4 + 3]).then_inc(exp_done, 1)
                    n["item"] += 1

                def copy_turned(it, i, head):
                    kts = head["tiles"][i][2]
                    act.wait_ge(turn_done, l * ITEMS + it + 1)
                    full = sum(k[1] == P for k in kts)
                    ins = act.activation(probT[:, 0:full * P], turn_ps[:, 0:full * P], ACT.Copy)
                    if full < len(kts):
                        w = kts[-1][1]
                        ins = act.activation(probT[0:w, full * P:(full + 1) * P],
                                             turn_ps[0:w, full * P:(full + 1) * P], ACT.Copy)
                    ins.then_inc(turned, 1)

                def round_output(it, i, head):
                    t0, t1, c0 = out_tokens(head["tiles"], i)
                    ot, o0, o1 = head["o"]
                    act.wait_ge(out_done, l * ITEMS + it + 2)
                    act.activation(O_HL[0][o0:o1, ot, t0:t1], out_ps[o0:o1, c0:P], ACT.Copy).then_inc(out_rounded, 1)

                def attend(heads, steps, when):
                    flat = [(h, i) for h in heads for i in range(NQ)]
                    base = n["item"]
                    for g, step in when[-1]:
                        steps(g)[step]()
                    exps(0, flat[0][0])
                    for j in range(len(flat) + 1):
                        if j:
                            round_output(base + j - 1, flat[j - 1][1], flat[j - 1][0])
                        if j + 1 < len(flat):
                            exps(flat[j + 1][1], flat[j + 1][0])
                        if j < len(flat):
                            copy_turned(base + j, flat[j][1], flat[j][0])
                        for g, step in when.get(j, ()):
                            steps(g)[step]()

                def branch(b):
                    asked()
                    for e in range(KT):
                        place()
                        n["job"] += 1
                        act.wait_ge(job_done, l * JOBS + n["job"] + 1)
                        act.activation(halves(TMP[:, e % 2]), job_halves((n["job"] - 1) % 2), ACT.Sigmoid,
                                       bias=g_col("b_gate", b * KT + e)).then_inc(gate_done, 1)
                        n["gate"] += 1
                        if e % 2:
                            place()
                            n["job"] += 2

                squares(lambda k: X[:, k], KT)
                for _ in range(U_MLA_IN):
                    place()
                    n["job"] += 1
                squares(lambda k: ZQ[:, k], QR)
                squares(lambda k: CKV[:, k, 0:NT], CR)
                n["job"] += 1

                def count(jobs, places=0):
                    def step():
                        for _ in range(places):
                            place()
                        n["job"] += jobs
                    return step

                def steps_mla(h):
                    return [count(1, 1), count(2), count(1), count(1)]

                heads = [dict(tiles=Q_TILES, bias=False, o=(h // 2, h % 2 * 64, h % 2 * 64 + 64)) for h in range(MLA_HEADS)]
                attend(heads, steps_mla, PLAN_MLA)
                branch(0)

                for p in range(RET_HEADS // 2):
                    place()
                    n["job"] += 1
                    place()
                    n["job"] += 1 + 2 + 1
                    for j in range(2):
                        place()
                        n["job"] += 5
                        n["job"] += 2
                        root(rstd[:, :])
                        place()
                        n["job"] += 1
                        act.wait_ge(job_done, l * JOBS + n["job"] + 1)
                        act.activation(halves(TMP[:, 0]), job_halves((n["job"] - 1) % 2), ACT.Sigmoid)\
                            .then_inc(gate_done, 1)
                        n["gate"] += 1
                branch(1)

                def steps_band(p):
                    return [count(1, 1)] * 3 + [count(1)]

                heads = [dict(tiles=Q_TILES, bias=True, o=(h // 2, h % 2 * 64, h % 2 * 64 + 64)) for h in range(BAND_HEADS)]
                attend(heads, steps_band, PLAN_BAND)
                branch(2)

                for _ in range(KT):
                    place()
                    n["job"] += 1
                squares(lambda k: M[:, k], KT)
                squares(lambda k: M[:, k, 0:MEM], KT, MEM)
                squares(lambda k: X[:, k], KT)

                def steps_mem(h):
                    return [count(1, 1), count(1, 1), count(1), count(1, 1)]

                heads = [dict(tiles=MEM_TILES, bias=False, o=(h, 0, P)) for h in range(MEM_HEADS)]
                attend(heads, steps_mem, PLAN_MEM)
                for _ in range(KT // 2):
                    place()
                    n["job"] += 2
                squares(lambda k: M[:, k], KT)
                squares(lambda k: X[:, k], KT)
                with act.Fori(0, FF_CHUNKS) as c:
                    at["job"], at["unit"], at["unit_raw"] = c * (2 * KT), c * (2 * KT), c * (2 * KT // RAW)
                    for _ in range(2 * KT):
                        place()
                        n["job"] += 1
                at["job"] = at["unit"] = at["unit_raw"] = 0
                n["unit"] += (FF_CHUNKS - 1) * 2 * KT
                n["job"] += (FF_CHUNKS - 1) * 2 * KT
                squares(lambda k: M[:, k], KT)
                n["job"] += n["job"] % 2
                for _ in range(SPARE):
                    place()
                counted(**n)
            for s in range(RAW):
                act.wait_ge(raw_loaded[s], (DEPTH * UNITS + LEAD) // RAW * 16)

        @block.vector
        def _(dve):
            v = nc.vector
            dve.sem_inc(job_free, 2)
            dve.sem_inc(probs, 2)
            dve.sem_inc(out_free, 1)
            dve.sem_inc(phase_done, 1)
            v.memset(small[:, :], 0.0)
            dve.drain()
            dve.wait_ge(x_loaded, 16)
            dve.wait_ge(c_loaded, 16)
            with dve.Fori(0, DEPTH) as l:
                n = dict(job=0, freed=0, gate=0, ready=0, ask=0, done=0, item=0, store=0)
                at = dict(job=0)

                def job():
                    n["job"] += 1
                    dve.wait_ge(job_done, l * JOBS + at["job"] + n["job"] + 1)
                    return (n["job"] - 1) % 2

                def skip():
                    n["job"] += 1

                def free(ins):
                    n["freed"] += 1
                    ins.then_inc(job_free, 1)

                def is_ready(ins):
                    n["ready"] += 1
                    ins.then_inc(ready, 1)

                def ask(ins):
                    n["ask"] += 1
                    ins.then_inc(act_asked, 1)

                def wait_act():
                    n["done"] += 1
                    dve.wait_ge(act_done, l * ROOTS + n["done"])

                def split(src, hi, lo):
                    v.tensor_copy(hi, src)
                    dve.drain()
                    return v.tensor_tensor(lo, src, hi.bitcast(F32), ALU.subtract)

                def copy_job(dst, p0=0, p1=P):
                    s = job()
                    free(v.tensor_copy(halves(dst), job_halves(s, p0, p1)))

                def store(ins=None):
                    n["store"] += 1
                    dve.drain()
                    dve.sem_inc(store_asked, 1)

                def wait_stores():
                    dve.wait_ge(stored, (l * STORES + n["store"]) * 16)

                def inv_root(scale, w=NT):
                    s = job()
                    if w == NT:
                        dst, src = halves(rstd[:, :]), job_halves(s)
                    else:
                        dst, src = rstd[:, 0:w], job_ps[s][:, 0:w]
                    free(v.tensor_scalar(dst, src, scale, EPS, ALU.mult, ALU.add))
                    dve.drain()
                    dve.sem_inc(act_asked, 1)
                    n["ask"] += 1
                    wait_act()
                    v.reciprocal(rstd[:, 0:w], rstd[:, 0:w])
                    dve.drain()

                def squares_may_start():
                    dve.drain()
                    dve.sem_inc(act_asked, 1)
                    n["ask"] += 1

                def norm_split(src, name, kt, hl, w=NT, each=True):
                    for k in range(0, kt, 2):
                        for j in range(2):
                            v.scalar_tensor_tensor(out=TMP[:, j, 0:w], in0=src(k + j), scalar=g_col(name, k + j),
                                                   in1=rstd[:, 0:w], op0=ALU.mult, op1=ALU.mult)
                        dve.drain()
                        ins = split(TMP[:, :, 0:w], hl[0][:, k:k + 2], hl[1][:, k:k + 2])
                        if each:
                            is_ready(ins)
                        dve.drain()
                    if not each:
                        is_ready(v.tensor_copy(small[:, 12:13], small[:, 13:14]))

                def post_norm(name):
                    squares_may_start()
                    inv_root(1.0 / D)
                    for k in range(0, KT, 2):
                        for j in range(2):
                            v.scalar_tensor_tensor(out=TMP[:, j], in0=M[:, k + j], scalar=g_col(name, k + j),
                                                   in1=rstd[:, :], op0=ALU.mult, op1=ALU.mult)
                        dve.drain()
                        v.tensor_tensor(X[:, k:k + 2], X[:, k:k + 2], TMP, ALU.add)
                        dve.drain()

                def rope(buf, p0, p1, scale=None):
                    s = job()
                    free(v.tensor_tensor(halves(rstd[p0:p1, :]), job_halves(s, p0, p1), halves(SIN[p0:p1, :]),
                                         ALU.mult))
                    v.tensor_tensor(buf[p0:p1, :], buf[p0:p1, :], COS[p0:p1, :], ALU.mult)
                    dve.drain()
                    if scale is None:
                        return v.tensor_tensor(buf[p0:p1, :], buf[p0:p1, :], rstd[p0:p1, :], ALU.add)
                    v.tensor_tensor(buf[p0:p1, :], buf[p0:p1, :], rstd[p0:p1, :], ALU.add)
                    dve.drain()
                    return v.tensor_scalar(buf[p0:p1, :], buf[p0:p1, :], scale, None, ALU.mult)

                def maxima(i, head):
                    it = n["item"]
                    s = it % 2
                    w = head["tiles"][i][1][1]
                    dve.wait_ge(score_done, l * ITEMS + it + 1)
                    src = score_ps[s][:, 0:w]
                    if head["bias"] is not None:
                        h = head["bias"]
                        if i == 0:
                            dve.wait_ge(b_loaded[h % 2], (l * 4 + h // 2 + 1) * 16)
                        parts = [(0, w, SEQ - w)] if i < NQ - 1 else [(0, DEC, SEQ - DEC), (DEC, w, SEQ - DEC - PAST)]
                        for a, b, x in parts:
                            v.scalar_tensor_tensor(out=PROB[:, s, a:b], in0=score_ps[s][:, a:b], scalar=BAND_HD ** -0.5,
                                                   in1=BIAS[:, h % 2, x:x + b - a], op0=ALU.mult, op1=ALU.add)
                        dve.drain()
                        src = PROB[:, s, 0:w]
                    v.tensor_reduce(small[:, s * 4 + 1:s * 4 + 2], src, AX_X, ALU.max, negate=True)\
                        .then_inc(negmax, 1)
                    n["item"] += 1

                def normalise(it, i, head):
                    s = it % 2
                    w = head["tiles"][i][1][1]
                    dve.wait_ge(exp_done, l * ITEMS + it + 1)
                    v.reciprocal(small[:, s * 4 + 3:s * 4 + 4], small[:, s * 4 + 2:s * 4 + 3])
                    dve.drain()
                    v.tensor_scalar(PROB[:, s, 0:w], PROB[:, s, 0:w], small[:, s * 4 + 3:s * 4 + 4], None,
                                    ALU.mult).then_inc(probs, 1)

                def split_output(it, i, head):
                    t0, t1, c0 = out_tokens(head["tiles"], i)
                    ot, o0, o1 = head["o"]
                    dve.wait_ge(out_rounded, l * ITEMS + it + 1)
                    v.tensor_tensor(O_HL[1][o0:o1, ot, t0:t1], out_ps[o0:o1, c0:P],
                                    O_HL[0][o0:o1, ot, t0:t1].bitcast(F32), ALU.subtract).then_inc(out_free, 1)

                def attend(heads, steps, when):
                    flat = [(h, i) for h in heads for i in range(NQ)]
                    base = n["item"]
                    for g, step in when[-1]:
                        steps(g)[step]()
                    maxima(0, flat[0][0])
                    for j in range(len(flat) + 1):
                        if j < len(flat):
                            normalise(base + j, flat[j][1], flat[j][0])
                        if j + 1 < len(flat):
                            maxima(flat[j + 1][1], flat[j + 1][0])
                        if j:
                            split_output(base + j - 1, flat[j - 1][1], flat[j - 1][0])
                            for g, step in when.get(j - 1, ()):
                                steps(g)[step]()

                def branch(first):
                    squares_may_start()
                    for e in range(KT):
                        if e % 2 == 0:
                            skip()
                            skip()
                        s = job()
                        n["gate"] += 1
                        dve.wait_ge(gate_done, l * GATES + n["gate"])
                        if first:
                            free(v.tensor_tensor(halves(M[:, e]), job_halves(s), halves(TMP[:, e % 2]), ALU.mult))
                        else:
                            v.tensor_tensor(halves(TMP[:, e % 2]), job_halves(s), halves(TMP[:, e % 2]), ALU.mult)
                            dve.drain()
                            free(v.tensor_tensor(M[:, e], M[:, e], TMP[:, e % 2], ALU.add))

                dve.wait_ge(layer_loaded, (l + 1) * 16 * LAYER_LOADS)
                dve.sem_inc(settled[1], 1)
                squares_may_start()
                inv_root(1.0 / D)
                norm_split(lambda k: X[:, k], "pre_mix", KT, U_HL)
                for k in range(QR):
                    copy_job(ZQ[:, k])
                for k in range(CR):
                    copy_job(CKV[:, k, 0:NT])
                copy_job(TMP[:, 0])
                squares_may_start()
                inv_root(1.0 / (QR * P))
                for k in range(QR):
                    v.scalar_tensor_tensor(out=ZQ[:, k], in0=ZQ[:, k], scalar=g_col("mla_q", k), in1=rstd[:, :],
                                           op0=ALU.mult, op1=ALU.mult)
                squares_may_start()
                split(m_sb[:, 0:QR * NT], arena[:, Z0:Z0 + QR * NT], arena[:, Z0 + QR * NT:Z0 + 2 * QR * NT])
                dve.drain()
                inv_root(1.0 / (CR * P))
                for k in range(CR):
                    v.scalar_tensor_tensor(out=CKV[:, k, 0:NT], in0=CKV[:, k, 0:NT], scalar=g_col("mla_kv", k),
                                           in1=rstd[:, :], op0=ALU.mult, op1=ALU.mult)
                dve.drain()
                z = Z0 + 2 * QR * NT
                split(m_sb[:, QR * NT:QR * NT + CR * KEYS], arena[:, z:z + CR * KEYS],
                      arena[:, z + CR * KEYS:z + 2 * CR * KEYS])
                dve.drain()
                s = job()
                free(v.tensor_tensor(halves(rstd[NOPE:QK, :]), job_halves(s, NOPE, QK), halves(SIN[NOPE:QK, :]),
                                     ALU.mult))
                v.tensor_tensor(TMP[NOPE:QK, 0], TMP[NOPE:QK, 0], COS[NOPE:QK, :], ALU.mult)
                dve.drain()
                for b in range(2):
                    ins = v.tensor_tensor(K[NOPE:QK, b, 0:NT], TMP[NOPE:QK, 0], rstd[NOPE:QK, :], ALU.add)
                is_ready(ins)
                store()
                store()
                dve.drain()

                def steps_mla(h):
                    b = h % 2

                    def queries():
                        s = job()
                        free(v.tensor_scalar(halves(Q[0:QK, b]), job_halves(s, 0, QK), QK ** -0.5, None, ALU.mult))

                    def keys_values():
                        s = job()
                        v.tensor_copy(halves(K[0:NOPE, b, 0:NT]), job_halves(s, 0, NOPE))
                        free(v.tensor_copy(halves(vT[:, 0:NT]), job_halves(s)))
                        s = job()
                        v.tensor_copy(K[0:NOPE, b, NT:KEYS], job_ps[s][0:NOPE, 0:PAST])
                        free(v.tensor_copy(vT[:, NT:KEYS], job_ps[s][:, 0:PAST]))

                    def rotate():
                        s = job()
                        v.tensor_tensor(halves(rstd[NOPE:QK, :]), job_halves(s, NOPE, QK), halves(SIN[NOPE:QK, :]),
                                        ALU.mult)
                        v.tensor_tensor(Q[NOPE:QK, b], Q[NOPE:QK, b], COS[NOPE:QK, :], ALU.mult)
                        dve.drain()
                        free(v.tensor_tensor(Q[NOPE:QK, b], Q[NOPE:QK, b], rstd[NOPE:QK, :], ALU.add))

                    def values():
                        s = job()
                        v.tensor_copy(V[:, b, 0:4, 0:MLA_V], tiles(job_ps[s][:, 0:512], 4)[:, :, NOPE:P])
                        v.tensor_copy(V[:, b, 4:6, 0:MLA_V], tiles(job_ps[s][:, 512:768], 2)[:, :, NOPE:P])
                        free(v.tensor_copy(V[0:DEC, b, 6, 0:MLA_V], job_ps[s][0:DEC, 768 + NOPE:768 + P]))

                    return [queries, keys_values, rotate, values]

                heads = [dict(tiles=Q_TILES, bias=None,
                              o=(h // 2, h % 2 * 64, h % 2 * 64 + 64)) for h in range(MLA_HEADS)]
                attend(heads, steps_mla, PLAN_MLA)
                dve.drain()
                wait_stores()
                dve.sem_inc(phase_done, 1)
                branch(True)

                dve.wait_ge(r_loaded, (l + 1) * 16 * RET_LOADS)
                v.memset(V[DEC:P, 0, 4, :], 0.0)
                v.memset(prob_sb[DEC:P, 512:512 + DEC], 0.0)
                for p in range(RET_HEADS // 2):
                    copy_job(Q[:, 0])
                    copy_job(K[:, 0, 0:NT])
                    dve.drain()
                    s = job()
                    v.tensor_tensor(halves(rstd[:, :]), job_halves(s), halves(SIN), ALU.mult)
                    v.tensor_tensor(Q[:, 0], Q[:, 0], COS, ALU.mult)
                    dve.drain()
                    free(v.tensor_tensor(Q[:, 0], Q[:, 0], rstd[:, :], ALU.add))
                    dve.drain()
                    for t in range(5):
                        w = P if t < 4 else DEC
                        v.tensor_tensor(QX[:, t * P:t * P + w], Q[:, 0, t * P:t * P + w], cst("cross", p * P, w),
                                        ALU.mult)
                    s = job()
                    v.tensor_tensor(halves(rstd[:, :]), job_halves(s), halves(SIN), ALU.mult)
                    v.tensor_tensor(K[:, 0, 0:NT], K[:, 0, 0:NT], COS, ALU.mult)
                    dve.drain()
                    v.tensor_tensor(K[:, 0, 0:NT], K[:, 0, 0:NT], rstd[:, :], ALU.add)
                    dve.drain()
                    free(v.tensor_scalar(K[:, 0, 0:NT], K[:, 0, 0:NT], RET_DK ** -0.5, None, ALU.mult))
                    s = job()
                    for j in range(2):
                        h, r0 = 2 * p + j, j * RET_DK
                        v.tensor_scalar(KW[:, 0:4, r0:r0 + RET_DK], tiles(job_ps[s][:, 0:512], 4)[:, :, r0:r0 + RET_DK],
                                        cst("w_prompt", h), None, ALU.mult)
                        ins = v.tensor_scalar(KW[0:DEC, 4, r0:r0 + RET_DK], job_ps[s][0:DEC, 512 + r0:512 + r0 + RET_DK],
                                              cst("w_sample", h, 1, 0, DEC), None, ALU.mult)
                    free(ins)
                    if p:
                        wait_stores()
                    for j in range(2):
                        h, r0, r1 = 2 * p + j, j * RET_DK, (j + 1) * RET_DK
                        copy_job(TMP[:, 0])
                        s = job()
                        v.tensor_copy(V[:, 0, 0:4, :], tiles(job_ps[s][:, 0:512], 4))
                        free(v.tensor_copy(V[0:DEC, 0, 4, :], job_ps[s][0:DEC, 512:512 + P]))
                        s = job()
                        for t in range(4):
                            v.tensor_tensor(prob_sb[:, t * P:(t + 1) * P], job_ps[s][:, t * P:(t + 1) * P],
                                            cst("decay", h * P, P), ALU.mult)
                        free(v.tensor_tensor(prob_sb[0:DEC, 512:512 + DEC], job_ps[s][0:DEC, 512:512 + DEC],
                                             cst("decay", h * P, DEC, 0, DEC), ALU.mult))
                        s = job()
                        gp, gs = cst("g_prompt", p, 1, r0, r1), cst("g_sample", p, 1, r0, r1)
                        v.tensor_copy(ST[r0:r1, 4, :], probT[r0:r1, p * P:(p + 1) * P])
                        v.tensor_copy(ST[r0:r1, 0, :], job_ps[s][r0:r1, 0:P])
                        for t in range(1, 4):
                            dve.drain()
                            v.scalar_tensor_tensor(out=ST[r0:r1, t, :], in0=ST[r0:r1, t - 1, :], scalar=gp,
                                                   in1=job_ps[s][r0:r1, t * P:(t + 1) * P], op0=ALU.mult, op1=ALU.add)
                        free(v.scalar_tensor_tensor(out=ST[r0:r1, 5, :], in0=ST[r0:r1, 4, :], scalar=gs,
                                                    in1=job_ps[s][r0:r1, 512:512 + P], op0=ALU.mult, op1=ALU.add))
                        is_ready(v.tensor_copy(small[:, 12:13], small[:, 13:14]))
                        s = job()
                        v.tensor_copy(TMP[:, 0, 0:SEQ], job_ps[s][:, 0:SEQ])
                        free(v.tensor_copy(TMP[:, 0, SEQ:NT], job_ps[s][:, 512:512 + DEC]))
                        dve.drain()
                        s = job()
                        free(v.scalar_tensor_tensor(out=halves(TMP[:, 1]), in0=job_halves(s), scalar=-1.0 / RET_DV,
                                                    in1=halves(TMP[:, 0]), op0=ALU.mult, op1=ALU.add))
                        dve.drain()
                        is_ready(v.tensor_tensor(TMP[:, 0], TMP[:, 1], TMP[:, 1], ALU.mult))
                        inv_root(1.0 / RET_DV)
                        v.scalar_tensor_tensor(out=TMP[:, 1], in0=TMP[:, 1], scalar=g_col("ret_gn", h),
                                               in1=rstd[:, :], op0=ALU.mult, op1=ALU.mult)
                        dve.drain()
                        s = job()
                        n["gate"] += 1
                        dve.wait_ge(gate_done, l * GATES + n["gate"])
                        free(v.tensor_tensor(halves(TMP[:, 0]), job_halves(s), halves(TMP[:, 0]), ALU.mult))
                        dve.drain()
                        v.tensor_tensor(TMP[:, 1], TMP[:, 1], TMP[:, 0], ALU.mult)
                        dve.drain()
                        split(TMP[:, 1], O_HL[0][:, h], O_HL[1][:, h])
                        dve.drain()
                    store()
                    store()
                is_ready(v.tensor_copy(small[:, 12:13], small[:, 13:14]))
                dve.drain()
                wait_stores()
                dve.sem_inc(phase_done, 1)
                branch(False)

                def steps_band(p):
                    b = p % 2

                    def keys():
                        wait_stores()
                        copy_job(K[:, b, 0:NT])

                    def values():
                        s = job()
                        v.tensor_copy(V[:, b, 0:4, :], tiles(job_ps[s][:, 0:512], 4))
                        free(v.tensor_copy(V[0:DEC, b, 6, :], job_ps[s][0:DEC, 768:768 + P]))
                        store()
                        store()

                    return [lambda: copy_job(Q[:, b]), keys, lambda: copy_job(vT[:, 0:NT]), values]

                heads = [dict(tiles=Q_TILES, bias=h, o=(h // 2, h % 2 * 64, h % 2 * 64 + 64))
                         for h in range(BAND_HEADS)]
                attend(heads, steps_band, PLAN_BAND)
                dve.drain()
                wait_stores()
                dve.sem_inc(phase_done, 1)
                branch(False)
                dve.drain()
                for k in range(0, KT, 2):
                    is_ready(split(M[:, k:k + 2], U_HL[0][:, k:k + 2], U_HL[1][:, k:k + 2]))
                for k in range(KT):
                    copy_job(M[:, k])
                post_norm("post_mix")

                dve.drain()
                dve.sem_inc(phase_done, 1)
                dve.wait_ge(mem_loaded, (l + 1) * 16)
                dve.sem_inc(settled[1], 1)
                squares_may_start()
                inv_root(1.0 / D, MEM)
                norm_split(lambda k: M[:, k, 0:MEM], "mem", KT, MEM_HL, MEM, each=False)
                squares_may_start()
                inv_root(1.0 / D)
                norm_split(lambda k: X[:, k], "pre_mem", KT, U_HL)

                def steps_mem(h):
                    b = h % 2

                    def keys():
                        wait_stores()
                        s = job()
                        free(v.tensor_copy(K[:, b, 0:MEM], job_ps[s][:, 0:MEM]))

                    def values_t():
                        s = job()
                        free(v.tensor_copy(vT[:, 0:MEM], job_ps[s][:, 0:MEM]))

                    def values():
                        s = job()
                        free(v.tensor_copy(V[:, b, 0:2, :], tiles(job_ps[s][:, 0:256], 2)))
                        store()
                        store()

                    def queries():
                        s = job()
                        free(v.tensor_scalar(halves(Q[:, b]), job_halves(s), MEM_HD ** -0.5, None, ALU.mult))

                    return [keys, values_t, values, queries]

                heads = [dict(tiles=MEM_TILES, bias=None, o=(h, 0, P)) for h in range(MEM_HEADS)]
                attend(heads, steps_mem, PLAN_MEM)
                wait_stores()
                for k in range(KT):
                    copy_job(M[:, k])
                post_norm("post_mem")

                squares_may_start()
                inv_root(1.0 / D)
                norm_split(lambda k: X[:, k], "pre_ff", KT, U_HL)
                v.memset(m_sb[:, :], 0.0)
                dve.drain()
                with dve.Fori(0, FF_CHUNKS) as c:
                    at["job"] = c * (2 * KT)
                    for e in range(KT):
                        s = job()
                        v.tensor_scalar(halves(TMP[:, e % 2]), job_halves(s), 0.0, None, ALU.max)
                        dve.drain()
                        v.tensor_tensor(TMP[:, e % 2], TMP[:, e % 2], TMP[:, e % 2], ALU.mult)
                        dve.drain()
                        free(split(TMP[:, e % 2], H_HL[0][:, e], H_HL[1][:, e]))
                    for e in range(KT):
                        s = job()
                        free(v.tensor_tensor(halves(M[:, e]), job_halves(s), halves(M[:, e]), ALU.add))
                    dve.drain()
                at["job"] = 0
                for k in ("job", "freed"):
                    n[k] += (FF_CHUNKS - 1) * 2 * KT
                post_norm("post_ff")
                if n["job"] % 2:
                    s = job()
                    free(v.tensor_copy(small[:, 14:15], job_ps[s][:, 0:1]))
                dve.drain()
                dve.sem_inc(phase_done, 1)
                counted(**n)

        @block.sync
        def _(sp):
            sp.dma_start(const[:, :], const_in).then_inc(c_loaded, 16)
            sp.dma_start(x_sb[:, :], x_in).then_inc(x_loaded, 16)

            def row(t, l, *more):
                ap = t[bass.ds(l, 1)]
                return ap

            with sp.Fori(0, DEPTH) as l:
                n = dict(store=0)

                def store(dst, src):
                    n["store"] += 1
                    sp.wait_ge(store_asked, l * STORES + n["store"])
                    sp.dma_start(dst, src).then_inc(stored, 16)

                sp.wait_ge(phase_done, l * DVE_PHASES + 1)
                sp.dma_start(gain[:, :], gain_in[bass.ds(l, 1)].rearrange("a p n -> p (a n)")).then_inc(layer_loaded, 16)
                sp.dma_start(cs_sb[:, :], rope_in[0]).then_inc(layer_loaded, 16)
                sp.dma_start(CKV[:, :, NT:KEYS], ckv_in[bass.ds(l, 1)].rearrange("a p k n -> p (a k) n"))\
                    .then_inc(layer_loaded, 16)
                for b in range(2):
                    sp.dma_start(K[NOPE:QK, b, NT:KEYS], kpe_in[bass.ds(l, 1)].rearrange("a p n -> p (a n)"))\
                        .then_inc(layer_loaded, 16)
                store(ckv_out[bass.ds(l, 1)].rearrange("a p k n -> p (a k) n"), CKV[:, :, 0:NT])
                store(kpe_out[bass.ds(l, 1)].rearrange("a p n -> p (a n)"), K[NOPE:QK, 0, 0:NT])
                sp.wait_ge(phase_done, l * DVE_PHASES + 2)
                sp.dma_start(cs_sb[:, :], rope_in[1]).then_inc(r_loaded, 16)
                sp.dma_start(probT[:, 0:2 * P], state_in[bass.ds(l, 1)].rearrange("a p h n -> p (a h n)"))\
                    .then_inc(r_loaded, 16)
                for p in range(2):
                    store(retp_out[bass.ds(l, 1), :, p].rearrange("a p n -> p (a n)"), ST[:, 3, :])
                    store(rets_out[bass.ds(l, 1), :, p].rearrange("a p n -> p (a n)"), ST[:, 5, :])
                sp.wait_ge(phase_done, l * DVE_PHASES + 3)

                def load_bias(h):
                    sp.dma_start(BIAS[:, h % 2], bias_in[bass.ds(l, 1), h].rearrange("a p n -> p (a n)"))\
                        .then_inc(b_loaded[h % 2], 16)

                def load_band(p):
                    sp.dma_start(K[:, p % 2, NT:KEYS], bandk_in[bass.ds(l, 1), p].rearrange("a p n -> p (a n)"))\
                        .then_inc(kv_loaded[p % 2], 16)
                    sp.dma_start(V[:, p % 2, 4:6, :], bandv_in[bass.ds(l, 1), p].rearrange("a p t n -> p (a t) n"))\
                        .then_inc(kv_loaded[p % 2], 16)

                for i in range(2):
                    load_bias(i)
                    load_band(i)
                for p in range(BAND_HEADS // 2):
                    store(bandk_out[bass.ds(l, 1), p].rearrange("a p n -> p (a n)"), K[:, p % 2, 0:NT])
                    store(bandv_out[bass.ds(l, 1), p].rearrange("a p n -> p (a n)"), vT[:, 0:NT])
                    for h in (2 * p, 2 * p + 1):
                        if h + 2 < BAND_HEADS:
                            sp.wait_ge(out_free, l * ITEMS + I_BAND + (h + 1) * NQ + 1)
                            load_bias(h + 2)
                    if p + 2 < BAND_HEADS // 2:
                        load_band(p + 2)

                def load_mem(h):
                    sp.dma_start(K[:, h % 2, MEM:2 * MEM], memk_in[bass.ds(l, 1), h].rearrange("a p n -> p (a n)"))\
                        .then_inc(kv_loaded[h % 2], 16)
                    sp.dma_start(V[:, h % 2, 2:4, :], memv_in[bass.ds(l, 1), h].rearrange("a p t n -> p (a t) n"))\
                        .then_inc(kv_loaded[h % 2], 16)

                sp.wait_ge(phase_done, l * DVE_PHASES + 4)
                for i in range(2):
                    load_mem(i)
                sp.wait_ge(phase_done, l * DVE_PHASES + 5)
                sp.dma_start(M[:, :, 0:MEM], mem_in).then_inc(mem_loaded, 16)
                for h in range(MEM_HEADS):
                    store(memk_out[bass.ds(l, 1), h].rearrange("a p n -> p (a n)"), K[:, h % 2, 0:MEM])
                    store(memv_out[bass.ds(l, 1), h].rearrange("a p n -> p (a n)"), vT[:, 0:MEM])
                    if h + 2 < MEM_HEADS:
                        sp.wait_ge(out_free, l * ITEMS + I_MEM + (h + 1) * NQ + 1)
                        load_mem(h + 2)
            sp.wait_ge(phase_done, DEPTH * DVE_PHASES + 1)
            sp.dma_start(y_out, x_sb[:, :]).then_inc(stored, 16)
            sp.wait_ge(stored, (DEPTH * STORES + 1) * 16)


SQUARES = 7 * KT + QR + CR
SQ_USES = 7 * (KT - 2) + QR - 2
ROOTS = 9 + RET_HEADS
LAYER_LOADS = 5
RET_LOADS = 2
DVE_PHASES = 5


def counted(**n):
    want = dict(job=JOBS, unit=UNITS, freed=DVE_FREED, gate=GATES, ready=READY, ask=REQS, item=ITEMS, done=ROOTS,
                store=STORES)
    assert all(want.get(k, v) == v for k, v in n.items()), n


def constants():
    c = np.zeros((P, NCONST), np.float32)

    def put(name, a):
        c[:a.shape[0], CONST[name]:CONST[name] + a.shape[1]] = a

    put("ident", np.eye(P))
    put("ones", np.ones((P, P)))
    for name, half, r0, r1 in (("rot_ret", RET_DK // 2, 0, P), ("rot_pe", ROPE // 2, NOPE, QK)):
        m = np.zeros((P, P))
        for i in range(r0, r1):
            j = (i - r0) % (2 * half)
            if j < half:
                m[i + half, i] = -1
            else:
                m[i - half, i] = 1
        put(name, m)
    first = np.zeros((1, P))
    first[0, :CHUNK] = 1
    put("first", first)
    neg = np.zeros((1, P))
    neg[0, CHUNK:] = NEG
    put("neg", neg)
    g = np.log1p(-np.exp2(-5.0 - np.arange(RET_HEADS)))
    t = np.arange(P)
    cross = np.zeros((P, 2 * P))
    gp, gs = np.zeros((P, 2)), np.zeros((P, 2))
    for p in range(2):
        for j in range(2):
            r = slice(j * RET_DK, (j + 1) * RET_DK)
            cross[r, p * P:(p + 1) * P] = np.exp(g[2 * p + j] * (t + 1.0))
            gp[r, p] = np.exp(g[2 * p + j] * P)
            gs[r, p] = np.exp(g[2 * p + j] * DEC)
    put("cross", cross)
    put("g_prompt", gp)
    put("g_sample", gs)
    diff = t[None, :] - t[:, None]
    put("decay", np.concatenate([np.where(diff >= 0, np.exp(x * np.maximum(diff, 0)), 0) for x in g], 1))
    put("w_prompt", np.stack([np.exp(x * (P - 1.0 - t)) for x in g], 1))
    put("w_sample", np.stack([np.exp(x * (DEC - 1.0 - t[:DEC])) for x in g], 1))
    pos = np.concatenate([np.arange(SEQ), PAST + np.arange(DEC)]).astype(np.float32)
    rope = np.zeros((2, P, 2 * NT), np.float32)
    for i, (half, r0, r1) in enumerate(((ROPE // 2, NOPE, QK), (RET_DK // 2, 0, P))):
        inv = np.float32(10000.0) ** (-np.arange(half, dtype=np.float32) / np.float32(half))
        ang = (inv[:, None] * pos[None, :]).astype(np.float32)
        rows = (np.arange(r0, r1) - r0) % half
        rope[i, r0:r1, :NT] = np.cos(ang)[rows]
        rope[i, r0:r1, NT:] = np.sin(ang)[rows]
    return c, rope


def kernel(**inputs):
    import concourse.bacc as bacc
    from concourse.bass_utils import run_bass_kernel_spmd

    a = {k: np.asarray(v) for k, v in inputs.items()}

    def fm(x):
        return x.T.reshape(-1, P, x.shape[0]).transpose(1, 0, 2)

    def w_tile(w, width=P):
        return w.reshape(-1, P, w.shape[1]).transpose(1, 0, 2).reshape(P, -1)

    units = []

    def add(*parts):
        u = np.concatenate(parts, 1)
        units.append(np.pad(u, ((0, 0), (0, D - u.shape[1]))))

    sizes = (384, 256, 32, 256, 256, 512, 512, 512, 512, 512, 3072)
    off = np.concatenate([[0], np.cumsum(sizes)])
    zq, zkv, zpe, rq, rk, rv, rg, cq, ck, cv, zg = off[:11]
    for l in range(DEPTH):
        w = a["w_in"][l]
        cols = lambda c: w_tile(w[:, c:c + P])

        def branch(b, wb):
            for e in range(0, KT, 2):
                add(cols(zg + b * D + e * P))
                add(cols(zg + b * D + (e + 1) * P))
                add(w_tile(wb[:, e * P:(e + 1) * P]), w_tile(wb[:, (e + 1) * P:(e + 2) * P]))

        for i in range(QR):
            add(cols(zq + i * P))
        for i in range(CR):
            add(cols(zkv + i * P))
        add(cols(zpe - NOPE))
        for h in range(MLA_HEADS):
            add(w_tile(a["w_mla_uq"][l][:, h]), w_tile(a["w_mla_ukv"][l][:, h]))
        branch(0, a["w_br_a"][l])
        for p in range(2):
            add(cols(rq + p * P))
            add(cols(rk + p * P))
            for h in (2 * p, 2 * p + 1):
                add(cols(rv + h * P))
                add(cols(rg + h * P))
        branch(1, a["w_br_b"][l])
        for p in range(4):
            for c in (cq, ck, cv):
                add(cols(c + p * P))
        branch(2, a["w_br_c"][l])
        for e in range(KT):
            add(w_tile(a["w_out"][l][:, e * P:(e + 1) * P]))
        for h in range(MEM_HEADS):
            for name in ("w_mem_k", "w_mem_v", "w_mem_q"):
                add(w_tile(a[name][l][:, h]))
        wo = a["w_mem_o"][l].reshape(MEM_HEADS * MEM_HD, D)
        for e in range(0, KT, 2):
            add(w_tile(wo[:, e * P:(e + 1) * P]), w_tile(wo[:, (e + 1) * P:(e + 2) * P]))
        for c in range(FF_CHUNKS):
            for e in range(KT):
                add(w_tile(a["w_up"][l][:, c * D + e * P:c * D + (e + 1) * P]))
            for e in range(KT):
                add(w_tile(a["w_down"][l][c * D:(c + 1) * D, e * P:(e + 1) * P]))
        for _ in range(SPARE):
            units.append(np.zeros((P, D), np.float32))
        assert len(units) == (l + 1) * UNITS
    for _ in range(LEAD):
        units.append(np.zeros((P, D), np.float32))

    def col(x):
        return x.reshape(DEPTH, -1, P).transpose(0, 2, 1)

    gains = np.concatenate([col(a[k]) for k in ("g_pre_mix", "g_post_mix", "g_pre_mem", "g_mem", "g_post_mem",
                                                "g_pre_ff", "g_post_ff", "g_mla_q", "g_mla_kv", "g_ret_gn",
                                                "b_gate")], 2)
    consts, rope = constants()
    rel = np.arange(P)[:, None] + (SEQ - P) - np.arange(SEQ)[None, :]
    bias = a["band_rel_bias"][:, :, np.clip(rel, -128, 128) + 128].astype(np.float32)
    bias[:, :, :CHUNK, SEQ - CHUNK:] = NEG

    def keyT(x, g):
        return x.reshape(DEPTH, x.shape[2], g, P).transpose(0, 2, 3, 1)

    def val(x, g):
        return x.reshape(DEPTH, 2, P, g, P).transpose(0, 3, 2, 1, 4)

    ins = dict(
        x=fm(np.concatenate([a["x_prompt"][0], a["x_sample"][0]])).reshape(P, -1),
        mem=fm(a["mem_prompt"][0]), w=np.stack(units),
        ckv=np.stack([fm(a["cache_mla_ckv"][l, 0]) for l in range(DEPTH)]),
        kpe=a["cache_mla_kpe"][:, 0].transpose(0, 2, 1),
        state=a["state_ret"][:, 0].reshape(DEPTH, 2, P, RET_DV).transpose(0, 2, 1, 3),
        bandk=keyT(a["cache_band_k"], 4), bandv=val(a["cache_band_v"], 4),
        memk=keyT(a["cache_mem_k"], 4), memv=val(a["cache_mem_v"], 4),
        bias=bias, gain=gains, const=consts, rope=rope)
    outs = dict(
        y=(P, KT * NT), o_ckv=(DEPTH, P, CR, NT), o_kpe=(DEPTH, ROPE, NT), o_retp=(DEPTH, P, 2, RET_DV),
        o_rets=(DEPTH, P, 2, RET_DV), o_bandk=(DEPTH, 4, P, NT), o_bandv=(DEPTH, 4, P, NT),
        o_memk=(DEPTH, 4, P, MEM), o_memv=(DEPTH, 4, P, MEM))
    nc = bacc.Bacc("TRN2", target_bir_lowering=False, num_devices=1)
    arrays = {k: np.ascontiguousarray(v) for k, v in ins.items()}
    args = [nc.dram_tensor("in_" + k, v.shape, F32, kind="ExternalInput").ap() for k, v in arrays.items()]
    args += [nc.dram_tensor("out_" + k, s, F32, kind="ExternalOutput").ap() for k, s in outs.items()]
    build(nc, *args)
    r = run_bass_kernel_spmd(nc, [{"in_" + k: v for k, v in arrays.items()}], core_ids=[0]).results[0]
    r = {k: r["out_" + k] for k in outs}

    y = np.asarray(r["y"]).reshape(P, KT, NT).transpose(2, 1, 0).reshape(NT, D)
    ckv = np.asarray(r["o_ckv"]).transpose(0, 3, 2, 1).reshape(DEPTH, NT, CR * P)
    kpe = np.asarray(r["o_kpe"]).transpose(0, 2, 1)
    ret = [np.asarray(r[k]).transpose(0, 2, 1, 3).reshape(DEPTH, 1, RET_HEADS, RET_DK, RET_DV)
           for k in ("o_retp", "o_rets")]
    bk, bv = (np.asarray(r[k]).transpose(0, 3, 1, 2).reshape(DEPTH, NT, BAND_HEADS, BAND_HD)
              for k in ("o_bandk", "o_bandv"))
    mk, mv = (np.asarray(r[k]).transpose(0, 3, 1, 2).reshape(DEPTH, 1, MEM, MEM_HEADS, MEM_HD)
              for k in ("o_memk", "o_memv"))
    cut = lambda t: (np.ascontiguousarray(t[:, None, :SEQ]), np.ascontiguousarray(t[:, None, SEQ:]))
    (pc, sc), (pk, sk), (pbk, sbk), (pbv, sbv) = cut(ckv), cut(kpe), cut(bk), cut(bv)
    return (np.ascontiguousarray(y[None, :SEQ]), np.ascontiguousarray(y[None, SEQ:]), pc, pk, ret[0], pbk, pbv,
            mk, mv, sc, sk, ret[1], sbk, sbv)
```

```python
from contextlib import ExitStack

import numpy as np

import concourse.bass as bass
from concourse import mybir

F32 = mybir.dt.float32
F32R = mybir.dt.float32r
ALU = mybir.AluOpType
ACT = mybir.ActivationFunctionType
AX_X = mybir.AxisListType.X

P = 128
DEPTH = 2
D = 1024
SEQ, DEC, PAST, MEM = 512, 64, 256, 256
NT = SEQ + DEC
HALF = NT // 2
KEYS = NT + PAST
KT = D // P
MLA_HEADS, NOPE, ROPE, MLA_V = 8, 64, 32, 64
QK = NOPE + ROPE
QR, CR = 384 // P, 256 // P
RET_HEADS, RET_DK, RET_DV = 4, 64, 128
BAND_HEADS, BAND_HD = 8, 64
MEM_HEADS, MEM_HD = 4, 128
FF = 4 * D
FF_CHUNKS = FF // D
OT = 512 // P
CHUNK = 64
EPS = 1e-6
NEG = -1e30

U_MLA_IN = QR + CR + 1
U_BRANCH = KT + KT // 2
U_RET = 2 * (2 + 2 * 2)
U_BAND = 4 * 3
U_MEM = MEM_HEADS * 3
U_FF = 2 * FF // P
_UNITS = U_MLA_IN + MLA_HEADS + 3 * U_BRANCH + U_RET + U_BAND + KT + U_MEM + KT // 2 + U_FF
UNITS = (_UNITS + 3) // 4 * 4
SPARE = UNITS - _UNITS
RING, RAW = 4, 2
LEAD = RING

GAINS = {}
_c = 0
for _n, _w in (("post_mix", KT), ("pre_mem", KT), ("mem", KT), ("post_mem", KT),
               ("pre_ff", KT), ("post_ff", KT), ("mla_q", QR), ("mla_kv", CR), ("ret_gn", RET_HEADS),
               ("b_gate", 3 * KT)):
    GAINS[_n] = _c
    _c += _w
NGAIN = _c

CONST = {}
_c = 0
for _n, _w in (("ident", P), ("ones", P), ("rot_ret", P), ("rot_pe", P), ("first", P), ("neg", P),
               ("cross", 2 * P), ("decay", RET_HEADS * P), ("w_prompt", RET_HEADS), ("w_sample", RET_HEADS),
               ("g_prompt", 2), ("g_sample", 2), ("eps", 1)):
    CONST[_n] = _c
    _c += _w
NCONST = _c

Q_TILES = [(i * P, (0, (i + 1) * P), [(j * P, P, j) for j in range(i + 1)]) for i in range(SEQ // P)]
Q_TILES.append((NT - P, (SEQ, DEC + PAST), [(DEC, P, 4), (DEC + P, P, 5), (0, DEC, 6)]))
MEM_TILES = [(i * P, (0, MEM), [(0, P, 0), (P, P, 1)]) for i in range(SEQ // P)]
MEM_TILES.append((NT - P, (MEM, MEM), [(0, P, 2), (P, P, 3)]))
NQ = len(Q_TILES)
V_TOKENS = [(i * P, P, i) for i in range(SEQ // P)]
ITEMS = (MLA_HEADS + BAND_HEADS + MEM_HEADS) * NQ
I_BAND = MLA_HEADS * NQ
I_MEM = I_BAND + BAND_HEADS * NQ



def out_tokens(tiles, i):
    t0 = tiles[i][0]
    return (t0, t0 + P, 0) if i < NQ - 1 else (SEQ, NT, P - DEC)


def plan(groups, per_group, offsets):
    at = {-1: [(0, step) for step in range(len(offsets))]}
    for g in range(1, groups):
        for step, off in enumerate(offsets):
            assert off < per_group - 2
            at.setdefault((g - 1) * per_group + off, []).append((g, step))
    return at


PLAN_MLA = plan(MLA_HEADS, NQ, (-1, 0, 1, 2))
PLAN_BAND = plan(BAND_HEADS // 2, 2 * NQ, (1, 3, 5, 7))
PLAN_MEM = plan(MEM_HEADS, NQ, (0, 1, 2, 0))
MEM_FIRST = 3
PLAN_MEM[-1] = PLAN_MEM[-1][MEM_FIRST:] + [(1, 0)]
PLAN_MEM[0].remove((1, 0))

HALVES = [(0, HALF, 0), (512, HALF, HALF)]

JOBS = 250
GATES = 3 * KT + RET_HEADS
REQS = 3 * KT + RET_HEADS + RET_HEADS // 2
READY = 42
ROUNDS = 33
ROOTS = 9 + RET_HEADS
SQUARES = 4 * KT + 3 + QR + CR
STORES = 2 + 2 * 2 + 2 * (BAND_HEADS // 2) + 2 * MEM_HEADS
LAYER_LOADS = 5
RET_LOADS = 2
DVE_PHASES = 4
AHEAD = dict(sq=KT, ask=KT, rounded=KT, done=1)


def build(nc, x_in, mem_in, w_in, ckv_in, kpe_in, state_in, bandk_in, bandv_in, memk_in, memv_in,
          bias_in, gain_in, gain_x_in, const_in, rope_in, y_out, ckv_out, kpe_out, retp_out, rets_out,
          bandk_out, bandv_out, memk_out, memv_out):
    with ExitStack() as ctx:
        def sb(name, cols, dt=F32):
            return ctx.enter_context(nc.sbuf_tensor(name, [P, cols], dt))

        def bank(name, n):
            return ctx.enter_context(nc.psum_tensor(name, [P, 512 * n], F32))

        def sem(name):
            return ctx.enter_context(nc.semaphore(name))

        def tiles(ap, k):
            return ap.rearrange("p (k n) -> p k n", k=k)

        x_sb = sb("x", KT * NT)
        m_sb = sb("m", KT * NT)
        tmp_sb = sb("tmp", 2 * NT)
        rstd = sb("rstd", NT)
        q_sb = sb("q", 2 * NT)
        k_sb = sb("k", 2 * KEYS)
        v_sb = sb("v", 2 * 7 * P)
        prob_sb = sb("prob", 3 * 512)
        probT = sb("probT", 512)
        bias_sb = sb("bias", 2 * 512)
        cs_sb = sb("cs", 2 * NT)
        const = sb("const", NCONST)
        gain = sb("gain", NGAIN)
        gain_x = sb("gain_x", KT)
        rstd_m = sb("rstd_m", MEM)
        rstd2 = sb("rstd2", NT)
        small = sb("small", 16)
        raw = sb("raw", RAW * D)
        w_hi = sb("w_hi", RING * D, F32R)
        w_lo = sb("w_lo", RING * D, F32R)
        arena = sb("arena", 3 * KT * NT + 2 * QR * NT + 2 * CR * KEYS, F32R)

        X, M = tiles(x_sb[:, :], KT), tiles(m_sb[:, :], KT)
        TMP, Q, K = tiles(tmp_sb[:, :], 2), tiles(q_sb[:, :], 2), tiles(k_sb[:, :], 2)
        V = v_sb[:, :].rearrange("p (s t n) -> p s t n", s=2, t=7)
        PROB, BIAS = tiles(prob_sb[:, :], 3), tiles(bias_sb[:, :], 2)
        COS, SIN = cs_sb[:, 0:NT], cs_sb[:, NT:2 * NT]
        SQ = Q
        SUM = SQ[:, 0]
        RTMP = bias_sb[:, 0:NT]
        rstd_c = TMP[:, 1]
        MEM_RAW = tiles(bias_sb[:, :], 4)
        UPD = tiles(prob_sb[:, 0:2 * NT], 2)
        vT = tmp_sb[:, 0:KEYS]
        RAWS = tiles(raw[:, :], RAW)
        WHI, WLO = tiles(w_hi[:, :], RING), tiles(w_lo[:, :], RING)
        ZQ = tiles(m_sb[:, 0:QR * NT], QR)
        CKV = tiles(m_sb[:, QR * NT:QR * NT + CR * KEYS], CR)
        ST = tiles(k_sb[:, KEYS:KEYS + 6 * P], 6)
        KW = V[:, 1]
        RO = prob_sb[:, 5 * P:5 * P + NT]
        RET_GATE = bias_sb[:, 0:NT], TMP[:, 1]
        QX = Q[:, 1]

        U0, O0, Z0 = 0, 2 * KT * NT, 3 * KT * NT

        def region(start, k, n):
            return tiles(arena[:, start:start + k * n], k)

        U_HL = region(U0, KT, NT), region(U0 + KT * NT, KT, NT)
        O_HL = region(O0, OT, NT), region(O0 + OT * NT, OT, NT)
        ZQ_HL = region(Z0, QR, NT), region(Z0 + QR * NT, QR, NT)
        CKV_HL = region(Z0 + 2 * QR * NT, CR, KEYS), region(Z0 + 2 * QR * NT + CR * KEYS, CR, KEYS)
        H_HL = region(O0, KT, NT), region(Z0, KT, NT)
        MEM_HL = region(Z0, KT, MEM), region(Z0 + KT * MEM, KT, MEM)

        job_ps = [bank(f"job{i}", 2) for i in range(2)]
        scores_ps = bank("scores", 2)
        score_ps = [scores_ps[:, i * 512:(i + 1) * 512] for i in range(2)]
        turn_ps = bank("turn", 1)
        out_ps = bank("outp", 1)

        def halves(ap):
            return ap.rearrange("p (b n) -> p b n", b=2)

        def job_halves(s, p0=0, p1=P):
            return halves(job_ps[s][p0:p1, :])[:, :, 0:HALF]

        def cst(name, i=0, w=1, p0=0, p1=P):
            return const[p0:p1, CONST[name] + i:CONST[name] + i + w]

        def g_col(name, i):
            if name == "next":
                return gain_x[:, i:i + 1]
            return gain[:, GAINS[name] + i:GAINS[name] + i + 1]

        IDENT = cst("ident", 0, P)
        ONES = cst("ones", 0, P)

        raw_loaded = [sem(f"raw_loaded{i}") for i in range(RAW)]
        hi_done, lo_done = sem("hi_done"), sem("lo_done")
        job_done, job_free, gate_done = sem("job_done"), sem("job_free"), sem("gate_done")
        sq_ready, sq_used = sem("sq_ready"), sem("sq_used")
        act_asked, act_done = sem("act_asked"), sem("act_done")
        ready = sem("ready")
        out_rounded = sem("out_rounded")
        rounded = sem("rounded")
        score_done, negmax, exp_done, probs = sem("score_done"), sem("negmax"), sem("exp_done"), sem("probs")
        turn_done, turned, out_done, out_free = sem("turn_done"), sem("turned"), sem("out_done"), sem("out_free")
        x_loaded, c_loaded = [sem(f"x_loaded{i}") for i in range(KT // 2)], sem("c_loaded")
        layer_loaded, r_loaded = sem("layer_loaded"), sem("r_loaded")
        kv_loaded = [sem(f"kv_loaded{i}") for i in range(2)]
        b_loaded = [sem(f"b_loaded{i}") for i in range(2)]
        mem_loaded = [sem(f"mem_loaded{i}") for i in range(2)]
        mem_split, gain_x_loaded = sem("mem_split"), sem("gain_x_loaded")
        store_asked, stored = sem("store_asked"), sem("stored")
        phase_done = sem("phase_done")

        settled = [sem(f"settled_{e}") for e in ("pe", "dve")]

        def counts(*names):
            return {k: AHEAD.get(k, 0) for k in names}

        block = ctx.enter_context(nc.Block())

        @block.tensor
        def _(pe):
            pe.sem_inc(job_done, 1)
            pe.sem_inc(sq_used, 2)
            pe.sem_inc(out_done, 1)
            pe.wait_ge(c_loaded, 16)

            def add_squares(k, kt, pieces=HALVES):
                for po, nn, so in pieces:
                    mm = pe.matmul(scores_ps[:, po:po + nn], ONES, SQ[:, k % 2, so:so + nn],
                                   start=(k == 0), stop=(k == kt - 1))
                mm.then_inc(sq_used, 1)

            for k in range(KT):
                pe.wait_ge(sq_ready, k + 1)
                add_squares(k, KT)
            with pe.Fori(0, DEPTH) as l:
                n = counts("job", "unit", "sq", "ready", "item")
                at = dict(job=0, unit=0)

                def slot():
                    pe.wait_ge(job_free, l * JOBS + at["job"] + n["job"] + 1)
                    n["job"] += 1
                    return job_ps[(n["job"] - 1) % 2]

                def evicted(but=0):
                    pe.wait_ge(job_free, l * JOBS + at["job"] + n["job"] - but + 2)

                def settle():
                    pe.sem_inc(settled[0], 1)

                def wait_ready():
                    n["ready"] += 1
                    pe.wait_ge(ready, l * READY + n["ready"])

                def unit():
                    pe.wait_ge(lo_done, l * UNITS + at["unit"] + n["unit"] + 3)
                    s = n["unit"] % RING
                    n["unit"] += 1
                    return s

                def stat(k, kt, pieces=HALVES):
                    n["sq"] += 1
                    pe.wait_ge(sq_ready, l * SQUARES + n["sq"])
                    add_squares(k, kt, pieces)

                def stat_m():
                    wait_ready()
                    for po, nn, so in HALVES:
                        pe.matmul(scores_ps[:, po:po + nn], ONES, SUM[:, so:so + nn], start=True, stop=False)
                    n["sq"] += 1
                    pe.wait_ge(sq_ready, l * SQUARES + n["sq"])
                    for po, nn, so in HALVES:
                        mm = pe.matmul(scores_ps[:, po:po + nn], ONES, SQ[:, 1, so:so + nn], start=False, stop=True)
                    mm.then_inc(sq_used, 1)

                def project(s, kt, hl, at_col=0, step=P, m=P, pieces=HALVES, each_ready=0, stats=False,
                            each_evicted=False):
                    ps = slot()
                    for k in range(kt):
                        if stats:
                            stat(k, kt)
                        if each_ready and k % each_ready == 0:
                            wait_ready()
                        if each_evicted:
                            evicted(but=kt - k)
                        c = at_col + k * step
                        for w, x in ((WHI, hl[0]), (WHI, hl[1]), (WLO, hl[0])):
                            for po, nn, so in pieces:
                                mm = pe.matmul(ps[0:m, po:po + nn], w[:, s, c:c + m], x[:, k, so:so + nn],
                                               start=(k == 0 and w is WHI and x is hl[0]),
                                               stop=(k == kt - 1 and w is WLO))
                    mm.then_inc(job_done, 1)

                def plain(lhsT, rhs, m=P, pieces=HALVES):
                    ps = slot()
                    for po, nn, so in pieces:
                        mm = pe.matmul(ps[0:m, po:po + nn], lhsT, rhs[:, so:so + nn], start=True, stop=True)
                    mm.then_inc(job_done, 1)

                def turn_values(toks, but=0):
                    evicted(but)
                    ps = slot()
                    for c, w, t in toks:
                        o = (t // 4) * 512 + (t % 4) * P
                        mm = pe.transpose(ps[0:w, o:o + P], vT[:, c:c + w], IDENT)
                    mm.then_inc(job_done, 1)

                def scores(i, head):
                    t0, (c, w), _ = head["tiles"][i]
                    r0, r1 = head["rows"]
                    it = n["item"]
                    s = it % 2
                    pe.wait_ge(exp_done, l * ITEMS + it + 1)
                    chunked = head["mask"] and i < NQ - 1
                    mm = pe.matmul(score_ps[s][:, 0:w], Q[r0:r1, head["q"], t0:t0 + P], K[r0:r1, head["k"], c:c + w],
                                   start=True, stop=not chunked)
                    if chunked:
                        mm = pe.matmul(score_ps[s][:, w - P:w], cst("first", 0, P, 0, 1), cst("neg", 0, P, 0, 1),
                                       start=False, stop=True)
                    mm.then_inc(score_done, 1)
                    n["item"] += 1

                def turn(it, i, head):
                    pe.wait_ge(probs, l * ITEMS + it + 1)
                    pe.wait_ge(turned, l * ITEMS + it + 1)
                    for j, (c, w, _) in enumerate(head["tiles"][i][2]):
                        mm = pe.transpose(turn_ps[0:w, j * P:(j + 1) * P], PROB[:, it % 3, c:c + w], IDENT)
                    mm.then_inc(turn_done, 1)

                def weigh(it, i, head):
                    kts = head["tiles"][i][2]
                    pe.wait_ge(turned, l * ITEMS + it + 2)
                    pe.wait_ge(out_free, l * ITEMS + it + 1)
                    v0, v1, o0 = head["v"]
                    for j, (c, w, t) in enumerate(kts):
                        mm = pe.matmul(out_ps[o0:o0 + v1 - v0, 0:P], V[0:w, head["vs"], t, v0:v1],
                                       probT[0:w, j * P:(j + 1) * P], start=(j == 0), stop=(j == len(kts) - 1))
                    mm.then_inc(out_done, 1)

                def attend(heads, steps, when):
                    flat = [(h, i) for h in heads for i in range(NQ)]
                    base = n["item"]
                    groups = [steps(g) for g in range(1 + max(g for w in when.values() for g, _ in w))]
                    for g, step in when[-1]:
                        groups[g][step]()
                    evicted()
                    for h, i in flat[:2]:
                        scores(i, h)
                    per_group = len(flat) // len(groups)
                    for j in range(len(flat) + 1):
                        if j + 2 < len(flat):
                            if (j + 2) % per_group == 0:
                                evicted(but=1)
                                values_job = n["job"]
                            scores(flat[j + 2][1], flat[j + 2][0])
                        if j > 1 and (j - 1) % per_group == 0:
                            pe.wait_ge(job_free, l * JOBS + values_job + 2)
                        if j:
                            weigh(base + j - 1, flat[j - 1][1], flat[j - 1][0])
                        if j < len(flat):
                            turn(base + j, flat[j][1], flat[j][0])
                        for g, step in when.get(j, ()):
                            groups[g][step]()

                def last_output_split():
                    pe.wait_ge(out_free, l * ITEMS + n["item"] + 1)

                def branch(wait_input, after=None, ahead=0):
                    for e2 in range(KT // 2):
                        for e in range(ahead if e2 == 0 else 0, 2):
                            project(unit(), KT, U_HL)
                        if e2 == 0:
                            wait_input()
                        s = unit()
                        for e in range(2):
                            project(s, OT, O_HL, at_col=e * OT * P)
                        if after:
                            after(e2)

                for i in range(CR + 1):
                    project(unit(), KT, U_HL, each_ready=int(i == 0))
                for k in range(CR):
                    stat(k, CR)
                project(unit(), KT, U_HL)
                evicted(but=1)
                plain(cst("rot_pe", 0, QK, 0, QK), TMP[0:QK, 0], m=QK)
                for i in range(1, QR):
                    project(unit(), KT, U_HL)

                def steps_mla(h):
                    s = []

                    def keys_values():
                        if h == 0:
                            wait_ready()
                        s.append(unit())
                        project(s[0], CR, CKV_HL, at_col=QR * QK)
                        project(s[0], CR, CKV_HL, at_col=QR * QK, pieces=[(0, PAST, NT)])

                    def queries():
                        if h == 0:
                            for k in range(QR):
                                stat(k, QR)
                            wait_ready()
                        project(s[0], QR, ZQ_HL, step=QK, m=QK)

                    def rotate():
                        evicted()
                        plain(cst("rot_pe", 0, QK, 0, QK), Q[0:QK, h % 2], m=QK)

                    return [keys_values, queries, rotate,
                            lambda: turn_values(V_TOKENS + [(NT, P, 4), (NT + P, P, 5), (SEQ, DEC, 6)], but=2)]

                heads = [dict(q=h % 2, k=h % 2, rows=(0, QK), mask=True, tiles=Q_TILES, vs=h % 2,
                              v=(0, MLA_V, (h % 2) * MLA_V)) for h in range(MLA_HEADS)]
                attend(heads, steps_mla, PLAN_MLA)
                branch(last_output_split)

                chunks = V_TOKENS + [(SEQ, DEC, 4)]
                project(unit(), KT, U_HL)
                project(unit(), KT, U_HL)
                for p in range(RET_HEADS // 2):
                    project(unit(), KT, U_HL)
                    evicted(but=1)
                    plain(cst("rot_ret", 0, P), Q[:, 0])
                    plain(cst("rot_ret", 0, P), K[:, 0])
                    project(unit(), KT, U_HL)
                    evicted(but=1)
                    ps = slot()
                    for c, w, t in chunks:
                        mm = pe.transpose(ps[0:w, t * P:(t + 1) * P], K[:, 0, c:c + w], IDENT)
                    mm.then_inc(job_done, 1)
                    for j in range(2):
                        r0, r1 = j * RET_DK, (j + 1) * RET_DK
                        filler = j == 0 or p + 1 < RET_HEADS // 2
                        turn_values(chunks, but=4)
                        ps = slot()
                        for c, w, t in chunks:
                            mm = pe.matmul(ps[0:w, t * P:t * P + w], K[r0:r1, 0, c:c + w], Q[r0:r1, 0, c:c + w],
                                           start=True, stop=True)
                        mm.then_inc(job_done, 1)
                        evicted(but=1)
                        ps = slot()
                        for c, w, t in chunks:
                            mm = pe.matmul(ps[r0:r1, t * P:(t + 1) * P], KW[0:w, t, r0:r1], V[0:w, 0, t, :],
                                           start=True, stop=True)
                        mm.then_inc(job_done, 1)
                        project(unit(), KT, U_HL)
                        wait_ready()
                        ps = slot()
                        for c, w, t in chunks:
                            cross = t > 0
                            mm = pe.matmul(ps[:, t * P:t * P + w], V[:, 0, t, :], prob_sb[:, t * P:t * P + w],
                                           start=True, stop=not cross)
                            if cross:
                                st = ST[r0:r1, t - 1 if t < 4 else 4, :]
                                mm = pe.matmul(ps[:, t * P:t * P + w], st, QX[r0:r1, c:c + w],
                                               start=False, stop=True)
                        mm.then_inc(job_done, 1)
                        evicted()
                        plain(ONES, RO)
                        if filler:
                            project(unit(), KT, U_HL)
                        wait_ready()
                        plain(ONES, rstd2[:, :])
                branch(wait_ready, ahead=1)

                def steps_band(p):
                    def values():
                        turn_values(V_TOKENS + [(SEQ, DEC, 6)])
                        pe.wait_ge(kv_loaded[p % 2], (l * 4 + p // 2 + 1) * 32)

                    return [lambda: project(unit(), KT, U_HL)] * 3 + [values]

                heads = [dict(q=h // 2 % 2, k=h // 2 % 2, rows=((h % 2) * 64, (h % 2) * 64 + 64), mask=False,
                              tiles=Q_TILES, vs=h // 2 % 2, v=((h % 2) * 64, (h % 2) * 64 + 64, (h % 2) * 64))
                         for h in range(BAND_HEADS)]
                attend(heads, steps_band, PLAN_BAND)

                def memory_stats(e2):
                    for k in (2 * e2, 2 * e2 + 1):
                        stat(k, KT, [(0, MEM, 0)])

                branch(last_output_split, memory_stats)

                for e in range(KT):
                    project(unit(), KT, U_HL, each_ready=2 * (e == 0))
                stat_m()

                def steps_mem(h):
                    def query():
                        project(unit(), KT, U_HL, each_ready=int(h == 0), stats=(h == 0))
                        pe.wait_ge(kv_loaded[h % 2], (l * 4 + 2 + h // 2 + 1) * 32)

                    return [lambda: project(unit(), KT, MEM_HL, pieces=[(0, MEM, 0)])] * 2 + [
                        lambda: turn_values([(0, P, 0), (P, P, 1)]), query]

                heads = [dict(q=h % 2, k=h % 2, rows=(0, P), mask=False, tiles=MEM_TILES, vs=h % 2, v=(0, P, 0))
                         for h in range(MEM_HEADS)]
                for step in steps_mem(0)[:MEM_FIRST]:
                    step()
                attend(heads, steps_mem, PLAN_MEM)
                last_output_split()
                for e in range(KT):
                    if e % 2 == 0:
                        s = unit()
                    project(s, OT, O_HL, at_col=e % 2 * OT * P)
                stat_m()

                def chunk(first=False):
                    for e in range(KT):
                        project(unit(), KT, U_HL, each_ready=int(first and e == 0), stats=(first and e == 0))
                    for e in range(KT):
                        project(unit(), KT, H_HL, each_evicted=(e == 0))

                chunk(first=True)
                settle()
                with pe.Fori(0, FF_CHUNKS - 2) as c:
                    at["job"], at["unit"] = c * (2 * KT), c * (2 * KT)
                    chunk()
                at["job"] = at["unit"] = 0
                for k in ("unit", "job"):
                    n[k] += (FF_CHUNKS - 3) * 2 * KT
                chunk()
                stat_m()
                if n["job"] % 2:
                    plain(IDENT, ONES, pieces=[(0, P, 0)])
                for _ in range(SPARE):
                    unit()
                for k in range(KT):
                    stat(k, KT)
                counted(**n)

        @block.gpsimd
        def _(pool):
            pool.sem_inc(lo_done, 2)

            def lo(g, u):
                pool.wait_ge(hi_done, g + 1)
                nc.gpsimd.tensor_tensor(WLO[:, u % RING, :], RAWS[:, u % RAW, :], WHI[:, u % RING, :].bitcast(F32),
                                        ALU.subtract).then_inc(lo_done, 1)

            with pool.Fori(0, DEPTH * UNITS, RING) as g:
                for j in range(RING):
                    lo(g + j, j)
            for j in range(LEAD - 1):
                lo(DEPTH * UNITS + j, j)

        @block.scalar
        def _(act):
            def load(g, u):
                act.dma_start(RAWS[:, u % RAW, :], w_in[bass.ds(g, 1)].rearrange("a p n -> p (a n)"))\
                    .then_inc(raw_loaded[u % RAW], 16)

            def hi(g, turn, u):
                act.wait_ge(raw_loaded[u % RAW], (turn + u // RAW + 1) * 16)
                act.activation(WHI[:, u % RING, :], RAWS[:, u % RAW, :], ACT.Copy).then_inc(hi_done, 1)

            act.sem_inc(turned, 1)
            act.sem_inc(exp_done, 2)
            load(0, 0)
            load(1, 1)
            hi(0, 0, 0)

            def root_of_sum(dst, features, w=NT):
                if w == NT:
                    dst, src = halves(dst), halves(scores_ps[:, :])[:, :, 0:HALF]
                else:
                    src = scores_ps[:, 0:w]
                act.activation(dst, src, ACT.Sqrt, bias=cst("eps"), scale=1.0 / features).then_inc(act_done, 1)

            def round_hi(dst, src, name, i):
                return act.activation(dst, src, ACT.Copy, scale=g_col(name, i))

            for k in range(KT):
                act.wait_ge(act_asked, k + 1)
                round_hi(U_HL[0][:, k], X[:, k], "next", k).then_inc(rounded, 1)
                act.wait_ge(sq_used, k + 1)
                act.activation(SQ[:, k % 2], X[:, k], ACT.Square).then_inc(sq_ready, 1)
            for u in range(RAW):
                if u:
                    hi(u, 0, u)
                act.wait_ge(lo_done, u + 3)
                load(u + 2, u + 2)
            hi(2, 0, 2)
            act.wait_ge(c_loaded, 16)
            act.wait_ge(sq_used, KT + 2)
            root_of_sum(rstd[:, :], D)
            with act.Fori(0, DEPTH) as l:
                n = counts("job", "unit", "gate", "sq", "ask", "item")
                at = dict(job=0, unit=0)

                def place():
                    u = n["unit"]
                    act.wait_ge(job_done, l * JOBS + at["job"] + n["job"] + 1)
                    hi(None, l * (UNITS // RAW) + at["unit_raw"], u + 3)
                    act.wait_ge(lo_done, l * UNITS + at["unit"] + u + 2 + 1 + 2)
                    load(l * UNITS + at["unit"] + (u + 4), u + 4)
                    n["unit"] += 1

                at["unit_raw"] = 0

                def asked():
                    n["ask"] += 1
                    act.wait_ge(act_asked, l * REQS + n["ask"])

                def evicted():
                    act.wait_ge(job_free, l * JOBS + at["job"] + n["job"] + 2)

                def square(k, src, w=NT):
                    act.wait_ge(sq_used, l * SQUARES + n["sq"] + 1)
                    n["sq"] += 1
                    act.activation(SQ[:, k % 2, 0:w], src, ACT.Square).then_inc(sq_ready, 1)

                def root_of(dst, features, w=NT):
                    act.wait_ge(sq_used, l * SQUARES + n["sq"] + 2)
                    root_of_sum(dst, features, w)

                def prepare_x(name):
                    for k in range(KT):
                        asked()
                        round_hi(U_HL[0][:, k], X[:, k], name, k).then_inc(rounded, 1)
                        square(k, X[:, k])

                def root(ap):
                    asked()
                    act.activation(ap, ap, ACT.Sqrt).then_inc(act_done, 1)

                def exps(i, head):
                    it = n["item"]
                    s = it % 2
                    w = head["tiles"][i][1][1]
                    act.wait_ge(negmax, l * ITEMS + it + 1)
                    src = PROB[:, it % 3, 0:w] if head["bias"] else score_ps[s][:, 0:w]
                    act.activation(PROB[:, it % 3, 0:w], src, ACT.Exp, bias=small[:, s * 4 + 1:s * 4 + 2],
                                   accum_out=small[:, s * 4 + 2:s * 4 + 3]).then_inc(exp_done, 1)
                    n["item"] += 1

                def copy_turned(it, i, head):
                    kts = head["tiles"][i][2]
                    act.wait_ge(turn_done, l * ITEMS + it + 1)
                    full = sum(k[1] == P for k in kts)
                    ins = act.activation(probT[:, 0:full * P], turn_ps[:, 0:full * P], ACT.Copy)
                    if full < len(kts):
                        w = kts[-1][1]
                        ins = act.activation(probT[0:w, full * P:(full + 1) * P],
                                             turn_ps[0:w, full * P:(full + 1) * P], ACT.Copy)
                    ins.then_inc(turned, 1)

                def round_output(it, i, head):
                    t0, t1, c0 = out_tokens(head["tiles"], i)
                    ot, o0, o1 = head["o"]
                    act.wait_ge(out_done, l * ITEMS + it + 2)
                    act.activation(O_HL[0][o0:o1, ot, t0:t1], out_ps[o0:o1, c0:P], ACT.Copy).then_inc(out_rounded, 1)

                def attend(heads, steps, when):
                    flat = [(h, i) for h in heads for i in range(NQ)]
                    base = n["item"]
                    for g, step in when[-1]:
                        steps(g)[step]()
                    exps(0, flat[0][0])
                    for j in range(len(flat) + 1):
                        if j + 1 < len(flat):
                            exps(flat[j + 1][1], flat[j + 1][0])
                        if j:
                            round_output(base + j - 1, flat[j - 1][1], flat[j - 1][0])
                        if j < len(flat):
                            copy_turned(base + j, flat[j][1], flat[j][0])
                        for g, step in when.get(j, ()):
                            steps(g)[step]()

                def round_merged(k):
                    for j in range(2):
                        ins = act.activation(U_HL[0][:, k + j], M[:, k + j], ACT.Copy)
                    ins.then_inc(rounded, 1)

                def branch(b, after=None, ahead=0):
                    for e in range(KT):
                        if e >= ahead:
                            place()
                            n["job"] += 1
                        evicted()
                        act.activation(TMP[:, e % 2], TMP[:, e % 2], ACT.Sigmoid,
                                       bias=g_col("b_gate", b * KT + e)).then_inc(gate_done, 1)
                        n["gate"] += 1
                        if e == KT - 1 and b == 2:
                            round_merged(0)
                            round_merged(2)
                        if e % 2:
                            place()
                            n["job"] += 2
                            if after:
                                after(e // 2)

                for _ in range(CR + 1):
                    place()
                    n["job"] += 1
                for k in range(CR):
                    act.wait_ge(job_free, l * JOBS + k + 1 + 2)
                    square(k, CKV[:, k, 0:NT])
                root_of(rstd_c, CR * P)
                place()
                n["job"] += 2
                for _ in range(1, QR):
                    place()
                    n["job"] += 1
                evicted()
                for k in range(QR):
                    ins = round_hi(ZQ_HL[0][:, k], ZQ[:, k], "mla_q", k)
                ins.then_inc(rounded, 1)
                for k in range(QR):
                    square(k, ZQ[:, k])
                root_of(rstd2[:, :], QR * P)

                def count(jobs, places=0):
                    def step():
                        for _ in range(places):
                            place()
                        n["job"] += jobs
                    return step

                def steps_mla(h):
                    return [count(2, 1), count(1), count(1), count(1)]

                heads = [dict(tiles=Q_TILES, bias=False, o=(h // 2, h % 2 * 64, h % 2 * 64 + 64)) for h in range(MLA_HEADS)]
                attend(heads, steps_mla, PLAN_MLA)
                branch(0)

                def placed(after=0):
                    place()
                    n["job"] += 1 + after

                placed()
                placed()
                for p in range(RET_HEADS // 2):
                    placed(2)
                    placed()
                    evicted()
                    act.activation(RET_GATE[1], RET_GATE[0], ACT.Sigmoid).then_inc(gate_done, 1)
                    n["job"] += 1
                    for j in range(2):
                        filler = j == 0 or p + 1 < RET_HEADS // 2
                        n["job"] += 3
                        placed()
                        if j:
                            asked()
                            act.activation(RET_GATE[0], RET_GATE[1], ACT.Sigmoid).then_inc(gate_done, 1)
                        n["job"] += 2
                        if filler:
                            placed()
                        n["job"] += 1
                        n["gate"] += 1
                        root(rstd2[:, :])
                branch(1, ahead=1)

                def steps_band(p):
                    return [count(1, 1)] * 3 + [count(1)]

                heads = [dict(tiles=Q_TILES, bias=True, o=(h // 2, h % 2 * 64, h % 2 * 64 + 64)) for h in range(BAND_HEADS)]
                attend(heads, steps_band, PLAN_BAND)

                def memory(e2):
                    act.wait_ge(mem_loaded[e2 % 2], (l * (KT // 4) + e2 // 2 + 1) * 16)
                    for k in (2 * e2, 2 * e2 + 1):
                        square(k, MEM_RAW[:, k % 4], MEM)
                    for k in (2 * e2, 2 * e2 + 1):
                        ins = round_hi(MEM_HL[0][:, k], MEM_RAW[:, k % 4], "mem", k)
                    ins.then_inc(rounded, 1)

                branch(2, memory)
                round_merged(4)
                root_of(rstd_m[:, :], D, MEM)
                evicted()
                round_merged(KT - 2)
                for e in range(KT):
                    place()
                    n["job"] += 1
                evicted()
                square(KT - 1, M[:, KT - 1])
                root_of(rstd[:, :], D)

                def steps_mem(h):
                    return [count(1, 1), count(1, 1), count(1), count(1, 1)]

                heads = [dict(tiles=MEM_TILES, bias=False, o=(h, 0, P)) for h in range(MEM_HEADS)]
                for step in steps_mem(0)[:MEM_FIRST]:
                    step()
                prepare_x("pre_mem")
                root_of(rstd[:, :], D)
                attend(heads, steps_mem, PLAN_MEM)
                for e in range(KT // 2):
                    place()
                    n["job"] += 2
                evicted()
                square(KT - 1, M[:, KT - 1])
                root_of(rstd[:, :], D)
                prepare_x("pre_ff")
                root_of(rstd[:, :], D)

                def chunk():
                    for e in range(2 * KT):
                        place()
                        n["job"] += 1

                chunk()
                with act.Fori(0, FF_CHUNKS - 2) as c:
                    at["job"], at["unit"], at["unit_raw"] = c * (2 * KT), c * (2 * KT), c * (2 * KT // RAW)
                    chunk()
                at["job"] = at["unit"] = at["unit_raw"] = 0
                n["unit"] += (FF_CHUNKS - 3) * 2 * KT
                n["job"] += (FF_CHUNKS - 3) * 2 * KT
                chunk()
                evicted()
                square(KT - 1, M[:, KT - 1])
                root_of(rstd[:, :], D)
                n["job"] += n["job"] % 2
                for _ in range(SPARE):
                    place()
                prepare_x("next")
                root_of(rstd[:, :], D)
                counted(**n)
            for s in range(RAW):
                act.wait_ge(raw_loaded[s], (DEPTH * UNITS + LEAD) // RAW * 16)

        @block.vector
        def _(dve):
            v = nc.vector
            dve.sem_inc(job_free, 2)
            dve.sem_inc(out_free, 1)
            dve.sem_inc(phase_done, 1)
            v.memset(small[:, :], 0.0)
            dve.drain()
            dve.wait_ge(gain_x_loaded, 16)
            for i in range(KT // 2):
                dve.wait_ge(x_loaded[i], 16)
                dve.sem_inc(act_asked, 2)
            dve.wait_ge(c_loaded, 16)
            for k in range(KT):
                dve.wait_ge(rounded, k + 1)
                v.scalar_tensor_tensor(out=U_HL[1][:, k], in0=X[:, k], scalar=g_col("next", k),
                                       in1=U_HL[0][:, k].bitcast(F32), op0=ALU.mult, op1=ALU.subtract)\
                    .then_inc(ready, 1)
            dve.wait_ge(act_done, 1)
            v.reciprocal(rstd[:, :], rstd[:, :])
            dve.drain()
            with dve.Fori(0, DEPTH) as l:
                n = counts("job", "gate", "ready", "ask", "done", "item", "store", "rounded")
                at = dict(job=0)

                def job():
                    n["job"] += 1
                    dve.wait_ge(job_done, l * JOBS + at["job"] + n["job"] + 1)
                    return (n["job"] - 1) % 2

                def free(ins):
                    ins.then_inc(job_free, 1)

                def is_ready(ins):
                    n["ready"] += 1
                    ins.then_inc(ready, 1)

                def ask(ins):
                    n["ask"] += 1
                    ins.then_inc(act_asked, 1)

                def wait_act():
                    n["done"] += 1
                    dve.wait_ge(act_done, l * ROOTS + n["done"])

                def split(src, hi, lo):
                    v.tensor_copy(hi, src)
                    dve.drain()
                    return v.tensor_tensor(lo, src, hi.bitcast(F32), ALU.subtract)

                def copy_job(dst):
                    s = job()
                    free(v.tensor_copy(halves(dst), job_halves(s)))

                def scale_job(dst):
                    s = job()
                    free(v.tensor_tensor(halves(dst), job_halves(s), halves(rstd[:, :]), ALU.mult))

                def store(ins=None):
                    n["store"] += 1
                    dve.drain()
                    dve.sem_inc(store_asked, 1)

                def wait_stores():
                    dve.wait_ge(stored, (l * STORES + n["store"]) * 16)

                def lows(tiles_of, name, hl, k0, k1):
                    n["rounded"] += 1
                    dve.wait_ge(rounded, l * ROUNDS + n["rounded"])
                    for k in range(k0, k1):
                        if name:
                            ins = v.scalar_tensor_tensor(out=hl[1][:, k], in0=tiles_of(k), scalar=g_col(name, k),
                                                         in1=hl[0][:, k].bitcast(F32), op0=ALU.mult, op1=ALU.subtract)
                        else:
                            ins = v.tensor_tensor(hl[1][:, k], tiles_of(k), hl[0][:, k].bitcast(F32), ALU.subtract)
                    return ins

                def invert(ap):
                    wait_act()
                    v.reciprocal(ap, ap)
                    dve.drain()

                def add_square(k):
                    if k < KT - 1:
                        dve.drain()
                        dst = rstd2[:, :] if k else SUM
                        ins = v.tensor_tensor(dst, M[:, k], M[:, k], ALU.mult)
                        if k:
                            dve.drain()
                            ins = v.tensor_tensor(SUM, SUM, rstd2[:, :], ALU.add)
                        if k == KT - 2:
                            is_ready(ins)

                def update_x(name, following):
                    def normed(k):
                        v.scalar_tensor_tensor(out=UPD[:, k % 2], in0=M[:, k], scalar=g_col(name, k),
                                               in1=rstd[:, :], op0=ALU.mult, op1=ALU.mult)

                    def low(k):
                        is_ready(lows(lambda i: X[:, i], following, U_HL, k, k + 1))

                    invert(rstd[:, :])
                    normed(0)
                    for k in range(KT):
                        dve.drain()
                        ask(v.tensor_tensor(X[:, k], X[:, k], UPD[:, k % 2], ALU.add))
                        if k + 1 < KT:
                            normed(k + 1)
                        if k:
                            low(k - 1)
                    low(KT - 1)
                    invert(rstd[:, :])

                def maxima(i, head):
                    it = n["item"]
                    s = it % 2
                    w = head["tiles"][i][1][1]
                    dve.wait_ge(score_done, l * ITEMS + it + 1)
                    src = score_ps[s][:, 0:w]
                    if head["bias"] is not None:
                        h = head["bias"]
                        if i == 0:
                            dve.wait_ge(b_loaded[h % 2], (l * 4 + h // 2 + 1) * 16)
                        parts = [(0, w, SEQ - w)] if i < NQ - 1 else [(0, DEC, SEQ - DEC), (DEC, w, SEQ - DEC - PAST)]
                        for a, b, x in parts:
                            v.scalar_tensor_tensor(out=PROB[:, it % 3, a:b], in0=score_ps[s][:, a:b], scalar=BAND_HD ** -0.5,
                                                   in1=BIAS[:, h % 2, x:x + b - a], op0=ALU.mult, op1=ALU.add)
                        dve.drain()
                        src = PROB[:, it % 3, 0:w]
                    v.tensor_reduce(small[:, s * 4 + 1:s * 4 + 2], src, AX_X, ALU.max, negate=True)\
                        .then_inc(negmax, 1)
                    n["item"] += 1

                def normalise(it, i, head):
                    s = it % 2
                    w = head["tiles"][i][1][1]
                    dve.wait_ge(exp_done, l * ITEMS + it + 3)
                    v.reciprocal(small[:, s * 4 + 3:s * 4 + 4], small[:, s * 4 + 2:s * 4 + 3])
                    dve.drain()
                    v.tensor_scalar(PROB[:, it % 3, 0:w], PROB[:, it % 3, 0:w], small[:, s * 4 + 3:s * 4 + 4], None,
                                    ALU.mult).then_inc(probs, 1)

                def split_output(it, i, head):
                    t0, t1, c0 = out_tokens(head["tiles"], i)
                    ot, o0, o1 = head["o"]
                    dve.wait_ge(out_rounded, l * ITEMS + it + 1)
                    v.tensor_tensor(O_HL[1][o0:o1, ot, t0:t1], out_ps[o0:o1, c0:P],
                                    O_HL[0][o0:o1, ot, t0:t1].bitcast(F32), ALU.subtract).then_inc(out_free, 1)

                def attend(heads, steps, when):
                    flat = [(h, i) for h in heads for i in range(NQ)]
                    base = n["item"]
                    for g, step in when[-1]:
                        steps(g)[step]()
                    for h, i in flat[:2]:
                        maxima(i, h)
                    for j in range(len(flat) + 1):
                        if j < len(flat):
                            normalise(base + j, flat[j][1], flat[j][0])
                        if j:
                            for g, step in when.get(j - 1, ()):
                                steps(g)[step]()
                        if j + 2 < len(flat):
                            maxima(flat[j + 2][1], flat[j + 2][0])
                        if j:
                            split_output(base + j - 1, flat[j - 1][1], flat[j - 1][0])

                def merged(k):
                    is_ready(lows(lambda i: M[:, i], None, U_HL, k, k + 2))

                def branch(first, after=None, ahead=0, last=False):
                    for e in range(KT):
                        if e % 2 == 0:
                            for j in range(0 if e else ahead, 2):
                                scale_job(TMP[:, j])
                            if last and e == KT - 2:
                                merged(0)
                                merged(2)
                        s = job()
                        n["gate"] += 1
                        dve.wait_ge(gate_done, l * GATES + n["gate"])
                        if first:
                            free(v.tensor_tensor(halves(M[:, e]), job_halves(s), halves(TMP[:, e % 2]), ALU.mult))
                        else:
                            v.tensor_tensor(halves(TMP[:, e % 2]), job_halves(s), halves(TMP[:, e % 2]), ALU.mult)
                            dve.drain()
                            free(v.tensor_tensor(M[:, e], M[:, e], TMP[:, e % 2], ALU.add))
                        if e % 2:
                            dve.drain()
                            if after:
                                after(e // 2)

                for k in range(CR):
                    scale_job(CKV[:, k, 0:NT])
                scale_job(TMP[:, 0])
                scale_job(ZQ[:, 0])
                dve.wait_ge(layer_loaded, (l + 1) * 16 * LAYER_LOADS)
                dve.sem_inc(settled[1], 1)
                s = job()
                free(v.tensor_tensor(halves(RTMP[NOPE:QK, :]), job_halves(s, NOPE, QK), halves(SIN[NOPE:QK, :]),
                                     ALU.mult))
                v.tensor_tensor(TMP[NOPE:QK, 0], TMP[NOPE:QK, 0], COS[NOPE:QK, :], ALU.mult)
                dve.drain()
                for b in range(2):
                    v.tensor_tensor(K[NOPE:QK, b, 0:NT], TMP[NOPE:QK, 0], RTMP[NOPE:QK, :], ALU.add)
                invert(rstd_c)
                scale_job(ZQ[:, 1])
                for k in range(CR):
                    v.scalar_tensor_tensor(out=CKV[:, k, 0:NT], in0=CKV[:, k, 0:NT], scalar=g_col("mla_kv", k),
                                           in1=rstd_c, op0=ALU.mult, op1=ALU.mult)
                dve.drain()
                z = Z0 + 2 * QR * NT
                is_ready(split(m_sb[:, QR * NT:QR * NT + CR * KEYS], arena[:, z:z + CR * KEYS],
                               arena[:, z + CR * KEYS:z + 2 * CR * KEYS]))
                scale_job(ZQ[:, 2])
                store()
                store()
                is_ready(lows(lambda k: ZQ[:, k], "mla_q", ZQ_HL, 0, QR))

                def steps_mla(h):
                    b = h % 2

                    def queries():
                        if h == 0:
                            invert(rstd2[:, :])
                        s = job()
                        free(v.scalar_tensor_tensor(out=halves(Q[0:QK, b]), in0=job_halves(s, 0, QK), scalar=QK ** -0.5,
                                                    in1=halves(rstd2[0:QK, :]), op0=ALU.mult, op1=ALU.mult))

                    def keys_values():
                        s = job()
                        v.tensor_copy(halves(K[0:NOPE, b, 0:NT]), job_halves(s, 0, NOPE))
                        free(v.tensor_copy(halves(vT[:, 0:NT]), job_halves(s)))
                        s = job()
                        v.tensor_copy(K[0:NOPE, b, NT:KEYS], job_ps[s][0:NOPE, 0:PAST])
                        free(v.tensor_copy(vT[:, NT:KEYS], job_ps[s][:, 0:PAST]))

                    def rotate():
                        s = job()
                        v.tensor_tensor(halves(RTMP[NOPE:QK, :]), job_halves(s, NOPE, QK), halves(SIN[NOPE:QK, :]),
                                        ALU.mult)
                        v.tensor_tensor(Q[NOPE:QK, b], Q[NOPE:QK, b], COS[NOPE:QK, :], ALU.mult)
                        dve.drain()
                        free(v.tensor_tensor(Q[NOPE:QK, b], Q[NOPE:QK, b], RTMP[NOPE:QK, :], ALU.add))

                    def values():
                        s = job()
                        v.tensor_copy(V[:, b, 0:4, 0:MLA_V], tiles(job_ps[s][:, 0:512], 4)[:, :, NOPE:P])
                        v.tensor_copy(V[:, b, 4:6, 0:MLA_V], tiles(job_ps[s][:, 512:768], 2)[:, :, NOPE:P])
                        free(v.tensor_copy(V[0:DEC, b, 6, 0:MLA_V], job_ps[s][0:DEC, 768 + NOPE:768 + P]))

                    return [keys_values, queries, rotate, values]

                heads = [dict(tiles=Q_TILES, bias=None,
                              o=(h // 2, h % 2 * 64, h % 2 * 64 + 64)) for h in range(MLA_HEADS)]
                attend(heads, steps_mla, PLAN_MLA)
                dve.drain()
                wait_stores()
                dve.sem_inc(phase_done, 1)
                branch(True)

                dve.wait_ge(r_loaded, (l + 1) * 16 * RET_LOADS)
                v.memset(V[DEC:P, 0, 4, :], 0.0)
                v.memset(prob_sb[DEC:P, 512:512 + DEC], 0.0)
                scale_job(Q[:, 0])
                scale_job(K[:, 0, 0:NT])

                def norm_head(h):
                    invert(rstd2[:, :])
                    v.scalar_tensor_tensor(out=RO, in0=RO, scalar=g_col("ret_gn", h), in1=rstd2[:, :],
                                           op0=ALU.mult, op1=ALU.mult)
                    dve.drain()

                def finish(h):
                    v.tensor_tensor(RO, RO, RET_GATE[h % 2], ALU.mult)
                    dve.drain()
                    if h % 2 == 0:
                        dve.sem_inc(act_asked, 1)
                        n["ask"] += 1
                    split(RO, O_HL[0][:, h], O_HL[1][:, h])
                    dve.drain()

                def silu(h):
                    n["gate"] += 1
                    dve.wait_ge(gate_done, l * GATES + n["gate"])
                    v.tensor_tensor(RET_GATE[h % 2], RET_GATE[h % 2], RET_GATE[1 - h % 2], ALU.mult)

                for p in range(RET_HEADS // 2):
                    if p:
                        norm_head(2 * p - 1)
                    scale_job(TMP[:, 0])
                    dve.drain()
                    s = job()
                    v.tensor_tensor(halves(RTMP), job_halves(s), halves(SIN), ALU.mult)
                    v.tensor_tensor(Q[:, 0], Q[:, 0], COS, ALU.mult)
                    dve.drain()
                    free(v.tensor_tensor(Q[:, 0], Q[:, 0], RTMP, ALU.add))
                    dve.drain()
                    for t in range(5):
                        w = P if t < 4 else DEC
                        v.tensor_tensor(QX[:, t * P:t * P + w], Q[:, 0, t * P:t * P + w], cst("cross", p * P, w),
                                        ALU.mult)
                    s = job()
                    v.tensor_tensor(halves(RTMP), job_halves(s), halves(SIN), ALU.mult)
                    v.tensor_tensor(K[:, 0, 0:NT], K[:, 0, 0:NT], COS, ALU.mult)
                    dve.drain()
                    v.tensor_tensor(K[:, 0, 0:NT], K[:, 0, 0:NT], RTMP, ALU.add)
                    dve.drain()
                    free(v.tensor_scalar(K[:, 0, 0:NT], K[:, 0, 0:NT], RET_DK ** -0.5, None, ALU.mult))
                    if p:
                        dve.drain()
                        finish(2 * p - 1)
                        store()
                        store()
                    scale_job(RET_GATE[0])
                    s = job()
                    for j in range(2):
                        h, r0 = 2 * p + j, j * RET_DK
                        v.tensor_scalar(KW[:, 0:4, r0:r0 + RET_DK], tiles(job_ps[s][:, 0:512], 4)[:, :, r0:r0 + RET_DK],
                                        cst("w_prompt", h), None, ALU.mult)
                        ins = v.tensor_scalar(KW[0:DEC, 4, r0:r0 + RET_DK], job_ps[s][0:DEC, 512 + r0:512 + r0 + RET_DK],
                                              cst("w_sample", h, 1, 0, DEC), None, ALU.mult)
                    free(ins)
                    for j in range(2):
                        h, r0, r1 = 2 * p + j, j * RET_DK, (j + 1) * RET_DK
                        s = job()
                        v.tensor_copy(V[:, 0, 0:4, :], tiles(job_ps[s][:, 0:512], 4))
                        free(v.tensor_copy(V[0:DEC, 0, 4, :], job_ps[s][0:DEC, 512:512 + P]))
                        s = job()
                        for t in range(4):
                            v.tensor_tensor(prob_sb[:, t * P:(t + 1) * P], job_ps[s][:, t * P:(t + 1) * P],
                                            cst("decay", h * P, P), ALU.mult)
                        free(v.tensor_tensor(prob_sb[0:DEC, 512:512 + DEC], job_ps[s][0:DEC, 512:512 + DEC],
                                             cst("decay", h * P, DEC, 0, DEC), ALU.mult))
                        if p and j == 0:
                            wait_stores()
                        s = job()
                        gp, gs = cst("g_prompt", p, 1, r0, r1), cst("g_sample", p, 1, r0, r1)
                        v.tensor_copy(ST[r0:r1, 4, :], probT[r0:r1, p * P:(p + 1) * P])
                        v.tensor_copy(ST[r0:r1, 0, :], job_ps[s][r0:r1, 0:P])
                        for t in range(1, 4):
                            dve.drain()
                            v.scalar_tensor_tensor(out=ST[r0:r1, t, :], in0=ST[r0:r1, t - 1, :], scalar=gp,
                                                   in1=job_ps[s][r0:r1, t * P:(t + 1) * P], op0=ALU.mult, op1=ALU.add)
                        free(v.scalar_tensor_tensor(out=ST[r0:r1, 5, :], in0=ST[r0:r1, 4, :], scalar=gs,
                                                    in1=job_ps[s][r0:r1, 512:512 + P], op0=ALU.mult, op1=ALU.add))
                        is_ready(v.tensor_copy(small[:, 12:13], small[:, 13:14]))
                        if j:
                            norm_head(h - 1)
                            finish(h - 1)
                        if j == 0:
                            scale_job(TMP[:, 0])
                        elif p + 1 < RET_HEADS // 2:
                            scale_job(Q[:, 0])
                        else:
                            scale_job(TMP[:, 0])
                        s = job()
                        v.tensor_copy(RO[:, 0:SEQ], job_ps[s][:, 0:SEQ])
                        free(v.tensor_copy(RO[:, SEQ:NT], job_ps[s][:, 512:512 + DEC]))
                        dve.drain()
                        s = job()
                        free(v.scalar_tensor_tensor(out=halves(RO), in0=job_halves(s), scalar=-1.0 / RET_DV,
                                                    in1=halves(RO), op0=ALU.mult, op1=ALU.add))
                        dve.drain()
                        is_ready(v.tensor_tensor(rstd2[:, :], RO, RO, ALU.mult))
                        silu(h)
                        dve.drain()
                        if j == 0:
                            scale_job(RET_GATE[1])
                        elif p + 1 < RET_HEADS // 2:
                            scale_job(K[:, 0, 0:NT])
                        s = job()
                        free(v.tensor_scalar(halves(rstd2[:, :]), job_halves(s), 1.0 / RET_DV, EPS, ALU.mult, ALU.add))
                        dve.drain()
                        dve.sem_inc(act_asked, 1)
                        n["ask"] += 1
                norm_head(RET_HEADS - 1)
                finish(RET_HEADS - 1)
                store()
                store()
                is_ready(v.tensor_copy(small[:, 12:13], small[:, 13:14]))
                dve.drain()
                wait_stores()
                dve.sem_inc(phase_done, 1)
                branch(False, ahead=1)

                def steps_band(p):
                    b = p % 2

                    def keys():
                        wait_stores()
                        scale_job(K[:, b, 0:NT])

                    def values():
                        s = job()
                        v.tensor_copy(V[:, b, 0:4, :], tiles(job_ps[s][:, 0:512], 4))
                        free(v.tensor_copy(V[0:DEC, b, 6, :], job_ps[s][0:DEC, 768:768 + P]))
                        store()
                        store()

                    return [lambda: scale_job(Q[:, b]), keys, lambda: scale_job(vT[:, 0:NT]), values]

                heads = [dict(tiles=Q_TILES, bias=h, o=(h // 2, h % 2 * 64, h % 2 * 64 + 64))
                         for h in range(BAND_HEADS)]
                attend(heads, steps_band, PLAN_BAND)
                dve.drain()
                wait_stores()
                dve.sem_inc(phase_done, 1)

                def memory(e2):
                    lows(lambda i: MEM_RAW[:, i % 4], "mem", MEM_HL, 2 * e2, 2 * e2 + 2).then_inc(mem_split, 1)

                branch(False, memory, last=True)
                merged(4)
                merged(6)
                invert(rstd_m[:, :])
                for k in range(KT):
                    copy_job(M[:, k])
                    add_square(k)

                def steps_mem(h):
                    b = h % 2

                    def keys():
                        wait_stores()
                        s = job()
                        free(v.tensor_tensor(K[:, b, 0:MEM], job_ps[s][:, 0:MEM], rstd_m[:, :], ALU.mult))

                    def values_t():
                        s = job()
                        free(v.tensor_tensor(vT[:, 0:MEM], job_ps[s][:, 0:MEM], rstd_m[:, :], ALU.mult))

                    def values():
                        s = job()
                        free(v.tensor_copy(V[:, b, 0:2, :], tiles(job_ps[s][:, 0:256], 2)))
                        store()
                        store()

                    def queries():
                        s = job()
                        free(v.scalar_tensor_tensor(out=halves(Q[:, b]), in0=job_halves(s), scalar=MEM_HD ** -0.5,
                                                    in1=halves(rstd[:, :]), op0=ALU.mult, op1=ALU.mult))

                    return [keys, values_t, values, queries]

                heads = [dict(tiles=MEM_TILES, bias=None, o=(h, 0, P)) for h in range(MEM_HEADS)]
                for step in steps_mem(0)[:MEM_FIRST]:
                    step()
                update_x("post_mix", "pre_mem")
                attend(heads, steps_mem, PLAN_MEM)
                wait_stores()
                for k in range(KT):
                    copy_job(M[:, k])
                    add_square(k)
                update_x("post_mem", "pre_ff")

                def chunk(first=False, last=False):
                    for e in range(KT):
                        s = job()
                        v.scalar_tensor_tensor(out=halves(TMP[:, e % 2]), in0=job_halves(s), scalar=0.0,
                                               in1=halves(rstd[:, :]), op0=ALU.max, op1=ALU.mult)
                        dve.drain()
                        v.tensor_tensor(TMP[:, e % 2], TMP[:, e % 2], TMP[:, e % 2], ALU.mult)
                        dve.drain()
                        free(split(TMP[:, e % 2], H_HL[0][:, e], H_HL[1][:, e]))
                    for e in range(KT):
                        if first:
                            copy_job(M[:, e])
                        else:
                            s = job()
                            free(v.tensor_tensor(halves(M[:, e]), job_halves(s), halves(M[:, e]), ALU.add))
                        if last:
                            add_square(e)
                    dve.drain()

                chunk(first=True)
                with dve.Fori(0, FF_CHUNKS - 2) as c:
                    at["job"] = c * (2 * KT)
                    chunk()
                at["job"] = 0
                n["job"] += (FF_CHUNKS - 3) * 2 * KT
                chunk(last=True)
                if n["job"] % 2:
                    s = job()
                    free(v.tensor_copy(small[:, 14:15], job_ps[s][:, 0:1]))
                dve.wait_ge(gain_x_loaded, (l + 2) * 16)
                dve.sem_inc(settled[1], 1)
                update_x("post_ff", "next")
                dve.drain()
                dve.sem_inc(phase_done, 1)
                counted(**n)

        @block.sync
        def _(sp):
            sp.dma_start(gain_x[:, :], gain_x_in[0]).then_inc(gain_x_loaded, 16)
            for i in range(KT // 2):
                sp.dma_start(x_sb[:, 2 * i * NT:2 * (i + 1) * NT], x_in[:, 2 * i * NT:2 * (i + 1) * NT])\
                    .then_inc(x_loaded[i], 16)
                if i == 0:
                    sp.dma_start(const[:, :], const_in).then_inc(c_loaded, 16)

            with sp.Fori(0, DEPTH) as l:
                n = dict(store=0)

                def store(dst, src):
                    n["store"] += 1
                    sp.wait_ge(store_asked, l * STORES + n["store"])
                    sp.dma_start(dst, src).then_inc(stored, 16)

                sp.wait_ge(phase_done, l * DVE_PHASES + 1)
                sp.dma_start(gain[:, :], gain_in[bass.ds(l, 1)].rearrange("a p n -> p (a n)")).then_inc(layer_loaded, 16)
                sp.dma_start(cs_sb[:, :], rope_in[0]).then_inc(layer_loaded, 16)
                sp.dma_start(CKV[:, :, NT:KEYS], ckv_in[bass.ds(l, 1)].rearrange("a p k n -> p (a k) n"))\
                    .then_inc(layer_loaded, 16)
                for b in range(2):
                    sp.dma_start(K[NOPE:QK, b, NT:KEYS], kpe_in[bass.ds(l, 1)].rearrange("a p n -> p (a n)"))\
                        .then_inc(layer_loaded, 16)
                store(ckv_out[bass.ds(l, 1)].rearrange("a p k n -> p (a k) n"), CKV[:, :, 0:NT])
                store(kpe_out[bass.ds(l, 1)].rearrange("a p n -> p (a n)"), K[NOPE:QK, 0, 0:NT])
                sp.wait_ge(phase_done, l * DVE_PHASES + 2)
                sp.dma_start(cs_sb[:, :], rope_in[1]).then_inc(r_loaded, 16)
                sp.dma_start(probT[:, 0:2 * P], state_in[bass.ds(l, 1)].rearrange("a p h n -> p (a h n)"))\
                    .then_inc(r_loaded, 16)
                sp.dma_start(gain_x[:, :], gain_x_in[bass.ds(l + 1, 1)].rearrange("a p n -> p (a n)"))\
                    .then_inc(gain_x_loaded, 16)
                for p in range(2):
                    store(retp_out[bass.ds(l, 1), :, p].rearrange("a p n -> p (a n)"), ST[:, 3, :])
                    store(rets_out[bass.ds(l, 1), :, p].rearrange("a p n -> p (a n)"), ST[:, 5, :])
                sp.wait_ge(phase_done, l * DVE_PHASES + 3)

                def load_bias(h):
                    sp.dma_start(BIAS[:, h % 2], bias_in[bass.ds(l, 1), h].rearrange("a p n -> p (a n)"))\
                        .then_inc(b_loaded[h % 2], 16)

                def load_band(p):
                    sp.dma_start(K[:, p % 2, NT:KEYS], bandk_in[bass.ds(l, 1), p].rearrange("a p n -> p (a n)"))\
                        .then_inc(kv_loaded[p % 2], 16)
                    sp.dma_start(V[:, p % 2, 4:6, :], bandv_in[bass.ds(l, 1), p].rearrange("a p t n -> p (a t) n"))\
                        .then_inc(kv_loaded[p % 2], 16)

                for i in range(2):
                    load_bias(i)
                    load_band(i)
                for p in range(BAND_HEADS // 2):
                    store(bandk_out[bass.ds(l, 1), p].rearrange("a p n -> p (a n)"), K[:, p % 2, 0:NT])
                    store(bandv_out[bass.ds(l, 1), p].rearrange("a p n -> p (a n)"), vT[:, 0:NT])
                    for h in (2 * p, 2 * p + 1):
                        if h + 2 < BAND_HEADS:
                            sp.wait_ge(out_free, l * ITEMS + I_BAND + (h + 1) * NQ + 1)
                            load_bias(h + 2)
                    if p + 2 < BAND_HEADS // 2:
                        load_band(p + 2)

                def load_mem(h):
                    sp.dma_start(K[:, h % 2, MEM:2 * MEM], memk_in[bass.ds(l, 1), h].rearrange("a p n -> p (a n)"))\
                        .then_inc(kv_loaded[h % 2], 16)
                    sp.dma_start(V[:, h % 2, 2:4, :], memv_in[bass.ds(l, 1), h].rearrange("a p t n -> p (a t) n"))\
                        .then_inc(kv_loaded[h % 2], 16)

                sp.wait_ge(phase_done, l * DVE_PHASES + 4)
                for i in range(2):
                    load_mem(i)
                for i in range(KT // 2):
                    if i >= 2:
                        sp.wait_ge(mem_split, l * (KT // 2) + i - 1)
                    sp.dma_start(MEM_RAW[:, i % 2 * 2:i % 2 * 2 + 2], mem_in[:, 2 * i:2 * i + 2]).then_inc(mem_loaded[i % 2], 16)
                for h in range(MEM_HEADS):
                    store(memk_out[bass.ds(l, 1), h].rearrange("a p n -> p (a n)"), K[:, h % 2, 0:MEM])
                    store(memv_out[bass.ds(l, 1), h].rearrange("a p n -> p (a n)"), vT[:, 0:MEM])
                    if h + 2 < MEM_HEADS:
                        sp.wait_ge(out_free, l * ITEMS + I_MEM + (h + 1) * NQ + 1)
                        load_mem(h + 2)
            sp.wait_ge(phase_done, DEPTH * DVE_PHASES + 1)
            sp.dma_start(y_out, x_sb[:, :]).then_inc(stored, 16)
            sp.wait_ge(stored, (DEPTH * STORES + 1) * 16)


def counted(**n):
    want = dict(job=JOBS, unit=UNITS, gate=GATES, ready=READY, ask=REQS, item=ITEMS, done=ROOTS,
                store=STORES, sq=SQUARES, rounded=ROUNDS)
    assert all(want[k] + AHEAD.get(k, 0) == v for k, v in n.items()), n


def constants():
    c = np.zeros((P, NCONST), np.float32)

    def put(name, a):
        c[:a.shape[0], CONST[name]:CONST[name] + a.shape[1]] = a

    put("ident", np.eye(P))
    put("ones", np.ones((P, P)))
    for name, half, r0, r1 in (("rot_ret", RET_DK // 2, 0, P), ("rot_pe", ROPE // 2, NOPE, QK)):
        m = np.zeros((P, P))
        for i in range(r0, r1):
            j = (i - r0) % (2 * half)
            if j < half:
                m[i + half, i] = -1
            else:
                m[i - half, i] = 1
        put(name, m)
    first = np.zeros((1, P))
    first[0, :CHUNK] = 1
    put("first", first)
    put("eps", np.full((P, 1), EPS))
    neg = np.zeros((1, P))
    neg[0, CHUNK:] = NEG
    put("neg", neg)
    g = np.log1p(-np.exp2(-5.0 - np.arange(RET_HEADS)))
    t = np.arange(P)
    cross = np.zeros((P, 2 * P))
    gp, gs = np.zeros((P, 2)), np.zeros((P, 2))
    for p in range(2):
        for j in range(2):
            r = slice(j * RET_DK, (j + 1) * RET_DK)
            cross[r, p * P:(p + 1) * P] = np.exp(g[2 * p + j] * (t + 1.0))
            gp[r, p] = np.exp(g[2 * p + j] * P)
            gs[r, p] = np.exp(g[2 * p + j] * DEC)
    put("cross", cross)
    put("g_prompt", gp)
    put("g_sample", gs)
    diff = t[None, :] - t[:, None]
    put("decay", np.concatenate([np.where(diff >= 0, np.exp(x * np.maximum(diff, 0)), 0) for x in g], 1))
    put("w_prompt", np.stack([np.exp(x * (P - 1.0 - t)) for x in g], 1))
    put("w_sample", np.stack([np.exp(x * (DEC - 1.0 - t[:DEC])) for x in g], 1))
    pos = np.concatenate([np.arange(SEQ), PAST + np.arange(DEC)]).astype(np.float32)
    rope = np.zeros((2, P, 2 * NT), np.float32)
    for i, (half, r0, r1) in enumerate(((ROPE // 2, NOPE, QK), (RET_DK // 2, 0, P))):
        inv = np.float32(10000.0) ** (-np.arange(half, dtype=np.float32) / np.float32(half))
        ang = (inv[:, None] * pos[None, :]).astype(np.float32)
        rows = (np.arange(r0, r1) - r0) % half
        rope[i, r0:r1, :NT] = np.cos(ang)[rows]
        rope[i, r0:r1, NT:] = np.sin(ang)[rows]
    return c, rope


def kernel(**inputs):
    import concourse.bacc as bacc
    from concourse.bass_utils import run_bass_kernel_spmd

    a = {k: np.asarray(v) for k, v in inputs.items()}

    def fm(x):
        return x.T.reshape(-1, P, x.shape[0]).transpose(1, 0, 2)

    def w_tile(w, width=P):
        return w.reshape(-1, P, w.shape[1]).transpose(1, 0, 2).reshape(P, -1)

    units = []

    def add(*parts):
        u = np.concatenate(parts, 1)
        units.append(np.pad(u, ((0, 0), (0, D - u.shape[1]))))

    sizes = (384, 256, 32, 256, 256, 512, 512, 512, 512, 512, 3072)
    off = np.concatenate([[0], np.cumsum(sizes)])
    zq, zkv, zpe, rq, rk, rv, rg, cq, ck, cv, zg = off[:11]
    for l in range(DEPTH):
        w = a["w_in"][l]
        cols = lambda c: w_tile(w[:, c:c + P])

        def branch(b, wb):
            for e in range(0, KT, 2):
                add(cols(zg + b * D + e * P))
                add(cols(zg + b * D + (e + 1) * P))
                add(w_tile(wb[:, e * P:(e + 1) * P]), w_tile(wb[:, (e + 1) * P:(e + 2) * P]))

        for i in range(CR):
            add(cols(zkv + i * P))
        add(cols(zpe - NOPE))
        for i in range(QR):
            add(cols(zq + i * P))
        for h in range(MLA_HEADS):
            add(w_tile(a["w_mla_uq"][l][:, h]), w_tile(a["w_mla_ukv"][l][:, h]))
        branch(0, a["w_br_a"][l])
        for p in range(2):
            add(cols(rq + p * P))
            add(cols(rk + p * P))
            for h in (2 * p, 2 * p + 1):
                add(cols(rv + h * P))
                add(cols(rg + h * P))
        branch(1, a["w_br_b"][l])
        for p in range(4):
            for c in (cq, ck, cv):
                add(cols(c + p * P))
        branch(2, a["w_br_c"][l])
        for e in range(KT):
            add(w_tile(a["w_out"][l][:, e * P:(e + 1) * P]))
        for h in range(MEM_HEADS):
            for name in ("w_mem_k", "w_mem_q", "w_mem_v") if h else ("w_mem_k", "w_mem_v", "w_mem_q"):
                add(w_tile(a[name][l][:, h]))
        wo = a["w_mem_o"][l].reshape(MEM_HEADS * MEM_HD, D)
        for e in range(0, KT, 2):
            add(w_tile(wo[:, e * P:(e + 1) * P]), w_tile(wo[:, (e + 1) * P:(e + 2) * P]))
        for c in range(FF_CHUNKS):
            for e in range(KT):
                add(w_tile(a["w_up"][l][:, c * D + e * P:c * D + (e + 1) * P]))
            for e in range(KT):
                add(w_tile(a["w_down"][l][c * D:(c + 1) * D, e * P:(e + 1) * P]))
        for _ in range(SPARE):
            units.append(np.zeros((P, D), np.float32))
        assert len(units) == (l + 1) * UNITS
    for _ in range(LEAD):
        units.append(np.zeros((P, D), np.float32))

    def col(x):
        return x.reshape(DEPTH, -1, P).transpose(0, 2, 1)

    gains = np.concatenate([col(a[k]) for k in ("g_post_mix", "g_pre_mem", "g_mem", "g_post_mem",
                                                "g_pre_ff", "g_post_ff", "g_mla_q", "g_mla_kv", "g_ret_gn",
                                                "b_gate")], 2)
    gain_x = np.concatenate([col(a["g_pre_mix"]), np.zeros((1, P, KT), np.float32)])
    consts, rope = constants()
    rel = np.arange(P)[:, None] + (SEQ - P) - np.arange(SEQ)[None, :]
    bias = a["band_rel_bias"][:, :, np.clip(rel, -128, 128) + 128].astype(np.float32)
    bias[:, :, :CHUNK, SEQ - CHUNK:] = NEG

    def keyT(x, g):
        return x.reshape(DEPTH, x.shape[2], g, P).transpose(0, 2, 3, 1)

    def val(x, g):
        return x.reshape(DEPTH, 2, P, g, P).transpose(0, 3, 2, 1, 4)

    ins = dict(
        x=fm(np.concatenate([a["x_prompt"][0], a["x_sample"][0]])).reshape(P, -1),
        mem=fm(a["mem_prompt"][0]), w=np.stack(units),
        ckv=np.stack([fm(a["cache_mla_ckv"][l, 0]) for l in range(DEPTH)]),
        kpe=a["cache_mla_kpe"][:, 0].transpose(0, 2, 1),
        state=a["state_ret"][:, 0].reshape(DEPTH, 2, P, RET_DV).transpose(0, 2, 1, 3),
        bandk=keyT(a["cache_band_k"], 4), bandv=val(a["cache_band_v"], 4),
        memk=keyT(a["cache_mem_k"], 4), memv=val(a["cache_mem_v"], 4),
        bias=bias, gain=gains, gain_x=gain_x, const=consts, rope=rope)
    outs = dict(
        y=(P, KT * NT), o_ckv=(DEPTH, P, CR, NT), o_kpe=(DEPTH, ROPE, NT), o_retp=(DEPTH, P, 2, RET_DV),
        o_rets=(DEPTH, P, 2, RET_DV), o_bandk=(DEPTH, 4, P, NT), o_bandv=(DEPTH, 4, P, NT),
        o_memk=(DEPTH, 4, P, MEM), o_memv=(DEPTH, 4, P, MEM))
    nc = bacc.Bacc("TRN2", target_bir_lowering=False, num_devices=1)
    arrays = {k: np.ascontiguousarray(v) for k, v in ins.items()}
    args = [nc.dram_tensor("in_" + k, v.shape, F32, kind="ExternalInput").ap() for k, v in arrays.items()]
    args += [nc.dram_tensor("out_" + k, s, F32, kind="ExternalOutput").ap() for k, s in outs.items()]
    build(nc, *args)
    r = run_bass_kernel_spmd(nc, [{"in_" + k: v for k, v in arrays.items()}], core_ids=[0]).results[0]
    r = {k: r["out_" + k] for k in outs}

    y = np.asarray(r["y"]).reshape(P, KT, NT).transpose(2, 1, 0).reshape(NT, D)
    ckv = np.asarray(r["o_ckv"]).transpose(0, 3, 2, 1).reshape(DEPTH, NT, CR * P)
    kpe = np.asarray(r["o_kpe"]).transpose(0, 2, 1)
    ret = [np.asarray(r[k]).transpose(0, 2, 1, 3).reshape(DEPTH, 1, RET_HEADS, RET_DK, RET_DV)
           for k in ("o_retp", "o_rets")]
    bk, bv = (np.asarray(r[k]).transpose(0, 3, 1, 2).reshape(DEPTH, NT, BAND_HEADS, BAND_HD)
              for k in ("o_bandk", "o_bandv"))
    mk, mv = (np.asarray(r[k]).transpose(0, 3, 1, 2).reshape(DEPTH, 1, MEM, MEM_HEADS, MEM_HD)
              for k in ("o_memk", "o_memv"))
    cut = lambda t: (np.ascontiguousarray(t[:, None, :SEQ]), np.ascontiguousarray(t[:, None, SEQ:]))
    (pc, sc), (pk, sk), (pbk, sbk), (pbv, sbv) = cut(ckv), cut(kpe), cut(bk), cut(bv)
    return (np.ascontiguousarray(y[None, :SEQ]), np.ascontiguousarray(y[None, SEQ:]), pc, pk, ret[0], pbk, pbv,
            mk, mv, sc, sk, ret[1], sbk, sbv)
```
